# Optimizing a Trainium2 kernel written in Bass

```python
import math
import jax, jax.numpy as jnp
from jax import lax
import numpy as np

D_MODEL = 1024
BATCH = 1
SEQ = 256
DEPTH = 2

N_MEM = 256
HEAD_DIM = 64
ROPE_DIM = HEAD_DIM // 4
ROPE_THETA = 500000.0
RMS_EPS = 1e-6
N_TOK_HEADS = 12
N_MEM_HEADS = 4
MIX_WIDTH = (N_TOK_HEADS + N_MEM_HEADS) * HEAD_DIM
MEM_Q = N_MEM_HEADS * HEAD_DIM
D_FF = ((8 * D_MODEL // 3 + 255) // 256) * 256
Q_BLOCK = 128

DSA_KV_RANK = 128
DSA_NOPE = HEAD_DIM - ROPE_DIM
IDX_HEADS = 8
IDX_DIM = 64
DSA_TOPK_MAX = 256
DSA_COLS = [N_TOK_HEADS * HEAD_DIM, DSA_KV_RANK, ROPE_DIM,
            IDX_HEADS * IDX_DIM, IDX_DIM, IDX_HEADS, MEM_Q]

NSA_GROUPS = 2
NSA_HPG = N_TOK_HEADS // NSA_GROUPS
CMP_LEN = 32
CMP_STRIDE = 16
CMP_HIDDEN = 128
SLC_LEN = 64
SLC_TOP_MAX = 16
WIN = 512
NSA_Q_BLOCK = 64
FORCE_SCORE = 1e9
NSA_KV = NSA_GROUPS * HEAD_DIM
NSA_COLS = [N_TOK_HEADS * HEAD_DIM, NSA_KV, NSA_KV, NSA_KV, NSA_KV, NSA_KV, NSA_KV,
            N_TOK_HEADS * 3, MEM_Q]

N_A = (DEPTH + 1) // 2
N_B = DEPTH // 2


def split_cols(x, sizes):
    return jnp.split(x, np.cumsum(sizes)[:-1].tolist(), axis=-1)

def rmsnorm(x, g):
    xf = x.astype(jnp.float32)
    y = xf * lax.rsqrt(jnp.mean(xf * xf, axis=-1, keepdims=True) + RMS_EPS)
    return (y * g.astype(jnp.float32)).astype(x.dtype)

def rope_tables(S):
    inv = ROPE_THETA ** (-np.arange(0, ROPE_DIM, 2, dtype=np.float64) / ROPE_DIM)
    ang = np.arange(S, dtype=np.float64)[:, None] * inv[None, :]
    return jnp.asarray(np.cos(ang).astype(np.float32)), jnp.asarray(np.sin(ang).astype(np.float32))

def apply_partial_rope(x, cos, sin):
    xr, xp = x[..., :ROPE_DIM], x[..., ROPE_DIM:]
    x1, x2 = xr[..., :ROPE_DIM // 2], xr[..., ROPE_DIM // 2:]
    c, s = cos[:, None, :], sin[:, None, :]
    rot = jnp.concatenate([x1 * c - x2 * s, x1 * s + x2 * c], axis=-1).astype(x.dtype)
    return jnp.concatenate([rot, xp], axis=-1)

def masked_softmax(s, mask):
    s = jnp.where(mask, s.astype(jnp.float32), -jnp.inf)
    m = jnp.max(s, axis=-1, keepdims=True)
    m = jnp.where(jnp.isfinite(m), m, 0.0)
    p = jnp.exp(s - m)
    return p / jnp.maximum(jnp.sum(p, axis=-1, keepdims=True), 1e-30)

def memory_attention(q_mem, mem_n, w_kv_mem):
    B, S, _ = q_mem.shape
    q = q_mem.reshape(B, S, N_MEM_HEADS, HEAD_DIM)
    k, v = jnp.split(mem_n @ w_kv_mem, 2, axis=-1)
    k = k.reshape(B, -1, N_MEM_HEADS, HEAD_DIM)
    v = v.reshape(B, -1, N_MEM_HEADS, HEAD_DIM)
    s = jnp.einsum('bshd,bnhd->bhsn', q, k).astype(jnp.float32) * HEAD_DIM ** -0.5
    p = jax.nn.softmax(s, axis=-1).astype(v.dtype)
    return jnp.einsum('bhsn,bnhd->bshd', p, v).reshape(B, S, MEM_Q)

def dsa_mixer(cols, ckv_norm, w_uk, w_uv, cos, sin):
    q, ckv, k_rope, q_idx, k_idx, w_idx = cols
    B, S, _ = q.shape
    q = apply_partial_rope(q.reshape(B, S, N_TOK_HEADS, HEAD_DIM), cos, sin)
    ckv = rmsnorm(ckv, ckv_norm)
    k_nope = ckv @ w_uk
    v = ckv @ w_uv
    k_r = apply_partial_rope(k_rope[:, :, None, :], cos, sin)[:, :, 0]
    k = jnp.concatenate([k_r, k_nope], axis=-1)
    q_idx = apply_partial_rope(q_idx.reshape(B, S, IDX_HEADS, IDX_DIM), cos, sin)
    k_idx = apply_partial_rope(k_idx[:, :, None, :], cos, sin)[:, :, 0]
    w_idx = w_idx.astype(jnp.float32) * (IDX_HEADS ** -0.5 * IDX_DIM ** -0.5)
    topk = min(DSA_TOPK_MAX, S // 4)
    key_pos = jnp.arange(S)
    gather = jax.vmap(lambda kb, ib: kb[ib])

    def block(i):
        t0 = i * Q_BLOCK
        qpos = t0 + jnp.arange(Q_BLOCK)
        qi = lax.dynamic_slice_in_dim(q, t0, Q_BLOCK, axis=1)
        qii = lax.dynamic_slice_in_dim(q_idx, t0, Q_BLOCK, axis=1)
        wi = lax.dynamic_slice_in_dim(w_idx, t0, Q_BLOCK, axis=1)
        logits = jnp.einsum('bthd,bsd->bths', qii, k_idx).astype(jnp.float32)
        score = jnp.einsum('bths,bth->bts', jax.nn.relu(logits), wi)
        causal = key_pos[None, :] <= qpos[:, None]
        score = jnp.where(causal[None], score, -jnp.inf)
        _, idx = lax.top_k(score, topk)
        k_sel = gather(k, idx)
        v_sel = gather(v, idx)
        valid = idx <= qpos[None, :, None]
        s = jnp.einsum('bthd,btkd->bthk', qi, k_sel) * HEAD_DIM ** -0.5
        p = masked_softmax(s, valid[:, :, None, :]).astype(v.dtype)
        return jnp.einsum('bthk,btkd->bthd', p, v_sel).reshape(B, Q_BLOCK, N_TOK_HEADS * HEAD_DIM)

    out = lax.map(block, jnp.arange(S // Q_BLOCK))
    return out.transpose(1, 0, 2, 3).reshape(B, S, N_TOK_HEADS * HEAD_DIM)

def cmp_to_slc_overlap(n_c, n_slc):
    c0 = np.arange(n_c) * CMP_STRIDE
    s0 = np.arange(n_slc) * SLC_LEN
    ov = np.minimum(c0[:, None] + CMP_LEN, s0[None, :] + SLC_LEN) - np.maximum(c0[:, None], s0[None, :])
    return jnp.asarray((np.clip(ov, 0, None) / CMP_LEN).astype(np.float32))

def compress(kv, pos_emb, w1, w2):
    B, S, G, Dh = kv.shape
    n_c = (S - CMP_LEN) // CMP_STRIDE + 1
    blk = np.arange(n_c)[:, None] * CMP_STRIDE + np.arange(CMP_LEN)[None, :]
    blocks = kv[:, blk] + pos_emb[None, None, :, None, :]
    flat = blocks.transpose(0, 1, 3, 2, 4).reshape(B, n_c, G, CMP_LEN * Dh)
    return jax.nn.gelu(flat @ w1) @ w2

def nsa_mixer(cols, pos_k, pos_v, ck_w1, ck_w2, cv_w1, cv_w2, cos, sin):
    q, kc, vc, ks, vs, kw, vw, gates = cols
    B, S, _ = q.shape
    G, J, Dh = NSA_GROUPS, NSA_HPG, HEAD_DIM
    q = q.reshape(B, S, N_TOK_HEADS, Dh)
    q_rot = apply_partial_rope(q, cos, sin)
    kc, vc = kc.reshape(B, S, G, Dh), vc.reshape(B, S, G, Dh)
    ks = apply_partial_rope(ks.reshape(B, S, G, Dh), cos, sin)
    vs = vs.reshape(B, S, G, Dh)
    kw = apply_partial_rope(kw.reshape(B, S, G, Dh), cos, sin)
    vw = vw.reshape(B, S, G, Dh)
    gates = jax.nn.sigmoid(gates.astype(jnp.float32)).astype(q.dtype).reshape(B, S, G, J, 3)
    scale = Dh ** -0.5

    k_cmp = compress(kc, pos_k, ck_w1, ck_w2)
    v_cmp = compress(vc, pos_v, cv_w1, cv_w2)
    n_c = k_cmp.shape[1]
    cmp_end = jnp.arange(n_c) * CMP_STRIDE + CMP_LEN - 1
    n_slc = S // SLC_LEN
    n_sel = min(SLC_TOP_MAX, n_slc)
    overlap = cmp_to_slc_overlap(n_c, n_slc)
    slc_ids = jnp.arange(n_slc)
    ks_b = ks.reshape(B, n_slc, SLC_LEN, G, Dh).transpose(0, 3, 1, 2, 4)
    vs_b = vs.reshape(B, n_slc, SLC_LEN, G, Dh).transpose(0, 3, 1, 2, 4)
    gather = jax.vmap(jax.vmap(lambda kb, ib: kb[ib]))
    kw_pad = jnp.pad(kw, ((0, 0), (WIN, 0), (0, 0), (0, 0)))
    vw_pad = jnp.pad(vw, ((0, 0), (WIN, 0), (0, 0), (0, 0)))

    def block(i):
        T = NSA_Q_BLOCK
        t0 = i * T
        qpos = t0 + jnp.arange(T)
        qc = lax.dynamic_slice_in_dim(q, t0, T, axis=1).reshape(B, T, G, J, Dh)
        qr = lax.dynamic_slice_in_dim(q_rot, t0, T, axis=1).reshape(B, T, G, J, Dh)
        gi = lax.dynamic_slice_in_dim(gates, t0, T, axis=1)
        s_c = jnp.einsum('btgjd,bcgd->btgjc', qc, k_cmp) * scale
        mask_c = cmp_end[None, :] <= qpos[:, None]
        p_c = masked_softmax(s_c, mask_c[None, :, None, None, :])
        o_c = jnp.einsum('btgjc,bcgd->btgjd', p_c.astype(v_cmp.dtype), v_cmp)
        imp = jnp.einsum('btgjc,cn->btgn', p_c, overlap)
        cur = qpos // SLC_LEN
        forced = (slc_ids[None] == 0) | (slc_ids[None] == cur[:, None]) | (slc_ids[None] == cur[:, None] - 1)
        admissible = slc_ids[None] <= cur[:, None]
        imp = jnp.where(forced[None, :, None, :], FORCE_SCORE, imp)
        imp = jnp.where(admissible[None, :, None, :], imp, -jnp.inf)
        _, sel = lax.top_k(imp, n_sel)
        sel_g = sel.transpose(0, 2, 1, 3)
        k_sel = gather(ks_b, sel_g).reshape(B, G, T, n_sel * SLC_LEN, Dh)
        v_sel = gather(vs_b, sel_g).reshape(B, G, T, n_sel * SLC_LEN, Dh)
        tok_pos = (sel_g[..., None] * SLC_LEN + jnp.arange(SLC_LEN)).reshape(B, G, T, n_sel * SLC_LEN)
        mask_s = tok_pos <= qpos[None, None, :, None]
        s_s = jnp.einsum('btgjd,bgtkd->bgtjk', qr, k_sel) * scale
        p_s = masked_softmax(s_s, mask_s[:, :, :, None, :]).astype(v_sel.dtype)
        o_s = jnp.einsum('bgtjk,bgtkd->btgjd', p_s, v_sel)
        kw_i = lax.dynamic_slice_in_dim(kw_pad, t0, WIN + T, axis=1)
        vw_i = lax.dynamic_slice_in_dim(vw_pad, t0, WIN + T, axis=1)
        kpos = t0 - WIN + jnp.arange(WIN + T)
        mask_w = (kpos[None] <= qpos[:, None]) & (kpos[None] > qpos[:, None] - WIN) & (kpos[None] >= 0)
        s_w = jnp.einsum('btgjd,bkgd->btgjk', qr, kw_i) * scale
        p_w = masked_softmax(s_w, mask_w[None, :, None, None, :]).astype(vw_i.dtype)
        o_w = jnp.einsum('btgjk,bkgd->btgjd', p_w, vw_i)
        o = gi[..., 0:1] * o_c + gi[..., 1:2] * o_s + gi[..., 2:3] * o_w
        return o.reshape(B, T, N_TOK_HEADS * Dh)

    out = lax.map(block, jnp.arange(S // NSA_Q_BLOCK))
    return out.transpose(1, 0, 2, 3).reshape(B, S, N_TOK_HEADS * HEAD_DIM)

def first_inputs(seed: int = 0) -> dict:
    key = jax.random.key(seed)
    ks = jax.random.split(key, 24)

    def w(k, shape, fan_in):
        return jax.random.normal(k, shape, jnp.float32) * fan_in ** -0.5

    def gain(k, shape):
        return 1.0 + 0.02 * jax.random.normal(k, shape, jnp.float32)

    return {
        "x": jax.random.normal(ks[0], (BATCH, SEQ, D_MODEL), jnp.float32),
        "mem": jax.random.normal(ks[1], (BATCH, N_MEM, D_MODEL), jnp.float32),
        "attn_norm": gain(ks[2], (DEPTH, D_MODEL)),
        "mem_norm": gain(ks[3], (DEPTH, D_MODEL)),
        "ffn_norm": gain(ks[4], (DEPTH, D_MODEL)),
        "final_norm": gain(ks[5], (D_MODEL,)),
        "dsa_w_in": w(ks[6], (N_A, D_MODEL, sum(DSA_COLS)), D_MODEL),
        "dsa_ckv_norm": gain(ks[7], (N_A, DSA_KV_RANK)),
        "dsa_w_uk": w(ks[8], (N_A, DSA_KV_RANK, DSA_NOPE), DSA_KV_RANK),
        "dsa_w_uv": w(ks[9], (N_A, DSA_KV_RANK, HEAD_DIM), DSA_KV_RANK),
        "nsa_w_in": w(ks[10], (N_B, D_MODEL, sum(NSA_COLS)), D_MODEL),
        "nsa_cmp_pos_k": 0.1 * jax.random.normal(ks[11], (N_B, CMP_LEN, HEAD_DIM), jnp.float32),
        "nsa_cmp_pos_v": 0.1 * jax.random.normal(ks[12], (N_B, CMP_LEN, HEAD_DIM), jnp.float32),
        "nsa_cmp_k_w1": w(ks[13], (N_B, CMP_LEN * HEAD_DIM, CMP_HIDDEN), CMP_LEN * HEAD_DIM),
        "nsa_cmp_k_w2": w(ks[14], (N_B, CMP_HIDDEN, HEAD_DIM), CMP_HIDDEN),
        "nsa_cmp_v_w1": w(ks[15], (N_B, CMP_LEN * HEAD_DIM, CMP_HIDDEN), CMP_LEN * HEAD_DIM),
        "nsa_cmp_v_w2": w(ks[16], (N_B, CMP_HIDDEN, HEAD_DIM), CMP_HIDDEN),
        "mem_w_kv": w(ks[17], (DEPTH, D_MODEL, 2 * MEM_Q), D_MODEL),
        "w_o": w(ks[18], (DEPTH, MIX_WIDTH, D_MODEL), MIX_WIDTH),
        "ffn_w_in": w(ks[19], (DEPTH, D_MODEL, 2 * D_FF), D_MODEL),
        "ffn_w_down": w(ks[20], (DEPTH, D_FF, D_MODEL), D_FF),
    }

def first_block(x, mem, attn_norm, mem_norm, ffn_norm, final_norm,
              dsa_w_in, dsa_ckv_norm, dsa_w_uk, dsa_w_uv,
              nsa_w_in, nsa_cmp_pos_k, nsa_cmp_pos_v,
              nsa_cmp_k_w1, nsa_cmp_k_w2, nsa_cmp_v_w1, nsa_cmp_v_w2,
              mem_w_kv, w_o, ffn_w_in, ffn_w_down):
    S = x.shape[1]
    cos, sin = rope_tables(S)
    for i in range(DEPTH):
        h = rmsnorm(x, attn_norm[i])
        mem_n = rmsnorm(mem, mem_norm[i])
        if i % 2 == 0:
            a = i // 2
            cols = split_cols(h @ dsa_w_in[a], DSA_COLS)
            q_mem = cols[-1]
            tok = dsa_mixer(cols[:-1], dsa_ckv_norm[a], dsa_w_uk[a], dsa_w_uv[a], cos, sin)
        else:
            b = i // 2
            cols = split_cols(h @ nsa_w_in[b], NSA_COLS)
            q_mem = cols[-1]
            tok = nsa_mixer(cols[:-1], nsa_cmp_pos_k[b], nsa_cmp_pos_v[b],
                            nsa_cmp_k_w1[b], nsa_cmp_k_w2[b], nsa_cmp_v_w1[b], nsa_cmp_v_w2[b],
                            cos, sin)
        o_mem = memory_attention(q_mem, mem_n, mem_w_kv[i])
        x = x + jnp.concatenate([tok, o_mem], axis=-1) @ w_o[i]
        h = rmsnorm(x, ffn_norm[i])
        g, u = jnp.split(h @ ffn_w_in[i], 2, axis=-1)
        x = x + (jax.nn.silu(g) * u) @ ffn_w_down[i]
    return rmsnorm(x, final_norm)


N_A_LAYERS = DEPTH // 2
N_B_LAYERS = DEPTH - N_A_LAYERS
CONV_WIDTH = 31
N_HEADS = D_MODEL // HEAD_DIM
N_KV_HEADS = N_HEADS // 4
GROUP = N_HEADS // N_KV_HEADS
WINDOW = 128
BLOCK = 128
N_BUCKETS = 32
MAX_DISTANCE = 128
D_FF_2 = -(-8 * D_MODEL // (3 * 256)) * 256
EPS = 1e-6
NEG_INF = -1e30


def rmsnorm_2(x, g):
    xf = x.astype(jnp.float32)
    xf = xf * lax.rsqrt(jnp.mean(xf * xf, axis=-1, keepdims=True) + EPS)
    return (xf * g.astype(jnp.float32)).astype(x.dtype)

def layernorm(x, g, b):
    xf = x.astype(jnp.float32)
    mu = jnp.mean(xf, axis=-1, keepdims=True)
    var = jnp.mean(jnp.square(xf - mu), axis=-1, keepdims=True)
    y = (xf - mu) * lax.rsqrt(var + EPS) * g.astype(jnp.float32) + b.astype(jnp.float32)
    return y.astype(x.dtype)

def swiglu_ffn(x, w_up, w_down):
    gate, up = jnp.split(x @ w_up, 2, axis=-1)
    return (jax.nn.silu(gate) * up) @ w_down

def conformer_conv(x, w_pw1, b_pw1, w_dw, b_dw, ln_g, ln_b, w_pw2, b_pw2):
    a = jax.nn.glu(x @ w_pw1 + b_pw1, axis=-1)
    y = lax.conv_general_dilated(
        a, w_dw[:, None, :].astype(a.dtype), window_strides=(1,),
        padding=((CONV_WIDTH - 1, 0),),
        dimension_numbers=('NWC', 'WIO', 'NWC'),
        feature_group_count=D_MODEL) + b_dw
    y = jax.nn.silu(layernorm(y, ln_g, ln_b))
    return y @ w_pw2 + b_pw2

def t5_causal_bucket(dist):
    max_exact = N_BUCKETS // 2
    d = jnp.maximum(dist, 0)
    log_ratio = jnp.log(jnp.maximum(d, 1).astype(jnp.float32) / max_exact) / math.log(MAX_DISTANCE / max_exact)
    large = max_exact + (log_ratio * (N_BUCKETS - max_exact)).astype(jnp.int32)
    large = jnp.minimum(large, N_BUCKETS - 1)
    return jnp.where(d < max_exact, d, large)

def banded_sink_attention(q, k, v, sinks, rel_bias):
    B, S = q.shape[0], q.shape[1]
    nb = S // BLOCK
    qb = q.reshape(B, nb, BLOCK, N_KV_HEADS, GROUP, HEAD_DIM)
    kb = k.reshape(B, nb, BLOCK, N_KV_HEADS, HEAD_DIM)
    vb = v.reshape(B, nb, BLOCK, N_KV_HEADS, HEAD_DIM)
    pad = ((0, 0), (1, 0), (0, 0), (0, 0), (0, 0))
    k_band = jnp.concatenate([jnp.pad(kb, pad)[:, :-1], kb], axis=2)
    v_band = jnp.concatenate([jnp.pad(vb, pad)[:, :-1], vb], axis=2)

    s = jnp.einsum('bnqhgd,bnkhd->bnhgqk', qb, k_band,
                   preferred_element_type=jnp.float32) * (HEAD_DIM ** -0.5)

    qi = jnp.arange(BLOCK, dtype=jnp.int32)
    kj = jnp.arange(2 * BLOCK, dtype=jnp.int32)
    dist = qi[:, None] + BLOCK - kj[None, :]
    in_window = (dist >= 0) & (dist < WINDOW)
    bias = rel_bias.astype(jnp.float32)[t5_causal_bucket(dist)]
    bias = jnp.transpose(bias, (2, 0, 1)).reshape(N_KV_HEADS, GROUP, BLOCK, 2 * BLOCK)
    key_pos = (jnp.arange(nb, dtype=jnp.int32)[:, None] - 1) * BLOCK + kj[None, :]
    mask = in_window[None, :, :] & (key_pos >= 0)[:, None, :]

    s = jnp.where(mask[None, :, None, None], s + bias, NEG_INF)
    sink = sinks.astype(jnp.float32).reshape(N_KV_HEADS, GROUP, 1, 1)
    m = jnp.maximum(jnp.max(s, axis=-1, keepdims=True), sink)
    p = jnp.exp(s - m)
    probs = p / (jnp.sum(p, axis=-1, keepdims=True) + jnp.exp(sink - m))
    o = jnp.einsum('bnhgqk,bnkhd->bnqhgd', probs.astype(v.dtype), v_band)
    return o.reshape(B, S, N_HEADS * HEAD_DIM)

def second_inputs(seed: int = 0) -> dict:
    key = jax.random.key(seed)
    ks = jax.random.split(key, 24)
    f32 = jnp.float32
    D, HD, KVD = D_MODEL, N_HEADS * HEAD_DIM, N_KV_HEADS * HEAD_DIM
    nrm = lambda k, shape, scale: jax.random.normal(k, shape, f32) * scale
    gain = lambda k, shape: 1.0 + 0.05 * jax.random.normal(k, shape, f32)
    return {
        "x": jax.random.normal(ks[0], (BATCH, SEQ, D), f32),
        "norm_mix": gain(ks[1], (DEPTH, D)),
        "norm_ffn": gain(ks[2], (DEPTH, D)),
        "conv_w_pw1": nrm(ks[3], (N_A_LAYERS, D, 2 * D), D ** -0.5),
        "conv_b_pw1": nrm(ks[4], (N_A_LAYERS, 2 * D), 0.02),
        "conv_w_dw": nrm(ks[5], (N_A_LAYERS, CONV_WIDTH, D), CONV_WIDTH ** -0.5),
        "conv_b_dw": nrm(ks[6], (N_A_LAYERS, D), 0.02),
        "conv_ln_g": gain(ks[7], (N_A_LAYERS, D)),
        "conv_ln_b": nrm(ks[8], (N_A_LAYERS, D), 0.02),
        "conv_w_pw2": nrm(ks[9], (N_A_LAYERS, D, D), D ** -0.5),
        "conv_b_pw2": nrm(ks[10], (N_A_LAYERS, D), 0.02),
        "norm_kv": gain(ks[11], (D,)),
        "w_kv": nrm(ks[12], (D, 2 * KVD), D ** -0.5),
        "w_q": nrm(ks[13], (N_B_LAYERS, D, HD), D ** -0.5),
        "w_o": nrm(ks[14], (N_B_LAYERS, HD, D), HD ** -0.5),
        "sinks": nrm(ks[15], (N_B_LAYERS, N_HEADS), 0.5),
        "rel_bias": nrm(ks[16], (N_BUCKETS, N_HEADS), 0.5),
        "ffn_w_up": nrm(ks[17], (DEPTH, D, 2 * D_FF_2), D ** -0.5),
        "ffn_w_down": nrm(ks[18], (DEPTH, D_FF_2, D), D_FF_2 ** -0.5),
        "norm_final": gain(ks[19], (D,)),
    }

def second_block(x, norm_mix, norm_ffn, conv_w_pw1, conv_b_pw1, conv_w_dw, conv_b_dw,
              conv_ln_g, conv_ln_b, conv_w_pw2, conv_b_pw2, norm_kv, w_kv, w_q, w_o,
              sinks, rel_bias, ffn_w_up, ffn_w_down, norm_final):
    B, S = x.shape[0], x.shape[1]
    h = x
    k_shared = v_shared = None
    for l in range(DEPTH):
        if l < N_A_LAYERS:
            i = l
            h = h + conformer_conv(rmsnorm_2(h, norm_mix[l]), conv_w_pw1[i], conv_b_pw1[i],
                                   conv_w_dw[i], conv_b_dw[i], conv_ln_g[i], conv_ln_b[i],
                                   conv_w_pw2[i], conv_b_pw2[i])
        else:
            if l == N_A_LAYERS:
                kv = rmsnorm_2(h, norm_kv) @ w_kv
                k_flat, v_flat = jnp.split(kv, 2, axis=-1)
                k_shared = k_flat.reshape(B, S, N_KV_HEADS, HEAD_DIM)
                v_shared = v_flat.reshape(B, S, N_KV_HEADS, HEAD_DIM)
            j = l - N_A_LAYERS
            q = (rmsnorm_2(h, norm_mix[l]) @ w_q[j]).reshape(B, S, N_HEADS, HEAD_DIM)
            attn = banded_sink_attention(q, k_shared, v_shared, sinks[j], rel_bias)
            h = h + attn @ w_o[j]
        h = h + swiglu_ffn(rmsnorm_2(h, norm_ffn[l]), ffn_w_up[l], ffn_w_down[l])
    return rmsnorm_2(h, norm_final)


def setup_inputs(seed=0):
    out = dict(first_inputs(seed))
    for name, value in second_inputs(seed + 1).items():
        if name != "x":
            out[name + "_2"] = value
    return out


def reference(
    x, mem, attn_norm, mem_norm, ffn_norm, final_norm, dsa_w_in, dsa_ckv_norm, dsa_w_uk,
    dsa_w_uv, nsa_w_in, nsa_cmp_pos_k, nsa_cmp_pos_v, nsa_cmp_k_w1, nsa_cmp_k_w2, nsa_cmp_v_w1,
    nsa_cmp_v_w2, mem_w_kv, w_o, ffn_w_in, ffn_w_down, norm_mix_2, norm_ffn_2, conv_w_pw1_2,
    conv_b_pw1_2, conv_w_dw_2, conv_b_dw_2, conv_ln_g_2, conv_ln_b_2, conv_w_pw2_2,
    conv_b_pw2_2, norm_kv_2, w_kv_2, w_q_2, w_o_2, sinks_2, rel_bias_2, ffn_w_up_2,
    ffn_w_down_2, norm_final_2,
):
    x = first_block(
        x, mem, attn_norm, mem_norm, ffn_norm, final_norm, dsa_w_in, dsa_ckv_norm, dsa_w_uk,
        dsa_w_uv, nsa_w_in, nsa_cmp_pos_k, nsa_cmp_pos_v, nsa_cmp_k_w1, nsa_cmp_k_w2,
        nsa_cmp_v_w1, nsa_cmp_v_w2, mem_w_kv, w_o, ffn_w_in, ffn_w_down,
    )
    return second_block(
        x, norm_mix_2, norm_ffn_2, conv_w_pw1_2, conv_b_pw1_2, conv_w_dw_2, conv_b_dw_2,
        conv_ln_g_2, conv_ln_b_2, conv_w_pw2_2, conv_b_pw2_2, norm_kv_2, w_kv_2, w_q_2, w_o_2,
        sinks_2, rel_bias_2, ffn_w_up_2, ffn_w_down_2, norm_final_2,
    )


_drawn_inputs = setup_inputs


def setup_inputs(seed=0):
    import zlib

    import numpy as np

    out = dict(_drawn_inputs(seed))
    spreads = {}
    factors = {'mem_norm': 8.0,
     'dsa_ckv_norm': 5.017,
     'nsa_cmp_pos_k': 41.942,
     'conv_b_pw1_2': 3.711,
     'conv_ln_b_2': 3.907,
     'norm_kv_2': 3.682,
     'sinks_2': 8.0,
     'nsa_cmp_pos_v': 4.658}
    for name, (base, spread) in spreads.items():
        noise = np.random.default_rng([zlib.crc32(name.encode()), seed]).standard_normal(out[name].shape)
        drawn = base * np.exp(spread * noise) if base else spread * noise
        out[name] = __import__('jax').numpy.asarray(drawn.astype(out[name].dtype))
    for name, factor in factors.items():
        out[name] = (out[name] * factor).astype(out[name].dtype)
    return out
```

```python
from contextlib import ExitStack

import numpy as np

import concourse.bass as bass
from concourse import mybir

F32 = mybir.dt.float32
F32R = mybir.dt.float32r
ALU = mybir.AluOpType
ACT = mybir.ActivationFunctionType
AX = mybir.AxisListType

P = 128
S = 256
D = 1024
DC = D // P
TB = S // P
DFF = 2816
HD = 64
N_TOK, N_MEM_H, N_BAND = 12, 4, 16
N_IDX = 8
TOPK = min(256, S // 4)
ROPE = 16
EPS = 1e-6
SCALE = HD ** -0.5
NEG = -1e30
LATER = 3.0e8
TAKEN = -3.3e38
CMP_LEN, CMP_STRIDE = 32, 16
NCMP = (S - CMP_LEN) // CMP_STRIDE + 1
HPG = 6
BUCKETS = 32
CONV = 31
SLOT = 2048
NR = 3
NS = 3
FF_STEPS = DFF // 256


def rope_constants():
    inv = 500000.0 ** (-np.arange(0, ROPE, 2, dtype=np.float64) / ROPE)
    ang = np.arange(S, dtype=np.float64)[:, None] * inv[None, :]
    cos, sin = np.cos(ang).astype(np.float32).T, np.sin(ang).astype(np.float32).T
    c, s = np.ones((P, S), np.float32), np.zeros((P, S), np.float32)
    rot = np.zeros((P, P), np.float32)
    half = ROPE // 2
    for h in range(0, P, HD):
        c[h:h + half], c[h + half:h + ROPE] = cos, cos
        s[h:h + half], s[h + half:h + ROPE] = sin, sin
        for d in range(half):
            rot[h + half + d, h + d] = -1.0
            rot[h + d, h + half + d] = 1.0
    return c, s, rot


def t5_bucket(dist):
    max_exact = BUCKETS // 2
    d = np.maximum(dist, 0)
    ratio = (np.log(np.maximum(d, 1).astype(np.float32) / np.float32(max_exact)).astype(np.float32)
             / np.float32(np.log(128 / max_exact)))
    large = max_exact + (ratio * np.float32(BUCKETS - max_exact)).astype(np.int32)
    return np.where(d < max_exact, d, np.minimum(large, BUCKETS - 1))


CONST_COLS = {}


def constants():
    c, s, rot = rope_constants()
    q, k = np.arange(P)[:, None], np.arange(S)[None, :]
    causal = np.concatenate([np.where(k[:, :P] <= q, 0, NEG), np.where(k <= q + P, 0, NEG)], 1)
    end = np.arange(NCMP) * CMP_STRIDE + CMP_LEN - 1
    cmp_mask = np.concatenate([np.where(end[None] <= q + P * b, 0, NEG) for b in range(TB)], 1)
    row = np.arange(P)[:, None]
    own_head = np.zeros((P, HPG * HD))
    own_head[:HPG * NCMP] = (row[:HPG * NCMP] // NCMP) == (np.arange(HPG * HD)[None] // HD)
    dist = 255 - np.arange(383)
    inside = (dist >= 0) & (dist < P)
    onehot = np.zeros((P, 383))
    onehot[:BUCKETS] = (t5_bucket(dist)[None] == np.arange(BUCKETS)[:, None]) & inside[None]
    outside = np.broadcast_to(np.where(inside, 0, NEG)[None], (P, 383))
    parts = [("ident", np.eye(P)), ("rot", rot), ("cos", c), ("sin", s), ("causal", causal),
             ("cmp_mask", cmp_mask), ("own_head", own_head),
             ("onehot", onehot), ("outside", outside)]
    at = 0
    for name, a in parts:
        CONST_COLS[name] = (at, at + a.shape[1])
        at += a.shape[1]
    return np.ascontiguousarray(np.concatenate([a for _, a in parts], 1).astype(np.float32))


constants()
C_MAIN = CONST_COLS["onehot"][0]
C_T5 = CONST_COLS["outside"][1] - C_MAIN


def build(nc, io, out):
    ctx = ExitStack()
    with ctx:
        _build(nc, ctx, io, out)


def _build(nc, ctx, io, out):
    def sb(name, cols, dt=F32):
        return ctx.enter_context(nc.sbuf_tensor(name, [P, cols], dt))[:, :]

    sems = {}

    def sem(name):
        if name not in sems:
            sems[name] = ctx.enter_context(nc.semaphore(name))
        return sems[name]

    raw = [sb(f"raw{i}", SLOT) for i in range(NR)]
    w_hi = [sb(f"w_hi{i}", SLOT, F32R) for i in range(NS)]
    w_lo = [sb(f"w_lo{i}", SLOT, F32R) for i in range(NS)]
    h_hi = [sb(f"h_hi{i}", DC * S, F32R).rearrange("p (c t) -> p c t", t=S) for i in range(2)]
    h_lo = [sb(f"h_lo{i}", DC * S, F32R).rearrange("p (c t) -> p c t", t=S) for i in range(2)]
    ff_hi = [sb(f"ff_hi{i}", 2 * S, F32R) for i in range(2)]
    ff_lo = [sb(f"ff_lo{i}", 2 * S, F32R) for i in range(2)]
    x_flat = sb("x", DC * S)
    x = x_flat.rearrange("p (c t) -> p c t", t=S)
    rstd = sb("rstd", S)
    rstd_mem = sb("rstd_mem", S)
    rms = sb("rms", S)
    tok_flat = sb("tok", TB * D)
    tok = tok_flat.rearrange("p (b n) -> p b n", n=D)
    PAD = CONV - 1
    APAD = S + PAD
    big = sb("big", max(DC * APAD + DC * S, 32 * P, N_BAND * S))
    mem_tok = big[:, 0:TB * D].rearrange("p (b n) -> p b n", n=D)
    mem_t = big[:, TB * D:2 * TB * D].rearrange("p (c t) -> p c t", t=S)
    cmp_w1 = big[:, 0:32 * P].rearrange("p (m l h) -> p m l h", m=2, l=16)
    glu_pad = big[:, 0:DC * APAD].rearrange("p (c t) -> p c t", t=APAD)
    conv_y = big[:, DC * APAD:DC * APAD + DC * S].rearrange("p (c t) -> p c t", t=S)
    t5_bias = big[:, 0:N_BAND * S].rearrange("p (h k) -> p h k", k=S)
    qa_flat = sb("qa", 8 * S)
    qa = qa_flat.rearrange("p (c t) -> p c t", t=S)
    qb_flat = sb("qb", 6 * S)
    qb = qb_flat.rearrange("p (c t) -> p c t", t=S)
    ka = sb("ka", 4 * S).rearrange("p (c t) -> p c t", t=S)
    va = sb("va", 2 * S)
    q_mem = sb("q_mem", 2 * S).rearrange("p (c t) -> p c t", t=S)
    k_mem = sb("k_mem", 4 * S).rearrange("p (l c t) -> p l c t", l=2, c=2)
    v_mem = sb("v_mem", 4 * S).rearrange("p (l b n) -> p l b n", l=2, b=2)
    scores = [sb(f"scores{i}", 2 * S) for i in range(2)]
    probs = [sb(f"probs{i}", 2 * S) for i in range(2)]
    probs_t = [sb(f"probs_t{i}", 2 * S) for i in range(2)]
    dsa_flat = sb("dsa_flat", 6 * P)
    dsa_mask, ranking = dsa_flat[:, 0:3 * P], dsa_flat[:, 3 * P:6 * P]
    cmp_v = dsa_flat.rearrange("p (g n) -> p g n", g=2)
    cmp_k = sb("cmp_k", 2 * NCMP)
    sink_exp = sb("sink_exp", 2 * N_BAND)
    top8 = sb("top8", 16)
    row_max = sb("row_max", 256)
    row_sum = sb("row_sum", 256)
    factor = sb("factor", 256)
    gates = sb("gates", TB * 36)
    w_idx = sb("w_idx", TB * N_IDX)
    vec_t = sb("vec_t", 4 * P)
    const = sb("const", C_MAIN)
    ones = sb("ones", P)
    w_uk = sb("w_uk", P)
    w_uv = sb("w_uv", HD)
    cmp_w2 = sb("cmp_w2", 3 * HD)
    rel_bias = sb("rel_bias", N_BAND)
    sinks = sb("sinks", N_BAND)
    eps_col = sb("eps_col", 1)
    bank = [ctx.enter_context(nc.psum_tensor(f"bank{i}", [P, 512], F32))[:, :] for i in range(8)]
    t5_row = nc.dram_tensor("t5_row", [P, N_BAND, 383], F32, kind="Internal").ap()

    def const_of(name, rows=P):
        a, b = CONST_COLS[name]
        return const[0:rows, a:b]

    ident = const_of("ident")
    rope_t = tok_flat[:, 0:512]
    stage = [tok_flat[:, 512 * k + 512:512 * k + 1024] for k in range(3)]
    t5_const = tok_flat[:, 0:C_T5]

    vec_rows, vec_col = [], {}

    def rows_of(name, ap, n):
        vec_col[name] = len(vec_rows)
        vec_rows.extend((name, ap, r) for r in range(n))

    def as_rows(ap):
        return ap.rearrange("a (r c) -> (a r) c", c=P)

    for name in ("attn_norm", "mem_norm", "ffn_norm"):
        rows_of(name, as_rows(io[name]), 16)
    rows_of("final_norm", io["final_norm"].rearrange("(r c) -> r c", c=P), 8)
    rows_of("ckv_norm", io["dsa_ckv_norm"], 1)
    rows_of("norm_mix", as_rows(io["norm_mix_2"]), 16)
    rows_of("norm_ffn", as_rows(io["norm_ffn_2"]), 16)
    rows_of("b_pw1", as_rows(io["conv_b_pw1_2"]), 16)
    rows_of("w_dw", io["conv_w_dw_2"][0].rearrange("k (r c) -> (k r) c", c=P), CONV * DC)
    for name, src in (("b_dw", "conv_b_dw_2"), ("ln_g", "conv_ln_g_2"), ("ln_b", "conv_ln_b_2"),
                      ("b_pw2", "conv_b_pw2_2")):
        rows_of(name, as_rows(io[src]), 8)
    rows_of("norm_kv", io["norm_kv_2"].rearrange("(r c) -> r c", c=P), 8)
    rows_of("norm_final", io["norm_final_2"].rearrange("(r c) -> r c", c=P), 8)
    for name, src in (("pos_k", "nsa_cmp_pos_k"), ("pos_v", "nsa_cmp_pos_v")):
        rows_of(name, io[src][0].rearrange("(l two) d -> l (two d)", two=2), 16)
    assert len(vec_rows) <= 4 * P
    vec_tok = qb_flat[:, 0:4 * P].rearrange("p (t c) -> p t c", c=P)

    def vec(name, c):
        k = vec_col[name] + c
        return vec_t[:, k:k + 1]

    slots = []

    def cols(w, n0, n1):
        slots.append((w[:, n0:n1].rearrange("(c p) n -> p c n", p=P), DC, n1 - n0))

    def stage_slots(name, ranges):
        first = len(slots)
        for w, n0, n1 in ranges:
            cols(w, n0, n1)
        return first

    def ffn_slots(w_in, w_down):
        first = len(slots)
        for s in range(FF_STEPS + 1):
            if s < FF_STEPS:
                cols(w_in, 256 * s, 256 * s + 256)
                cols(w_in, DFF + 256 * s, DFF + 256 * s + 256)
            if s >= 1:
                slots.append((w_down[256 * (s - 1):256 * s, :].rearrange("(c p) n -> p c n", p=P), 2, D))
        return first, w_in, w_down

    kv0, kv1 = io["mem_w_kv"][0], io["mem_w_kv"][1]
    dsa, nsa = io["dsa_w_in"][0], io["nsa_w_in"][0]
    G_MEM = [stage_slots("mem0", [(kv0, 0, 256), (kv0, 256, 512)]),
             stage_slots("mem1", [(kv1, 0, 256), (kv1, 256, 512)])]
    G_DSA = stage_slots("dsa", [(dsa, 1424, 1496), (dsa, 912, 1168), (dsa, 1168, 1424), (dsa, 0, 256),
                                (dsa, 256, 512), (dsa, 512, 768), (dsa, 768, 912), (dsa, 1496, 1752)])
    G_WO0 = stage_slots("wo0", [(io["w_o"][0], 256 * i, 256 * i + 256) for i in range(4)])
    FF = [ffn_slots(io["ffn_w_in"][0], io["ffn_w_down"][0])]
    G_NSA = stage_slots("nsa", [(nsa, 256 * i, 256 * i + 256) for i in range(6)]
                        + [(nsa, 1536, 1572), (nsa, 1572, 1828)])
    G_WO1 = stage_slots("wo1", [(io["w_o"][1], 256 * i, 256 * i + 256) for i in range(4)])
    FF.append(ffn_slots(io["ffn_w_in"][1], io["ffn_w_down"][1]))
    pw1, pw2 = io["conv_w_pw1_2"][0], io["conv_w_pw2_2"][0]
    G_PW1 = stage_slots("pw1", [r for i in range(4) for r in
                                ((pw1, 256 * i, 256 * i + 256), (pw1, D + 256 * i, D + 256 * i + 256))])
    G_PW2 = stage_slots("pw2", [(pw2, 256 * i, 256 * i + 256) for i in range(4)])
    FF.append(ffn_slots(io["ffn_w_up_2"][0], io["ffn_w_down_2"][0]))
    G_KV = stage_slots("kv", [(io["w_kv_2"], 0, 256), (io["w_kv_2"], 256, 512)])
    G_Q = stage_slots("q", [(io["w_q_2"][0], 256 * i, 256 * i + 256) for i in range(4)])
    G_WO2 = stage_slots("wo2", [(io["w_o_2"][0], 256 * i, 256 * i + 256) for i in range(4)])
    FF.append(ffn_slots(io["ffn_w_up_2"][1], io["ffn_w_down_2"][1]))
    NSLOT = len(slots)

    proj_index, n = [], 0
    for g, (_, chunks, _) in enumerate(slots):
        proj_index.append(n if chunks == DC else None)
        n += chunks == DC

    proj_index, n = [], 0
    for _, chunks, _ in slots:
        proj_index.append(n)
        n += chunks == DC

    PROD = ["mem0", "mem1", "attn0", "o0", "ffn0", "attn1", "o1", "ffn1", "mix0", "conv", "ffn2",
            "kv", "mix1", "o2", "ffn3"]
    prod = {name: i for i, name in enumerate(PROD)}
    ff_last = [f[0] + 3 * FF_STEPS - 3 for f in FF]
    last_use = [G_MEM[0] + 1, G_MEM[1] + 1, G_DSA + 7, G_WO0 + 3, ff_last[0], G_NSA + 7, G_WO1 + 3,
                ff_last[1], G_PW1 + 7, G_PW2 + 3, ff_last[2], G_KV + 1, G_Q + 3, G_WO2 + 3, ff_last[3]]

    SUMS = ["mem", "attn0", "ckv", "ffn0", "attn1", "ffn1", "final1", "mix0", "ln", "ffn2", "kv",
            "ffn3", "final2"]
    sum_no = {name: i for i, name in enumerate(SUMS)}
    ADDED = [name for name in SUMS if name != "ckv"]
    added_no = {name: i for i, name in enumerate(ADDED)}

    UPDATE = ["load", "ff0", "ff1", "renorm", "ff2", "ff3"]
    BY_SLOT = {"wo0": G_WO0, "wo1": G_WO1, "pw2": G_PW2, "wo2": G_WO2}

    CAUSAL = [(0, P), (P, 3 * P)]
    FULL = [(0, 2 * P), (2 * P, 4 * P)]
    CAUSAL_BLOCKS = [(0, 0), (1, 0), (1, 1)]
    FULL_BLOCKS = [(0, 0), (0, 1), (1, 0), (1, 1)]
    RUNS, n = {}, 0
    for name, heads in (("dsa", N_TOK), ("mem0", N_MEM_H), ("slc", N_TOK), ("win", N_TOK),
                        ("mem1", N_MEM_H), ("band", N_BAND)):
        full = name.startswith("mem")
        RUNS[name] = (n, heads, FULL if full else CAUSAL, FULL_BLOCKS if full else CAUSAL_BLOCKS)
        n += heads
    TURNED = {"o0": 0, "o1": 1, "o2": 2}

    ROT = ["k_idx", "q_idx0", "q_idx1", "q0", "q1", "q2", "k_rope",
           "nq0", "nq1", "nq2", "ks", "kw"]
    rot_no = {name: i for i, name in enumerate(ROT)}
    rot_src = {
        "k_idx": stage[2][0:HD, 0:S], "q_idx0": stage[0], "q_idx1": stage[1],
        "q0": stage[0], "q1": stage[1], "q2": stage[0], "k_rope": qa_flat[0:ROPE, S:2 * S],
        "nq0": qa_flat[:, 0:512], "nq1": qa_flat[:, 512:1024], "nq2": qa_flat[:, 1024:1536],
        "ks": stage[1][:, 0:S], "kw": stage[2][:, 0:S],
    }

    def rot_shape(name):
        src = rot_src[name]
        return src.shape[0], src.shape[1]

    def rot_bank(name):
        return bank[2 + rot_no[name] % 2]

    def landed(eng, g, j=0):
        eng.wait_ge(sem(f"raw_landed{g % NR}"), 16 * (g // NR + 1) + 32 * j)

    def slot_cols(g):
        return slots[g][1] * slots[g][2]

    def proj_bank(g):
        return bank[4 + proj_index[g] % 4]

    def used(eng, g, j=0):
        eng.wait_ge(sem("slot_used"), g + 1 + 6 * j)

    def evicted(eng, g, j=0):
        eng.wait_ge(sem("proj_evicted"), proj_index[g] + 1 + 4 * j)

    def x_updated(eng, u, c2):
        if u in BY_SLOT:
            evicted(eng, BY_SLOT[u] + c2)
        else:
            eng.wait_ge(sem("x_ready"), 4 * UPDATE.index(u) + c2 + 1)

    def set_free(eng, p):
        if p >= 2:
            used(eng, last_use[p - 2])

    def halves(ap):
        return ap.rearrange("p (c t) -> p c t", t=S)

    def over_two(ap):
        return bass.AP(ap.tensor, ap.offset, [ap.ap[0], [0, 2], ap.ap[1]])

    block = ctx.enter_context(nc.Block())

    @block.sync
    def _(sp):
        def load(g, j=0, src=None):
            ap, chunks, w = slots[g]
            if g >= NR:
                sp.wait_ge(sem("w_lo_done"), g - NR + 1 + 6 * j)
            sp.dma_start(raw[g % NR][:, 0:chunks * w].rearrange("p (c n) -> p c n", c=chunks),
                         ap if src is None else src).then_inc(sem(f"raw_landed{g % NR}"), 16)

        def ffn(first, w_in, w_down):
            for g in range(first, first + 5):
                load(g)
            with sp.Fori(0, (FF_STEPS - 3) // 2) as j:
                for u in (0, 1):
                    g = first + 5 + 3 * u
                    n0 = 256 * (2 + u)
                    gate = w_in[:, bass.ds(512 * j + n0, 256)].rearrange("(c p) n -> p c n", p=P)
                    up = w_in[:, bass.ds(512 * j + n0 + DFF, 256)].rearrange("(c p) n -> p c n", p=P)
                    down = w_down[bass.ds(512 * j + n0 - 256, 256), :].rearrange("(c p) n -> p c n", p=P)
                    load(g, j, gate)
                    load(g + 1, j, up)
                    load(g + 2, j, down)
            for g in range(first + 3 * FF_STEPS - 4, first + 3 * FF_STEPS):
                load(g)

        g = 0
        firsts = {f[0]: f for f in FF}
        while g < NSLOT:
            if g in firsts:
                ffn(*firsts[g])
                g += 3 * FF_STEPS
            else:
                load(g)
                g += 1
        for b in range(TB):
            sp.wait_ge(sem("result_ready"), 2 * (b + 1))
            sp.dma_start(out[0, b * P:(b + 1) * P, :], tok[:, b, :]).then_inc(sem("out_written"), 16)
        sp.wait_ge(sem("out_written"), 16 * TB)
        sp.wait_ge(sem("t5_stored"), 16)

    pieces, r = [], 0
    while r < len(vec_rows):
        name, ap, r0 = vec_rows[r]
        m = 1
        while r + m < len(vec_rows) and vec_rows[r + m][0] == name and (r + m) % P:
            m += 1
        pieces.append((r, m, ap[r0:r0 + m, :]))
        r += m
    VEC_ALL, SMALL_ALL = 16 * len(pieces), 16 * 8

    @block.gpsimd
    def _(pool):
        def add_squares(name):
            k = added_no[name]
            for i in range(1, 4):
                pool.wait_ge(sem("squared"), 4 * k + i + 1)
                if i > 1:
                    pool.wait_ge(sem("partly_added"), 3 * k + i - 1)
                pool.tensor_tensor(qa_flat[:, 0:512], qa_flat[:, 0:512], qa_flat[:, 512 * i:512 * i + 512],
                                   ALU.add).then_inc(sem("partly_added"), 1)
            pool.wait_ge(sem("partly_added"), 3 * k + 3)
            pool.tensor_tensor(qa_flat[:, 0:S], qa_flat[:, 0:S], qa_flat[:, S:2 * S],
                               ALU.add).then_inc(sem("added"), 1)

        pool.memset(vec_tok, 0.0).then_inc(sem("cleared"), 1)
        pool.memset(w_uk, 0.0).then_inc(sem("cleared"), 1)
        pool.memset(ones, 1.0).then_inc(sem("cleared"), 1)
        pool.memset(eps_col, EPS).then_inc(sem("cleared"), 1)
        pool.dma_start(mem_tok, io["mem"][0].rearrange("(b p) n -> p b n", p=P)).then_inc(sem("mem_landed"), 16)
        pool.dma_start(const, io["const"][:, 0:C_MAIN]).then_inc(sem("const_landed"), 16)
        pool.dma_start(tok, io["x"][0].rearrange("(b p) n -> p b n", p=P)).then_inc(sem("x_landed"), 16)
        pool.wait_ge(sem("cleared"), 2)
        for r, m, src in pieces:
            pool.dma_start(vec_tok[r % P:r % P + m, r // P, :], src).then_inc(sem("vec_landed"), 16)
        for half in (0, HD):
            pool.dma_start(w_uk[:, half + ROPE:half + HD], io["dsa_w_uk"][0]).then_inc(sem("small_landed"), 16)
        pool.dma_start(w_uv, io["dsa_w_uv"][0]).then_inc(sem("small_landed"), 16)
        for k, name in enumerate(("nsa_cmp_k_w2", "nsa_cmp_k_w2", "nsa_cmp_v_w2")):
            pool.dma_start(cmp_w2[:, k * HD:(k + 1) * HD], io[name][0]).then_inc(sem("small_landed"), 16)
        pool.dma_start(rel_bias[0:BUCKETS, :], io["rel_bias_2"]).then_inc(sem("small_landed"), 16)
        pool.dma_start(sinks, bass.AP(io["sinks_2"].tensor, 0, [[0, P], [1, N_BAND]])).then_inc(sem("small_landed"), 16)
        add_squares("mem")
        pool.wait_ge(sem("h_ready"), 4 * (prod["mem1"] + 1))
        for m, name in enumerate(("nsa_cmp_k_w1", "nsa_cmp_v_w1")):
            pool.dma_start(cmp_w1[:, m], io[name][0].rearrange("(l p) h -> p l h", p=P)).then_inc(sem("cmp_w1_landed"), 16)
        for name in ("attn0", "ffn0", "attn1"):
            add_squares(name)
        pool.wait_ge(sem("h_ready"), 4 * (prod["o1"] + 1))
        pool.dma_start(t5_const, io["const"][:, C_MAIN:C_MAIN + C_T5]).then_inc(sem("t5_landed"), 16)
        pool.memset(glu_pad[:, :, 0:PAD], 0.0).then_inc(sem("pad_cleared"), 1)
        for name in ("ffn1", "final1", "mix0"):
            add_squares(name)
        pool.wait_ge(sem("t5_row_ready"), 1)
        row = tok_flat[0:N_BAND, C_T5:C_T5 + 383]
        pool.dma_start(t5_row.rearrange("q h m -> h q m"),
                       bass.AP(row.tensor, row.offset, [row.ap[0], [0, P], row.ap[1]])).then_inc(sem("t5_stored"), 16)
        add_squares("ln")
        pool.wait_ge(sem("t5_stored"), 16)
        pool.wait_ge(sem("h_ready"), 4 * (prod["conv"] + 1))
        for h0 in range(0, N_BAND, 4):
            pool.dma_start(t5_bias[:, h0:h0 + 4, :], bass.AP(t5_row.tensor, h0 * 383 + P - 1,
                                                            [[N_BAND * 383 - 1, P], [383, 4], [1, S]])
                           ).then_inc(sem("t5_bias_landed"), 16)
        for name in ("ffn2", "kv", "ffn3", "final2"):
            add_squares(name)

    @block.scalar
    def _(act):
        def convert(g, j=0):
            if g >= NSLOT:
                return
            landed(act, g, j)
            if g >= NS:
                used(act, g - NS, j)
            n = slot_cols(g)
            nc.scalar.activation(w_hi[g % NS][:, 0:n], raw[g % NR][:, 0:n], ACT.Copy).then_inc(sem("w_hi_done"), 1)

        def unit(g):
            convert(g + 2)

        def split_hi(p, src, gain, ready):
            set_free(act, p)
            for c in range(DC):
                if c % 2 == 0:
                    ready(c // 2)
                ins = nc.scalar.activation(h_hi[p % 2][:, c, :], src[:, c, :], ACT.Copy, scale=gain(c))
                if c % 2:
                    ins.then_inc(sem("h_hi_done"), 1)

        def squares(name, src, ready):
            k = sum_no[name]
            if k >= 1:
                act.wait_ge(sem("sum_ready"), k)
            for c2 in range(4):
                ready(c2)
                nc.scalar.activation(halves(qa_flat)[:, 2 * c2:2 * c2 + 2, :], src[:, 2 * c2:2 * c2 + 2, :],
                                     ACT.Square).then_inc(sem("squared"), 1)

        def root(name, scale=1.0 / D):
            k = sum_no[name]
            act.wait_ge(sem("sum_ready"), k + 1)
            if k >= 1:
                act.wait_ge(sem("rstd_ready"), k)
            nc.scalar.activation(rms, bank[0][:, 0:S], ACT.Sqrt, scale=scale,
                                 bias=eps_col[:, 0:1]).then_inc(sem("root_done"), 1)

        def norm(name, u, gain):
            split_hi(prod[name], x, gain, lambda c2: x_updated(act, u, c2))
            squares(name, x, lambda c2: x_updated(act, u, c2))
            root(name)

        def softmax(run):
            first, heads, extent, _ = RUNS[run]
            in_psum = extent is FULL
            for n in range(first, first + heads):
                act.wait_ge(sem("max_ready"), n + 1)
                if n >= 2:
                    act.wait_ge(sem("probs_turned"), n - 1)
                for b in range(TB):
                    lo, hi = extent[b]
                    src = bank[n % 2] if in_psum else scores[n % 2]
                    col = slice(2 * n + b, 2 * n + b + 1)
                    ins = nc.scalar.activation(probs[n % 2][:, lo:hi], src[:, lo:hi], ACT.Exp,
                                               bias=row_max[:, col], scale=SCALE if in_psum else 1.0,
                                               accum_out=row_sum[:, col])
                ins.then_inc(sem("exp_done"), 1)
                if run == "band":
                    h = n - first
                    nc.scalar.activation(sink_exp[:, 2 * h:2 * h + 2], row_max[:, 2 * n:2 * n + 2], ACT.Exp,
                                         bias=sinks[:, h:h + 1]).then_inc(sem("sink_done"), 1)

        def turned_o(name):
            p, k = prod[name], TURNED[name]
            set_free(act, p)
            for c2 in range(4):
                act.wait_ge(sem("o_turned"), 4 * k + c2 + 1)
                nc.scalar.activation(h_hi[p % 2][:, 2 * c2:2 * c2 + 2, :], halves(bank[c2]),
                                     ACT.Copy).then_inc(sem("h_hi_done"), 1)

        def ffn(f):
            first = FF[f][0]

            def gate(s, g, j=0):
                evicted(act, g, j)
                nc.scalar.activation(scores[1], scores[0], ACT.Silu).then_inc(sem("silu_done"), 1)

            def hidden(s, g, j=0):
                evicted(act, g, j)
                nc.scalar.activation(ff_hi[s % 2], probs[0], ACT.Copy).then_inc(sem("ff_hi_done"), 1)

            def step(s, j=0):
                g = first + 3 * s - 1
                convert(g + 2, j)
                gate(s, g, j)
                convert(g + 3, j)
                convert(g + 4, j)
                hidden(s, g + 1, j)

            convert(first + 2)
            gate(0, first)
            convert(first + 3)
            hidden(0, first + 1)
            step(1)
            with act.Fori(0, (FF_STEPS - 3) // 2) as j:
                step(2, j)
                step(3, j)
            step(FF_STEPS - 1)
            convert(first + 3 * FF_STEPS - 1 + 2)

        convert(0)
        convert(1)
        act.wait_ge(sem("vec_ready"), 1)
        act.wait_ge(sem("cleared"), 4)
        squares("mem", mem_t, lambda c2: act.wait_ge(sem("mem_turned"), c2 + 1))
        for layer in range(2):
            split_hi(prod[f"mem{layer}"], mem_t, lambda c: vec("mem_norm", DC * layer + c), lambda c2: None)
        root("mem")
        for g in range(4):
            unit(g)
        norm("attn0", "load", lambda c: vec("attn_norm", c))

        for g in range(G_DSA, G_DSA + 3):
            unit(g)
        for h in range(N_IDX):
            act.wait_ge(sem("idx_scored"), h + 1)
            if h >= 2:
                act.wait_ge(sem("idx_weighed"), h - 1)
            nc.scalar.activation(scores[h % 2][:, 0:3 * P], bank[h % 2][:, 0:3 * P],
                                 ACT.Relu).then_inc(sem("idx_relu"), 1)
        for g in range(G_DSA + 3, G_DSA + 7):
            unit(g)
        evicted(act, G_DSA + 6)
        nc.scalar.activation(qa_flat[:, 2 * S:3 * S], qa_flat[:, 0:S], ACT.Square).then_inc(sem("ckv_squared"), 1)
        root("ckv", 1.0 / P)
        unit(G_DSA + 7)
        softmax("dsa")
        softmax("mem0")
        turned_o("o0")
        for g in range(G_WO0, G_WO0 + 4):
            unit(g)
        norm("ffn0", "wo0", lambda c: vec("ffn_norm", c))
        ffn(0)
        norm("attn1", "ff0", lambda c: vec("attn_norm", DC + c))

        for g in range(G_NSA, G_NSA + 4):
            unit(g)
        evicted(act, G_NSA + 3)
        for m in range(2):
            ft = probs_t[m][:, 0:32 * NCMP].rearrange("p (l g c) -> p l g c", l=16, g=2)
            for par in range(2):
                for grp in range(2):
                    src = stage[0][grp * HD:(grp + 1) * HD, m * S:(m + 1) * S]
                    view = bass.AP(src.tensor, src.offset + par, [src.ap[0], [2, 16], [CMP_STRIDE, NCMP]])
                    nc.scalar.activation(ft[par * HD:(par + 1) * HD, :, grp, :], view,
                                         ACT.Copy).then_inc(sem("ft_copied"), 1)
        unit(G_NSA + 4)
        for m in range(2):
            act.wait_ge(sem("cmp_hidden"), m + 1)
            nc.scalar.activation(scores[0][:, 32 * m:32 * m + 2 * NCMP], bank[m][:, 0:2 * NCMP],
                                 ACT.Gelu_apprx_tanh).then_inc(sem("gelu_done"), 1)
        for g in range(G_NSA + 5, G_NSA + 7):
            unit(g)
        evicted(act, G_NSA + 6)
        nc.scalar.activation(probs[1][0:36, 0:S], probs[1][0:36, S:2 * S], ACT.Sigmoid).then_inc(sem("gates_open"), 1)
        unit(G_NSA + 7)
        act.wait_ge(sem("cmp_shifted"), 1)
        nc.scalar.activation(probs[0][:, 0:24 * NCMP], scores[1][:, 0:24 * NCMP], ACT.Exp).then_inc(sem("cmp_exp"), 1)
        for run in ("slc", "win", "mem1"):
            softmax(run)
        turned_o("o1")
        for g in range(G_WO1, G_WO1 + 4):
            unit(g)
        norm("ffn1", "wo1", lambda c: vec("ffn_norm", DC + c))
        ffn(1)
        squares("final1", x, lambda c2: x_updated(act, "ff1", c2))
        root("final1")

        norm("mix0", "renorm", lambda c: vec("norm_mix", c))
        for i in range(4):
            unit(G_PW1 + 2 * i)
            unit(G_PW1 + 2 * i + 1)
            evicted(act, G_PW1 + 2 * i + 1)
            for t in range(2):
                nc.scalar.activation(scores[1][:, S * t:S * t + S], scores[0][:, S * t:S * t + S], ACT.Sigmoid,
                                     bias=vec("b_pw1", DC + 2 * i + t)).then_inc(sem("glu_sigmoid"), 1)
        squares("ln", conv_y, lambda c2: act.wait_ge(sem("centred"), c2 + 1))
        root("ln")
        p = prod["conv"]
        set_free(act, p)
        for c in range(DC):
            act.wait_ge(sem("ln_scaled"), c // 2 + 1)
            nc.scalar.activation(conv_y[:, c, :], conv_y[:, c, :], ACT.Silu, scale=vec("ln_g", c),
                                 bias=vec("ln_b", c)).then_inc(sem("conv_silu"), 1)
        for c2 in range(4):
            act.wait_ge(sem("conv_silu"), 2 * c2 + 2)
            nc.scalar.activation(h_hi[p % 2][:, 2 * c2:2 * c2 + 2, :], conv_y[:, 2 * c2:2 * c2 + 2, :],
                                 ACT.Copy).then_inc(sem("h_hi_done"), 1)
        for g in range(G_PW2, G_PW2 + 4):
            unit(g)
        norm("ffn2", "pw2", lambda c: vec("norm_ffn", c))
        ffn(2)

        norm("kv", "ff2", lambda c: vec("norm_kv", c))
        split_hi(prod["mix1"], x, lambda c: vec("norm_mix", DC + c), lambda c2: None)
        for g in range(G_KV, G_KV + 2 + 4):
            unit(g)
        softmax("band")
        turned_o("o2")
        for g in range(G_WO2, G_WO2 + 4):
            unit(g)
        norm("ffn3", "wo2", lambda c: vec("norm_ffn", DC + c))
        ffn(3)
        squares("final2", x, lambda c2: x_updated(act, "ff3", c2))
        root("final2")

    @block.vector
    def _(dve):
        chain = [0]

        def link(ins):
            chain[0] += 1
            ins.then_inc(sem("dve_link"), 1)
            dve.wait_ge(sem("dve_link"), chain[0])

        def convert(g, j=0):
            if g >= NSLOT:
                return
            dve.wait_ge(sem("w_hi_done"), g + 1 + 6 * j)
            n = slot_cols(g)
            nc.vector.tensor_tensor(w_lo[g % NS][:, 0:n], raw[g % NR][:, 0:n], w_hi[g % NS][:, 0:n].bitcast(F32),
                                    ALU.subtract).then_inc(sem("w_lo_done"), 1)

        def take(g, dst, scale=rstd, j=0, rows=P, n=2):
            used(dve, g, j)
            src = proj_bank(g)[0:rows, 0:n * S]
            if n == 2:
                ins = nc.vector.tensor_tensor(halves(dst), halves(src), over_two(scale[0:rows]), ALU.mult)
            else:
                ins = nc.vector.tensor_tensor(dst, src, scale[0:rows], ALU.mult)
            ins.then_inc(sem("proj_evicted"), 1)

        def split_lo(p, src, gain):
            for c in range(DC):
                if c % 2 == 0:
                    dve.wait_ge(sem("h_hi_done"), 4 * p + c // 2 + 1)
                ins = nc.vector.scalar_tensor_tensor(h_lo[p % 2][:, c, :], src[:, c, :], gain(c),
                                                     h_hi[p % 2][:, c, :].bitcast(F32), ALU.mult, ALU.subtract)
                if c % 2:
                    ins.then_inc(sem("h_ready"), 1)

        def split_lo_pairs(p, src):
            for c2 in range(4):
                dve.wait_ge(sem("h_hi_done"), 4 * p + c2 + 1)
                nc.vector.tensor_tensor(h_lo[p % 2][:, 2 * c2:2 * c2 + 2, :], src(c2),
                                        h_hi[p % 2][:, 2 * c2:2 * c2 + 2, :].bitcast(F32),
                                        ALU.subtract).then_inc(sem("h_ready"), 1)

        def inverse(name, dst=rstd):
            dve.wait_ge(sem("root_done"), sum_no[name] + 1)
            ins = nc.vector.reciprocal(dst, rms)
            ins.then_inc(sem("rstd_ready"), 1)
            dve.wait_ge(sem("rstd_ready"), sum_no[name] + 1)

        def norm(name, gain):
            split_lo(prod[name], x, gain)
            inverse(name)

        def rotate(name, dst):
            rows, n = rot_shape(name)
            src, two = rot_src[name], n == 2 * S
            cos, sin = const_of("cos", rows), const_of("sin", rows)
            if two:
                cos, sin, src = over_two(cos), over_two(sin), halves(src)
            shape = halves if two else (lambda ap: ap)
            dve.wait_ge(sem("rotated"), rot_no[name] + 1)
            link(nc.vector.tensor_tensor(shape(rope_t[0:rows, 0:n]), shape(rot_bank(name)[0:rows, 0:n]), sin, ALU.mult))
            link(nc.vector.tensor_tensor(shape(dst), src, cos, ALU.mult))
            link(nc.vector.tensor_tensor(shape(dst), shape(dst), shape(rope_t[0:rows, 0:n]), ALU.add))

        def mark(name, ins):
            ins.then_inc(sem(name), 1)

        def attend(run, mask=None, gate=None, col0=0, init=None):
            first, heads, extent, blocks = RUNS[run]
            width = extent[1][1]
            full = extent is FULL

            def masked(n):
                dve.wait_ge(sem("qk_done"), n + 1)
                pair = row_max[:, 2 * n:2 * n + 2]
                if full:
                    link(nc.vector.tensor_reduce(pair, halves(bank[n % 2]), AX.X, ALU.max))
                    mark("max_ready", nc.vector.tensor_scalar(pair, pair, -SCALE, None, ALU.mult))
                    return
                if n >= 2:
                    dve.wait_ge(sem("exp_done"), n - 1)
                for b in range(TB):
                    lo, hi = extent[b]
                    ins = nc.vector.tensor_tensor_reduce(
                        scores[n % 2][:, lo:hi], bank[n % 2][:, lo:hi], mask(n - first, b), SCALE,
                        NEG if init is None else init(n - first), ALU.add, ALU.max, row_max[:, 2 * n + b:2 * n + b + 1])
                link(ins)
                mark("max_ready", nc.vector.tensor_scalar(pair, pair, -1.0, None, ALU.mult))

            def copy_t(n):
                dve.wait_ge(sem("probs_turned"), n + 1)
                if n >= 2:
                    dve.wait_ge(sem("pv_done"), n - 1)
                mark("probs_t_ready", nc.vector.tensor_copy(probs_t[n % 2][:, 0:width], bank[2 + n % 2][:, 0:width]))

            def outputs(grp):
                dve.wait_ge(sem("pv_done"), 4 * grp + 4)
                fac = factor[:, 8 * grp:8 * grp + 8]
                den = row_sum[:, 8 * grp:8 * grp + 8]
                h0 = 4 * grp - first
                if run == "band":
                    dve.wait_ge(sem("sink_done"), h0 + 4)
                    link(nc.vector.tensor_tensor(fac, den, sink_exp[:, 2 * h0:2 * h0 + 8], ALU.add))
                    den = fac
                link(nc.vector.reciprocal(fac, den))
                if gate is not None:
                    of = gates.rearrange("p (b h k) -> p h b k", b=TB, k=3)[:, h0:h0 + 4, :, gate]
                    link(nc.vector.tensor_tensor(fac.rearrange("p (h b) -> p h b", b=TB),
                                                 fac.rearrange("p (h b) -> p h b", b=TB), of, ALU.mult))
                f = bass.AP(fac.tensor, fac.offset, [fac.ap[0], [1, TB], [TB, 4], [0, HD]])
                o = bank[4 + grp % 2].rearrange("p (b h d) -> p b h d", b=TB, h=4)
                dst = tok[:, :, col0 + HD * h0:col0 + HD * h0 + 4 * HD]
                if gate is None:
                    mark("o_evicted", nc.vector.tensor_tensor(dst.rearrange("p b (h d) -> p b h d", d=HD), o, f, ALU.mult))
                else:
                    part = qa_flat[:, 0:512]
                    link(nc.vector.tensor_tensor(part.rearrange("p (b h d) -> p b h d", b=TB, h=4), o, f, ALU.mult))
                    mark("o_evicted", nc.vector.tensor_tensor(dst, dst, halves(part), ALU.add))
                    dve.wait_ge(sem("o_evicted"), grp + 1)

            for i in range(first, first + heads + 2):
                if i < first + heads:
                    masked(i)
                if first <= i - 1 < first + heads:
                    copy_t(i - 1)
                if i - 2 >= first and (i - 2) % 4 == 3:
                    outputs((i - 2) // 4)

        def turned_o(name):
            split_lo_pairs(prod[name], lambda c2: halves(bank[c2]))

        def add_slots(g0, bias=None):
            for i in range(4):
                g = g0 + i
                convert(g + 2)
                used(dve, g)
                xs = x[:, 2 * i:2 * i + 2, :]
                if bias is None:
                    mark("proj_evicted", nc.vector.tensor_tensor(xs, halves(proj_bank(g)), xs, ALU.add))
                else:
                    for t in range(2):
                        c = 2 * i + t
                        ins = nc.vector.scalar_tensor_tensor(x[:, c, :], proj_bank(g)[:, S * t:S * t + S], vec(bias, c),
                                                             x[:, c, :], ALU.add, ALU.add)
                    mark("proj_evicted", ins)

        def ffn(f):
            first = FF[f][0]
            n0 = FF_STEPS * f

            def gates_of(g, j=0):
                take(g, scores[0], j=j)

            def hidden(s, g, j=0):
                dve.wait_ge(sem("silu_done"), n0 + s + 1 + 2 * j)
                mark("silu_scaled", nc.vector.tensor_tensor(halves(probs_t[0]), halves(scores[1]), over_two(rstd), ALU.mult))
                used(dve, g, j)
                dve.wait_ge(sem("silu_scaled"), n0 + s + 1 + 2 * j)
                mark("proj_evicted", nc.vector.tensor_tensor(probs[0], proj_bank(g), probs_t[0], ALU.mult))
                dve.wait_ge(sem("ff_hi_done"), n0 + s + 1 + 2 * j)
                mark("ff_ready", nc.vector.tensor_tensor(ff_lo[s % 2], probs[0], ff_hi[s % 2].bitcast(F32), ALU.subtract))

            def step(s, j=0):
                g = first + 3 * s - 1
                convert(g + 2, j)
                gates_of(g, j)
                convert(g + 3, j)
                convert(g + 4, j)
                hidden(s, g + 1, j)

            convert(first + 2)
            gates_of(first)
            convert(first + 3)
            hidden(0, first + 1)
            step(1)
            with dve.Fori(0, (FF_STEPS - 3) // 2) as j:
                step(2, j)
                step(3, j)
            step(FF_STEPS - 1)
            g = first + 3 * FF_STEPS - 1
            convert(g + 2)
            for c2 in range(4):
                dve.wait_ge(sem("down_done"), 4 * f + c2 + 1)
                xs = x[:, 2 * c2:2 * c2 + 2, :]
                mark("x_ready", nc.vector.tensor_tensor(xs, halves(bank[c2]), xs, ALU.add))

        def rescale_x(name, gain, signal):
            inverse(name)
            for c in range(DC):
                ins = nc.vector.scalar_tensor_tensor(x[:, c, :], x[:, c, :], gain(c), rstd, ALU.mult, ALU.mult)
                if c % 2:
                    mark(signal, ins)

        dve.wait_ge(sem("vec_turned"), 1)
        mark("vec_ready", nc.vector.tensor_copy(vec_t, bank[1]))
        for c2 in range(4):
            dve.wait_ge(sem("mem_t_done"), c2 + 1)
            mark("mem_turned", nc.vector.tensor_copy(mem_t[:, 2 * c2:2 * c2 + 2, :], halves(bank[4 + c2])))
        convert(0)
        convert(1)
        dve.wait_ge(sem("mem_turned"), 4)
        dve.wait_ge(sem("vec_ready"), 1)
        for layer in range(2):
            split_lo(prod[f"mem{layer}"], mem_t, lambda c: vec("mem_norm", DC * layer + c))
        inverse("mem", rstd_mem)
        for c2 in range(4):
            dve.wait_ge(sem("x_t_done"), c2 + 1)
            mark("x_ready", nc.vector.tensor_copy(x[:, 2 * c2:2 * c2 + 2, :], halves(bank[c2])))
        for layer in range(2):
            g = G_MEM[layer]
            convert(g + 2)
            take(g, k_mem[:, layer].rearrange("p c t -> p (c t)"), rstd_mem)
            convert(g + 3)
            take(g + 1, probs[layer], rstd_mem)
            dve.wait_ge(sem("v_turned"), layer + 1)
            mark("v_mem_ready", nc.vector.tensor_copy(v_mem[:, layer].rearrange("p b n -> p (b n)"), bank[1 + layer]))
        dve.wait_ge(sem("x_ready"), 4)
        norm("attn0", lambda c: vec("attn_norm", c))

        g = G_DSA
        convert(g + 2)
        take(g, stage[2][0:72, 0:S], rows=72, n=1)
        convert(g + 3)
        take(g + 1, stage[0])
        rotate("k_idx", ka[0:HD, 1, :])
        nc.vector.tensor_copy(ka[HD:P, 1, :], ka[0:HD, 1, :])
        dve.wait_ge(sem("w_idx_turned"), 1)
        link(nc.vector.tensor_scalar(w_idx, bank[1][:, 0:TB * N_IDX], N_IDX ** -0.5 * HD ** -0.5, None, ALU.mult))
        convert(g + 4)
        take(g + 2, stage[1])
        rotate("q_idx0", qa_flat[:, 1024:1536])
        dve.wait_ge(sem("rotated"), rot_no["q_idx1"] + 1)
        rotate("q_idx1", qa_flat[:, 1536:2048])
        mark("idx_inputs", nc.vector.tensor_copy(top8[:, 0:1], w_idx[:, 0:1]))
        for h in range(N_IDX):
            dve.wait_ge(sem("idx_relu"), h + 1)
            if h:
                dve.wait_ge(sem("idx_weighed"), h)
            for b, (lo, hi) in enumerate(CAUSAL):
                w = w_idx[:, b * N_IDX + h:b * N_IDX + h + 1]
                r, s_h = ranking[:, lo:hi], scores[h % 2][:, lo:hi]
                if h == 0:
                    ins = nc.vector.tensor_scalar(r, s_h, w, 0.0, ALU.mult, ALU.add)
                else:
                    ins = nc.vector.scalar_tensor_tensor(r, s_h, w, r, ALU.mult, ALU.add)
            mark("idx_weighed", ins)
        dve.wait_ge(sem("idx_weighed"), N_IDX)
        link(nc.vector.scalar_tensor_tensor(ranking, const_of("causal"), LATER, ranking, ALU.mult, ALU.add))

        def take_top(rounds):
            for _ in range(rounds):
                for b, (lo, hi) in enumerate(CAUSAL):
                    chain[0] += 1
                    nc.vector.max(top8[:, 8 * b:8 * b + 8], ranking[:, lo:hi]).then_inc(sem("dve_link"), 1)
                for b, (lo, hi) in enumerate(CAUSAL):
                    dve.wait_ge(sem("dve_link"), chain[0] - (1 - b) if b == 0 else chain[0] - 1)
                    chain[0] += 1
                    nc.vector.match_replace(ranking[:, lo:hi], top8[:, 8 * b:8 * b + 8], ranking[:, lo:hi],
                                            TAKEN).then_inc(sem("dve_link"), 1)
                dve.wait_ge(sem("dve_link"), chain[0])

        for i in range(3):
            g = G_DSA + 3 + i
            convert(g + 2)
            take(g, stage[i % 2])
            take_top(2)
            if i:
                rotate(f"q{i - 1}", qb_flat[:, 512 * (i - 1):512 * i])
        g = G_DSA + 6
        convert(g + 2)
        used(dve, g)
        link(nc.vector.tensor_tensor(qa_flat[0:ROPE, S:2 * S], proj_bank(g)[0:ROPE, S:2 * S], rstd[0:ROPE], ALU.mult))
        mark("proj_evicted", nc.vector.tensor_tensor(qa_flat[:, 0:S], proj_bank(g)[:, 0:S], rstd, ALU.mult))
        rotate("q2", qb_flat[:, 1024:1536])
        take_top(TOPK // 8 - 6)
        link(nc.vector.tensor_scalar(dsa_mask, ranking, TAKEN, NEG, ALU.not_equal, ALU.mult))
        link(nc.vector.tensor_tensor(dsa_mask, dsa_mask, const_of("causal"), ALU.add))
        inverse("ckv", rstd_mem)
        mark("ckv_normed", nc.vector.scalar_tensor_tensor(qa_flat[:, 3 * S:4 * S], qa_flat[:, 0:S], vec("ckv_norm", 0),
                                                          rstd_mem, ALU.mult, ALU.mult))
        g = G_DSA + 7
        convert(g + 2)
        take(g, q_mem.rearrange("p c t -> p (c t)"))
        dve.wait_ge(sem("k_nope_done"), 1)
        mark("k_nope_copied", nc.vector.tensor_copy(ka[:, 0, :], bank[1][:, 0:S]))
        dve.wait_ge(sem("k_nope_copied"), 1)
        rotate("k_rope", ka[0:ROPE, 0, :])
        nc.vector.tensor_copy(ka[HD:HD + ROPE, 0, :], ka[0:ROPE, 0, :])
        dve.wait_ge(sem("dsa_v_done"), 1)
        mark("dsa_kv_ready", nc.vector.tensor_copy(va[:, 0:2 * HD], bank[1][:, 0:2 * HD]))
        attend("dsa", mask=lambda h, b: dsa_mask[:, CAUSAL[b][0]:CAUSAL[b][1]])
        attend("mem0", col0=N_TOK * HD)
        turned_o("o0")
        add_slots(G_WO0)
        dve.wait_ge(sem("proj_evicted"), proj_index[G_WO0 + 3] + 1)
        norm("ffn0", lambda c: vec("ffn_norm", c))
        ffn(0)
        dve.wait_ge(sem("x_ready"), 4 * 2)
        norm("attn1", lambda c: vec("attn_norm", DC + c))

        for i in range(3):
            g = G_NSA + i
            convert(g + 2)
            take(g, qa_flat[:, 512 * i:512 * i + 512])
            if i:
                rotate(f"nq{i - 1}", qb_flat[:, 512 * (i - 1):512 * i])
        g = G_NSA + 3
        convert(g + 2)
        take(g, stage[0])
        rotate("nq2", qb_flat[:, 1024:1536])
        for m, name in enumerate(("pos_k", "pos_v")):
            dve.wait_ge(sem("ft_copied"), 4 * m + 4)
            ft = probs_t[m][:, 0:32 * NCMP].rearrange("p (l n) -> p l n", l=16)
            pos = vec_t[:, vec_col[name]:vec_col[name] + 16]
            mark("ft_ready", nc.vector.tensor_tensor(ft, ft, bass.AP(pos.tensor, pos.offset, [pos.ap[0], [1, 16], [0, 2 * NCMP]]),
                                                     ALU.add))
        g = G_NSA + 4
        convert(g + 2)
        take(g, stage[1])
        dve.wait_ge(sem("gelu_done"), 2)
        hv = scores[0][:, 32:32 + 2 * NCMP]
        mark("hv_spread", nc.vector.tensor_copy(
            scores[1][:, 0:2 * HPG * NCMP].rearrange("p (g h c) -> p g h c", g=2, h=HPG),
            bass.AP(hv.tensor, hv.offset, [hv.ap[0], [NCMP, 2], [0, HPG], [1, NCMP]])))
        dve.wait_ge(sem("cmp_out"), 1)
        link(nc.vector.tensor_copy(cmp_k, bank[0][:, 0:2 * NCMP]))
        rows = HPG * NCMP
        for grp in range(2):
            v = bank[1][0:rows, HD * grp:HD * grp + HD]
            ins = nc.vector.tensor_tensor(
                cmp_v[0:rows, grp, :].rearrange("p (h d) -> p h d", h=HPG),
                bass.AP(v.tensor, v.offset, [v.ap[0], [0, HPG], [1, HD]]),
                const_of("own_head", rows).rearrange("p (h d) -> p h d", h=HPG), ALU.mult)
        mark("cmp_kv_ready", ins)
        g = G_NSA + 5
        convert(g + 2)
        take(g, stage[2])

        def both_ways(name, c):
            rotate(name, ka[:, c, :])
            nc.vector.tensor_copy(ka[0:HD, c + 1, :], ka[HD:P, c, :])
            link(nc.vector.tensor_copy(ka[HD:P, c + 1, :], ka[0:HD, c, :]))

        both_ways("ks", 0)
        g = G_NSA + 6
        convert(g + 2)
        take(g, probs[1][0:36, S:2 * S], rows=36, n=1)
        both_ways("kw", 2)
        dve.wait_ge(sem("v_turned"), 3)
        link(nc.vector.tensor_copy(va, bank[1]))
        g = G_NSA + 7
        convert(g + 2)
        take(g, q_mem.rearrange("p c t -> p (c t)"))
        dve.wait_ge(sem("gates_turned"), 1)
        mark("nsa_ready", nc.vector.tensor_copy(gates, bank[2][:, 0:TB * 36]))
        dve.wait_ge(sem("nsa_ready"), 1)
        nb = TB * N_TOK
        dve.wait_ge(sem("cmp_scored"), 1)
        sc3 = scores[1][:, 0:nb * NCMP].rearrange("p (n c) -> p n c", c=NCMP)
        cm = const_of("cmp_mask")
        half = N_TOK // 2
        for b in range(TB):
            for odd in range(2):
                ins = nc.vector.tensor_tensor(
                    sc3[:, b * N_TOK + odd:(b + 1) * N_TOK:2, :],
                    bank[odd][:, b * half * NCMP:(b + 1) * half * NCMP].rearrange("p (n c) -> p n c", c=NCMP),
                    bass.AP(cm.tensor, cm.offset + b * NCMP, [cm.ap[0], [0, half], [1, NCMP]]), ALU.add)
        link(ins)
        mx = factor[:, 128:128 + nb]
        den = factor[:, 160:160 + nb]
        fac = factor[:, 192:192 + nb]
        link(nc.vector.tensor_reduce(mx, sc3, AX.X, ALU.max))
        link(nc.vector.tensor_scalar(mx, mx, NEG / 10, None, ALU.max))

        def per_row(ap, n):
            return bass.AP(ap.tensor, ap.offset, [ap.ap[0], [1, nb], [0, n]])

        link(nc.vector.tensor_tensor(sc3, sc3, per_row(mx, NCMP), ALU.subtract))
        mark("cmp_shifted", nc.vector.tensor_scalar(scores[1][:, 0:nb * NCMP], scores[1][:, 0:nb * NCMP], SCALE, None, ALU.mult))
        dve.wait_ge(sem("cmp_exp"), 1)
        link(nc.vector.tensor_reduce(den, probs[0][:, 0:nb * NCMP].rearrange("p (n c) -> p n c", c=NCMP), AX.X, ALU.add))
        link(nc.vector.tensor_scalar(den, den, 1e-30, None, ALU.max))
        link(nc.vector.reciprocal(fac, den))
        link(nc.vector.tensor_tensor(fac, fac, gates.rearrange("p (n k) -> p n k", k=3)[:, :, 0], ALU.mult))
        dve.wait_ge(sem("cmp_turned"), 1)
        mark("cmp_t_ready", nc.vector.tensor_copy(probs_t[0][0:rows, :], bank[2][0:rows, :]))
        for b in range(TB):
            for grp in range(2):
                dve.wait_ge(sem("cmp_pv"), 2 * b + grp + 1)
                f = fac[:, b * N_TOK + grp * HPG:b * N_TOK + (grp + 1) * HPG]
                w = HPG * HD
                link(nc.vector.tensor_tensor(
                    tok[:, b, grp * w:(grp + 1) * w].rearrange("p (h d) -> p h d", d=HD),
                    bank[4 + 2 * b + grp][:, 0:w].rearrange("p (h d) -> p h d", d=HD),
                    bass.AP(f.tensor, f.offset, [f.ap[0], [1, HPG], [0, HD]]), ALU.mult))
        mark("cmp_evicted", nc.vector.tensor_copy(top8[:, 1:2], fac[:, 0:1]))
        causal = lambda h, b: const_of("causal")[:, CAUSAL[b][0]:CAUSAL[b][1]]
        attend("slc", mask=causal, gate=1)
        attend("win", mask=causal, gate=2)
        attend("mem1", col0=N_TOK * HD)
        turned_o("o1")
        add_slots(G_WO1)
        dve.wait_ge(sem("proj_evicted"), proj_index[G_WO1 + 3] + 1)
        norm("ffn1", lambda c: vec("ffn_norm", DC + c))
        ffn(1)
        dve.wait_ge(sem("x_ready"), 4 * 3)
        rescale_x("final1", lambda c: vec("final_norm", c), "x_ready")

        dve.wait_ge(sem("x_ready"), 4 * 4)
        norm("mix0", lambda c: vec("norm_mix", c))
        dve.wait_ge(sem("t5_rows_done"), 1)
        link(nc.vector.tensor_tensor(tok_flat[0:N_BAND, C_T5:C_T5 + 383], bank[2][0:N_BAND, 0:383],
                                     tok_flat[0:N_BAND, 383:766], ALU.add))
        mark("t5_row_ready", nc.vector.tensor_scalar(tok_flat[0:N_BAND, C_T5:C_T5 + 383], tok_flat[0:N_BAND, C_T5:C_T5 + 383],
                                                     1.0 / SCALE, None, ALU.mult))
        dve.wait_ge(sem("pad_cleared"), 1)
        taps = 0
        for i in range(4):
            g = G_PW1 + 2 * i
            convert(g + 2)
            take(g, probs[0])
            convert(g + 3)
            take(g + 1, scores[0])
            for t in range(2):
                dve.wait_ge(sem("glu_sigmoid"), 2 * i + t + 1)
                if t == 0:
                    evicted(dve, g)
                c = 2 * i + t
                link(nc.vector.scalar_tensor_tensor(glu_pad[:, c, PAD:APAD], probs[0][:, S * t:S * t + S], vec("b_pw1", c),
                                                    scores[1][:, S * t:S * t + S], ALU.add, ALU.mult))
            for k in range(CONV):
                for c in (2 * i, 2 * i + 1):
                    src, w = glu_pad[:, c, k:k + S], vec("w_dw", DC * k + c)
                    if k == 0:
                        ins = nc.vector.tensor_scalar(conv_y[:, c, :], src, w, vec("b_dw", c), ALU.mult, ALU.add)
                    else:
                        dve.wait_ge(sem("tap_done"), taps - 1)
                        ins = nc.vector.scalar_tensor_tensor(conv_y[:, c, :], src, w, conv_y[:, c, :], ALU.mult, ALU.add)
                    mark("tap_done", ins)
                    taps += 1
        dve.wait_ge(sem("ln_summed"), 1)
        mean = probs_t[0][:, 0:S]
        link(nc.vector.tensor_scalar(mean, bank[0][:, 0:S], 1.0 / D, None, ALU.mult))
        for c2 in range(4):
            ys = conv_y[:, 2 * c2:2 * c2 + 2, :]
            mark("centred", nc.vector.tensor_tensor(ys, ys, over_two(mean), ALU.subtract))
        inverse("ln")
        for c2 in range(4):
            ys = conv_y[:, 2 * c2:2 * c2 + 2, :]
            mark("ln_scaled", nc.vector.tensor_tensor(ys, ys, over_two(rstd), ALU.mult))
        split_lo_pairs(prod["conv"], lambda c2: conv_y[:, 2 * c2:2 * c2 + 2, :])
        add_slots(G_PW2, "b_pw2")
        dve.wait_ge(sem("proj_evicted"), proj_index[G_PW2 + 3] + 1)
        norm("ffn2", lambda c: vec("norm_ffn", c))
        ffn(2)

        dve.wait_ge(sem("x_ready"), 4 * 5)
        norm("kv", lambda c: vec("norm_kv", c))
        split_lo(prod["mix1"], x, lambda c: vec("norm_mix", DC + c))
        g = G_KV
        convert(g + 2)
        take(g, ka[:, 0:2, :].rearrange("p c t -> p (c t)"))
        evicted(dve, g)
        nc.vector.tensor_copy(ka[0:HD, 2:4, :], ka[HD:P, 0:2, :])
        link(nc.vector.tensor_copy(ka[HD:P, 2:4, :], ka[0:HD, 0:2, :]))
        convert(g + 3)
        take(g + 1, probs[0])
        for i in range(4):
            g = G_Q + i
            convert(g + 2)
            take(g, qa_flat[:, 512 * i:512 * i + 512])
            if i == 0:
                dve.wait_ge(sem("v_turned"), 4)
                mark("band_v_ready", nc.vector.tensor_copy(va, bank[1]))
        dve.wait_ge(sem("t5_bias_landed"), 64)
        attend("band", mask=lambda h, b: t5_bias[:, h, P:S] if b == 0 else t5_bias[:, h, :],
               init=lambda h: sinks[:, h:h + 1])
        turned_o("o2")
        add_slots(G_WO2)
        dve.wait_ge(sem("proj_evicted"), proj_index[G_WO2 + 3] + 1)
        norm("ffn3", lambda c: vec("norm_ffn", DC + c))
        ffn(3)
        dve.wait_ge(sem("x_ready"), 4 * 6)
        rescale_x("final2", lambda c: vec("norm_final", c), "y_ready")
        for i in range(4):
            dve.wait_ge(sem("y_turned"), i + 1)
            mark("result_ready", nc.vector.tensor_copy(tok[:, i // 2, 512 * (i % 2):512 * (i % 2) + 512], bank[4 + i]))

    @block.tensor
    def _(pe):
        mm = nc.tensor.matmul
        turn = nc.tensor.transpose

        def mark(name, ins):
            ins.then_inc(sem(name), 1)

        def three(out_ap, hi, lo, act_hi, act_lo, start, stop, skip=False):
            mm(out_ap, hi, act_hi, start=start, stop=False, skip_group_check=skip)
            mm(out_ap, hi, act_lo, start=False, stop=False, skip_group_check=skip)
            return mm(out_ap, lo, act_hi, start=False, stop=stop, skip_group_check=skip)

        def project(g, p, fresh=False, j=0):
            w = slots[g][2]
            hi = w_hi[g % NS][:, 0:DC * w].rearrange("p (c n) -> p c n", c=DC)
            lo = w_lo[g % NS][:, 0:DC * w].rearrange("p (c n) -> p c n", c=DC)
            pe.wait_ge(sem("w_lo_done"), g + 1 + 6 * j)
            if proj_index[g] >= 4:
                pe.wait_ge(sem("proj_evicted"), proj_index[g] - 3 + 4 * j)
            for t, n0 in enumerate(range(0, w, P)):
                m = min(P, w - n0)
                for c in range(DC):
                    if fresh and t == 0 and c % 2 == 0:
                        pe.wait_ge(sem("h_ready"), 4 * p + c // 2 + 1)
                    ins = three(proj_bank(g)[0:m, S * t:S * t + S], hi[:, c, n0:n0 + m], lo[:, c, n0:n0 + m],
                                h_hi[p % 2][:, c, :], h_lo[p % 2][:, c, :], c == 0, c == DC - 1)
            mark("slot_used", ins)

        def total(name, src=None):
            if src is None:
                pe.wait_ge(sem("added"), added_no[name] + 1)
                src = qa_flat[:, 0:S]
            mark("sum_ready", mm(bank[0][:, 0:S], ones, src, start=True, stop=True))

        def rotate(name):
            rows, n = rot_shape(name)
            mark("rotated", mm(rot_bank(name)[0:rows, 0:n], const_of("rot", rows)[:, 0:rows], rot_src[name],
                               start=True, stop=True))

        def turn_v(src, dst):
            for t in range(2):
                for b in range(TB):
                    ins = turn(dst[:, S * b + P * t:S * b + P * t + P], src[:, S * t + P * b:S * t + P * b + P], ident)
            mark("v_turned", ins)

        def attend(run, q, k, v, ready):
            first, heads, extent, blocks = RUNS[run]
            ready()

            def qk(n):
                h = n - first
                half = slice(HD * (h % 2), HD * (h % 2) + HD)
                qt = q(h)[half]
                for b in range(TB):
                    lo, hi = extent[b]
                    ins = mm(bank[n % 2][:, lo:hi], qt[:, P * b:P * b + P], k(h)[half, 0:hi - lo], start=True, stop=True)
                mark("qk_done", ins)

            def turn_probs(n):
                pe.wait_ge(sem("exp_done"), n + 1)
                if n >= 2:
                    pe.wait_ge(sem("probs_t_ready"), n - 1)
                for i in range(len(blocks)):
                    ins = turn(bank[2 + n % 2][:, P * i:P * i + P], probs[n % 2][:, P * i:P * i + P], ident)
                mark("probs_turned", ins)

            def pv(n):
                h = n - first
                pe.wait_ge(sem("probs_t_ready"), n + 1)
                if n % 4 == 0 and n >= 8:
                    pe.wait_ge(sem("o_evicted"), n // 4 - 1)
                for b in range(TB):
                    mine = [i for i, (qb_, _) in enumerate(blocks) if qb_ == b]
                    for i in mine:
                        ins = mm(bank[4 + n // 4 % 2][:, S * b + HD * (n % 4):S * b + HD * (n % 4) + HD],
                                 probs_t[n % 2][:, P * i:P * i + P], v(h, blocks[i][1]),
                                 start=i == mine[0], stop=i == mine[-1])
                mark("pv_done", ins)

            qk(first)
            qk(first + 1)
            for n in range(first, first + heads):
                turn_probs(n)
                if n + 2 < first + heads:
                    qk(n + 2)
                if n > first:
                    pv(n - 1)
            pv(first + heads - 1)

        def turn_o(name):
            pe.wait_ge(sem("o_evicted"), {"o0": 4, "o1": 11, "o2": 15}[name])
            for c2 in range(4):
                for c in (2 * c2, 2 * c2 + 1):
                    for b in range(TB):
                        at = S * (c % 2) + P * b
                        ins = turn(bank[c2][:, at:at + P], tok[:, b, P * c:P * c + P], ident)
                mark("o_turned", ins)

        def turn_tokens(src, banks, name):
            for c2 in range(4):
                for c in (2 * c2, 2 * c2 + 1):
                    for b in range(TB):
                        at = S * (c % 2) + P * b
                        ins = turn(banks[c2][:, at:at + P], src[:, b, P * c:P * c + P], ident)
                mark(name, ins)

        def ffn(f, p):
            first = FF[f][0]
            n0 = FF_STEPS * f

            def down(s, g, j=0, start=False, stop=False):
                pe.wait_ge(sem("w_lo_done"), g + 1 + 6 * j)
                pe.wait_ge(sem("ff_ready"), n0 + s + 1 + 2 * j)
                hi = w_hi[g % NS].rearrange("p (c n) -> p c n", c=2)
                lo = w_lo[g % NS].rearrange("p (c n) -> p c n", c=2)
                for m in range(DC):
                    for c in range(2):
                        ins = three(bank[m // 2][:, S * (m % 2):S * (m % 2) + S], hi[:, c, P * m:P * m + P],
                                    lo[:, c, P * m:P * m + P], ff_hi[s % 2][:, S * c:S * c + S],
                                    ff_lo[s % 2][:, S * c:S * c + S], start and c == 0 and m % 2 == 0,
                                    stop and c == 1 and m % 2 == 1, skip=True)
                    if stop and m % 2 == 1:
                        mark("down_done", ins)
                if not stop:
                    mark("slot_used", ins)

            def step(s, j=0):
                g = first + 3 * s - 1
                project(g, p, j=j)
                project(g + 1, p, j=j)
                down(s - 1, g + 2, j, start=(s == 1))

            project(first, p, fresh=True)
            total(PROD[p])
            project(first + 1, p)
            pe.wait_ge(sem("root_done"), sum_no[PROD[p]] + 1)
            step(1)
            with pe.Fori(0, (FF_STEPS - 3) // 2) as j:
                step(2, j)
                step(3, j)
            step(FF_STEPS - 1)
            down(FF_STEPS - 1, first + 3 * FF_STEPS - 1, stop=True)
            pe.wait_ge(sem("down_done"), 4 * f + 4)
            pe.nop().then_inc(sem("slot_used"), 1)

        pe.wait_ge(sem("const_landed"), 16)
        pe.wait_ge(sem("vec_landed"), VEC_ALL)
        for t in range(4):
            ins = turn(bank[1][:, P * t:P * t + P], vec_tok[:, t, :], ident)
        mark("vec_turned", ins)
        pe.wait_ge(sem("mem_landed"), 16)
        turn_tokens(mem_tok, bank[4:8], "mem_t_done")
        pe.wait_ge(sem("cleared"), 4)
        total("mem")
        pe.wait_ge(sem("root_done"), 1)
        pe.wait_ge(sem("vec_ready"), 1)
        pe.wait_ge(sem("x_landed"), 16)
        turn_tokens(tok, bank[0:4], "x_t_done")
        for layer in range(2):
            g = G_MEM[layer]
            p = prod[f"mem{layer}"]
            project(g, p, fresh=True)
            project(g + 1, p)
            pe.wait_ge(sem("x_ready"), 4)
            evicted(pe, g + 1)
            turn_v(probs[layer], bank[1 + layer])
        p = prod["attn0"]
        g = G_DSA
        project(g, p, fresh=True)
        total("attn0")
        project(g + 1, p)
        pe.wait_ge(sem("v_mem_ready"), 2)
        evicted(pe, g)
        rotate("k_idx")
        for b in range(TB):
            ins = turn(bank[1][:, N_IDX * b:N_IDX * b + N_IDX], stage[2][HD:HD + N_IDX, P * b:P * b + P],
                       ident[HD:HD + N_IDX, HD:HD + N_IDX])
        mark("w_idx_turned", ins)
        project(g + 2, p)
        evicted(pe, g + 1)
        rotate("q_idx0")
        evicted(pe, g + 2)
        rotate("q_idx1")
        project(g + 3, p)
        pe.wait_ge(sem("idx_inputs"), 1)
        for h in range(N_IDX):
            half = slice(HD * (h % 2), HD * (h % 2) + HD)
            if h >= 2:
                pe.wait_ge(sem("idx_relu"), h - 1)
            for b, (lo, hi) in enumerate(CAUSAL):
                ins = mm(bank[h % 2][:, lo:hi], qa[half, 4 + h // 2, P * b:P * b + P], ka[half, 1, 0:hi - lo],
                         start=True, stop=True)
            mark("idx_scored", ins)
        for i in range(3):
            project(g + 4 + i, p)
            evicted(pe, g + 3 + i)
            rotate(f"q{i}")
        pe.wait_ge(sem("ckv_squared"), 1)
        pe.wait_ge(sem("idx_relu"), N_IDX)
        total("ckv", qa_flat[:, 2 * S:3 * S])
        project(g + 7, p)
        pe.wait_ge(sem("ckv_normed"), 1)
        pe.wait_ge(sem("small_landed"), SMALL_ALL)
        ckv = qa_flat[:, 3 * S:4 * S]
        mark("k_nope_done", mm(bank[1][:, 0:S], w_uk, ckv, start=True, stop=True))
        rotate("k_rope")
        pe.wait_ge(sem("k_nope_copied"), 1)
        for b in range(TB):
            ins = mm(bank[1][:, HD * b:HD * b + HD], ckv[:, P * b:P * b + P], w_uv, start=True, stop=True)
        mark("dsa_v_done", ins)

        def dsa_ready():
            pe.wait_ge(sem("dsa_kv_ready"), 1)

        attend("dsa", lambda h: qb[:, h // 2, :], lambda h: ka[:, 0, :],
               lambda h, kb: va[:, HD * kb:HD * kb + HD], dsa_ready)
        attend("mem0", lambda h: q_mem[:, h // 2, :], lambda h: k_mem[:, 0, h // 2, :],
               lambda h, kb: v_mem[:, 0, kb, HD * h:HD * h + HD], lambda: None)
        turn_o("o0")
        for i in range(4):
            project(G_WO0 + i, prod["o0"], fresh=(i == 0))
        ffn(0, prod["ffn0"])
        p = prod["attn1"]
        g = G_NSA
        project(g, p, fresh=True)
        total("attn1")
        for i in range(3):
            project(g + 1 + i, p)
            evicted(pe, g + i)
            rotate(f"nq{i}")
        pe.wait_ge(sem("cmp_w1_landed"), 32)
        for m in range(2):
            pe.wait_ge(sem("ft_ready"), m + 1)
            for l in range(16):
                ins = mm(bank[m][:, 0:2 * NCMP], cmp_w1[:, m, l, :], probs_t[m][:, 2 * NCMP * l:2 * NCMP * (l + 1)],
                         start=(l == 0), stop=(l == 15))
            mark("cmp_hidden", ins)
        project(g + 4, p)
        pe.wait_ge(sem("hv_spread"), 1)
        mm(bank[0][:, 0:2 * NCMP], cmp_w2[:, 0:2 * HD], scores[0][:, 0:2 * NCMP], start=True, stop=True)
        rows = HPG * NCMP
        for grp in range(2):
            ins = mm(bank[1][0:rows, HD * grp:HD * grp + HD], scores[1][:, rows * grp:rows * (grp + 1)],
                     cmp_w2[:, 2 * HD:3 * HD], start=True, stop=True)
        mark("cmp_out", ins)
        project(g + 5, p)
        rotate("ks")
        project(g + 6, p)
        evicted(pe, g + 5)
        rotate("kw")
        pe.wait_ge(sem("cmp_kv_ready"), 1)
        for k in range(2):
            for b in range(TB):
                ins = turn(bank[1][:, S * k + P * b:S * k + P * b + P], stage[1 + k][:, S + P * b:S + P * b + P], ident)
        mark("v_turned", ins)
        project(g + 7, p)
        pe.wait_ge(sem("gates_open"), 1)
        evicted(pe, g + 7)
        for b in range(TB):
            ins = turn(bank[2][:, 36 * b:36 * b + 36], probs[1][0:36, P * b:P * b + P], ident[0:36, 0:36])
        mark("gates_turned", ins)
        for b in range(TB):
            for h in range(N_TOK):
                half = slice(HD * (h % 2), HD * (h % 2) + HD)
                at = (b * N_TOK // 2 + h // 2) * NCMP
                ins = mm(bank[h % 2][:, at:at + NCMP], qa[half, h // 2, P * b:P * b + P],
                         cmp_k[half, NCMP * (h // HPG):NCMP * (h // HPG + 1)], start=True, stop=True)
        mark("cmp_scored", ins)
        pe.wait_ge(sem("cmp_exp"), 1)
        pe.wait_ge(sem("nsa_ready"), 1)
        for b in range(TB):
            for grp in range(2):
                i = 2 * b + grp
                ins = turn(bank[2][0:rows, P * i:P * i + P], probs[0][:, rows * i:rows * (i + 1)], ident)
        mark("cmp_turned", ins)
        pe.wait_ge(sem("cmp_t_ready"), 1)
        for i in range(4):
            mark("cmp_pv", mm(bank[4 + i][:, 0:HPG * HD], probs_t[0][0:rows, P * i:P * i + P], cmp_v[0:rows, i % 2, :],
                              start=True, stop=True))

        def nsa_k(first_tile):
            return lambda h: ka[:, first_tile + (h // HPG != h % 2), :]

        def nsa_v(k):
            return lambda h, kb: va[:, S * k + P * kb + HD * (h // HPG):S * k + P * kb + HD * (h // HPG) + HD]

        attend("slc", lambda h: qb[:, h // 2, :], nsa_k(0), nsa_v(0), lambda: pe.wait_ge(sem("cmp_evicted"), 1))
        attend("win", lambda h: qb[:, h // 2, :], nsa_k(2), nsa_v(1), lambda: None)
        attend("mem1", lambda h: q_mem[:, h // 2, :], lambda h: k_mem[:, 1, h // 2, :],
               lambda h, kb: v_mem[:, 1, kb, HD * h:HD * h + HD], lambda: None)
        turn_o("o1")
        for i in range(4):
            project(G_WO1 + i, prod["o1"], fresh=(i == 0))
        ffn(1, prod["ffn1"])
        total("final1")
        p = prod["mix0"]
        pe.wait_ge(sem("t5_landed"), 16)
        pe.wait_ge(sem("x_ready"), 4 * 3)
        mark("t5_rows_done", mm(bank[2][0:N_BAND, 0:383], rel_bias[0:BUCKETS, :], tok_flat[0:BUCKETS, 0:383],
                                start=True, stop=True))
        project(G_PW1, p, fresh=True)
        total("mix0")
        for g in range(G_PW1 + 1, G_PW1 + 8):
            project(g, p)
        pe.wait_ge(sem("root_done"), sum_no["mix0"] + 1)
        for c in range(DC):
            pe.wait_ge(sem("tap_done"), 2 * CONV * (c // 2 + 1))
            ins = mm(bank[0][:, 0:S], ones, conv_y[:, c, :], start=(c == 0), stop=(c == DC - 1))
        mark("ln_summed", ins)
        total("ln")
        for i in range(4):
            project(G_PW2 + i, prod["conv"], fresh=(i == 0))
        ffn(2, prod["ffn2"])
        project(G_KV, prod["kv"], fresh=True)
        total("kv")
        project(G_KV + 1, prod["kv"])
        project(G_Q, prod["mix1"], fresh=True)
        evicted(pe, G_KV + 1)
        turn_v(probs[0], bank[1])
        for g in range(G_Q + 1, G_Q + 4):
            project(g, prod["mix1"])

        def band_ready():
            pe.wait_ge(sem("band_v_ready"), 1)
            evicted(pe, G_Q + 3)

        attend("band", lambda h: qa[:, h // 2, :],
               lambda h: ka[:, h // 8 + (0 if (h // 4) % 2 == h % 2 else 2), :],
               lambda h, kb: va[:, S * kb + HD * (h // 4):S * kb + HD * (h // 4) + HD], band_ready)
        turn_o("o2")
        for i in range(4):
            project(G_WO2 + i, prod["o2"], fresh=(i == 0))
        ffn(3, prod["ffn3"])
        total("final2")
        for i in range(4):
            b = i // 2
            for k in range(4):
                c = 4 * (i % 2) + k
                if b == 0 and c % 2 == 0:
                    pe.wait_ge(sem("y_ready"), c // 2 + 1)
                ins = turn(bank[4 + i][:, P * k:P * k + P], x[:, c, P * b:P * b + P], ident)
            mark("y_turned", ins)


_INS = ["x", "mem", "attn_norm", "mem_norm", "ffn_norm", "final_norm", "dsa_w_in", "dsa_ckv_norm", "dsa_w_uk",
        "dsa_w_uv", "nsa_w_in", "nsa_cmp_pos_k", "nsa_cmp_pos_v", "nsa_cmp_k_w1", "nsa_cmp_k_w2",
        "nsa_cmp_v_w1", "nsa_cmp_v_w2", "mem_w_kv", "w_o", "ffn_w_in", "ffn_w_down", "norm_mix_2",
        "norm_ffn_2", "conv_w_pw1_2", "conv_b_pw1_2", "conv_w_dw_2", "conv_b_dw_2", "conv_ln_g_2",
        "conv_ln_b_2", "conv_w_pw2_2", "conv_b_pw2_2", "norm_kv_2", "w_kv_2", "w_q_2", "w_o_2", "sinks_2",
        "rel_bias_2", "ffn_w_up_2", "ffn_w_down_2", "norm_final_2"]


def kernel(**inputs):
    import concourse.bacc as bacc
    from concourse.bass_utils import run_bass_kernel_spmd

    nc = bacc.Bacc("TRN2", target_bir_lowering=False, num_devices=1)
    arrays = {name: np.ascontiguousarray(inputs[name]) for name in _INS}
    arrays["const"] = constants()
    io = {name: nc.dram_tensor(f"in_{name}", a.shape, mybir.dt.from_np(a.dtype), kind="ExternalInput").ap()
          for name, a in arrays.items()}
    out = nc.dram_tensor("result", (1, S, D), F32, kind="ExternalOutput").ap()
    build(nc, io, out)
    r = run_bass_kernel_spmd(nc, [{f"in_{name}": a for name, a in arrays.items()}], core_ids=[0])
    return r.results[0]["result"]
```

```python
from contextlib import ExitStack

import numpy as np

import concourse.bass as bass
from concourse import mybir

F32 = mybir.dt.float32
F32R = mybir.dt.float32r
ALU = mybir.AluOpType
ACT = mybir.ActivationFunctionType
AX = mybir.AxisListType

P = 128
S = 256
D = 1024
DC = D // P
TB = S // P
DFF = 2816
HD = 64
N_TOK, N_MEM_H, N_BAND = 12, 4, 16
N_IDX = 8
TOPK = min(256, S // 4)
ROPE = 16
EPS = 1e-6
SCALE = HD ** -0.5
NEG = -1e30
LATER = 3.0e8
TAKEN = -3.3e38
CMP_LEN, CMP_STRIDE = 32, 16
NCMP = (S - CMP_LEN) // CMP_STRIDE + 1
HPG = 6
BUCKETS = 32
CONV = 31
SLOT = 2048
NR = 3
NS = 3
FF_STEPS = DFF // 256


def rope_constants():
    inv = 500000.0 ** (-np.arange(0, ROPE, 2, dtype=np.float64) / ROPE)
    ang = np.arange(S, dtype=np.float64)[:, None] * inv[None, :]
    cos, sin = np.cos(ang).astype(np.float32).T, np.sin(ang).astype(np.float32).T
    c, s = np.ones((P, S), np.float32), np.zeros((P, S), np.float32)
    rot = np.zeros((P, P), np.float32)
    half = ROPE // 2
    for h in range(0, P, HD):
        c[h:h + half], c[h + half:h + ROPE] = cos, cos
        s[h:h + half], s[h + half:h + ROPE] = sin, sin
        for d in range(half):
            rot[h + half + d, h + d] = -1.0
            rot[h + d, h + half + d] = 1.0
    return c, s, rot


def t5_bucket(dist):
    max_exact = BUCKETS // 2
    d = np.maximum(dist, 0)
    ratio = (np.log(np.maximum(d, 1).astype(np.float32) / np.float32(max_exact)).astype(np.float32)
             / np.float32(np.log(128 / max_exact)))
    large = max_exact + (ratio * np.float32(BUCKETS - max_exact)).astype(np.int32)
    return np.where(d < max_exact, d, np.minimum(large, BUCKETS - 1))


CONST_COLS = {}


def constants():
    c, s, rot = rope_constants()
    q, k = np.arange(P)[:, None], np.arange(S)[None, :]
    causal = np.concatenate([np.where(k[:, :P] <= q, 0, NEG), np.where(k <= q + P, 0, NEG)], 1)
    end = np.arange(NCMP) * CMP_STRIDE + CMP_LEN - 1
    cmp_mask = np.concatenate([np.where(end[None] <= q + P * b, 0, NEG) for b in range(TB)], 1)
    row = np.arange(P)[:, None]
    own_head = row // NCMP == np.arange(HPG)[None]
    dist = 255 - np.arange(383)
    inside = (dist >= 0) & (dist < P)
    onehot = np.zeros((P, 383))
    onehot[:BUCKETS] = (t5_bucket(dist)[None] == np.arange(BUCKETS)[:, None]) & inside[None]
    outside = np.broadcast_to(np.where(inside, 0, NEG)[None], (P, 383))
    parts = [("ident", np.eye(P)), ("rot", rot), ("cos", c), ("sin", s), ("causal", causal),
             ("cmp_mask", cmp_mask), ("own_head", own_head),
             ("onehot", onehot), ("outside", outside)]
    at = 0
    for name, a in parts:
        CONST_COLS[name] = (at, at + a.shape[1])
        at += a.shape[1]
    return np.ascontiguousarray(np.concatenate([a for _, a in parts], 1).astype(np.float32))


constants()
C_MAIN = CONST_COLS["onehot"][0]
C_T5 = CONST_COLS["outside"][1] - C_MAIN


def build(nc, io, out):
    ctx = ExitStack()
    with ctx:
        _build(nc, ctx, io, out)


def _build(nc, ctx, io, out):
    def sb(name, cols, dt=F32):
        return ctx.enter_context(nc.sbuf_tensor(name, [P, cols], dt))[:, :]

    sems = {}

    def sem(name):
        if name not in sems:
            sems[name] = ctx.enter_context(nc.semaphore(name))
        return sems[name]

    raw = [sb(f"raw{i}", SLOT) for i in range(NR)]
    w_hi = [sb(f"w_hi{i}", SLOT, F32R) for i in range(NS)]
    w_lo = [sb(f"w_lo{i}", SLOT, F32R) for i in range(NS)]
    h_hi = [sb(f"h_hi{i}", DC * S, F32R).rearrange("p (c t) -> p c t", t=S) for i in range(2)]
    h_lo = [sb(f"h_lo{i}", DC * S, F32R).rearrange("p (c t) -> p c t", t=S) for i in range(2)]
    ff_hi = [sb(f"ff_hi{i}", 2 * S, F32R) for i in range(2)]
    ff_lo = [sb(f"ff_lo{i}", 2 * S, F32R) for i in range(2)]
    x_flat = sb("x", DC * S)
    x = x_flat.rearrange("p (c t) -> p c t", t=S)
    rstd = sb("rstd", S)
    rstd_mem = sb("rstd_mem", S)
    tok_flat = sb("tok", TB * D)
    tok = tok_flat.rearrange("p (b n) -> p b n", n=D)
    PAD = CONV - 1
    APAD = S + PAD
    big = sb("big", max(DC * APAD + DC * S, 32 * P, N_BAND * S))
    mem_tok = big[:, 0:TB * D].rearrange("p (b n) -> p b n", n=D)
    mem_t = big[:, TB * D:2 * TB * D].rearrange("p (c t) -> p c t", t=S)
    cmp_w1 = big[:, 0:32 * P].rearrange("p (m l h) -> p m l h", m=2, l=16)
    glu_pad = big[:, 0:DC * APAD].rearrange("p (c t) -> p c t", t=APAD)
    conv_y = big[:, DC * APAD:DC * APAD + DC * S].rearrange("p (c t) -> p c t", t=S)
    t5_bias = big[:, 0:N_BAND * S].rearrange("p (h k) -> p h k", k=S)
    qa_flat = sb("qa", 8 * S)
    qa = qa_flat.rearrange("p (c t) -> p c t", t=S)
    qb_flat = sb("qb", 6 * S)
    qb = qb_flat.rearrange("p (c t) -> p c t", t=S)
    va = sb("va", 2 * S)
    q_mem = sb("q_mem", 2 * S).rearrange("p (c t) -> p c t", t=S)
    keys = sb("keys", 8 * S).rearrange("p (c t) -> p c t", t=S)
    k_mem = [keys[:, 4:8], sb("k_mem1", 4 * S).rearrange("p (h t) -> p h t", h=N_MEM_H)]
    v_mem = sb("v_mem", 4 * S).rearrange("p (l b n) -> p l b n", l=2, b=2)
    scores = [sb(f"scores{i}", 2 * S) for i in range(2)]
    probs = [sb(f"probs{i}", 2 * S) for i in range(2)]
    probs_t = [sb(f"probs_t{i}", 2 * S) for i in range(2)]
    rms = probs_t[1][:, 0:S]
    dsa_flat = sb("dsa_flat", 6 * P)
    dsa_mask, ranking = dsa_flat[:, 0:3 * P], dsa_flat[:, 3 * P:6 * P]
    cmp_v = dsa_flat.rearrange("p (g n) -> p g n", g=2)
    cmp_k = sb("cmp_k", 4 * NCMP).rearrange("p (h n) -> p h n", h=2)
    sink_exp = sb("sink_exp", 2 * N_BAND)
    top8 = sb("top8", 16)
    shift = sb("shift", 128)
    row_sum = sb("row_sum", 128)
    factor = sb("factor", 256)
    gates = sb("gates", TB * 36)
    w_idx = sb("w_idx", TB * N_IDX)
    vec_t = sb("vec_t", 4 * P)
    const = sb("const", C_MAIN)
    ones = sb("ones", P)
    w_uk = sb("w_uk", P)
    w_uv = sb("w_uv", HD)
    cmp_w2 = sb("cmp_w2", 3 * HD)
    rel_bias = sb("rel_bias", N_BAND)
    sinks = sb("sinks", N_BAND)
    neg_sinks = sb("neg_sinks", N_BAND)
    eps_col = sb("eps_col", 1)
    bank = [ctx.enter_context(nc.psum_tensor(f"bank{i}", [P, 512], F32))[:, :] for i in range(8)]
    t5_row = nc.dram_tensor("t5_row", [P, N_BAND, 383], F32, kind="Internal").ap()

    def const_of(name, rows=P):
        a, b = CONST_COLS[name]
        return const[0:rows, a:b]

    ident = const_of("ident")
    rope_t = tok_flat[:, 0:512]
    stage = [tok_flat[:, 512 * k + 512:512 * k + 1024] for k in range(3)]
    t5_const = tok_flat[:, 0:C_T5]

    vec_rows, vec_col = [], {}

    def rows_of(name, ap, n):
        vec_col[name] = len(vec_rows)
        vec_rows.extend((name, ap, r) for r in range(n))

    def as_rows(ap):
        return ap.rearrange("a (r c) -> (a r) c", c=P)

    for name in ("attn_norm", "mem_norm", "ffn_norm"):
        rows_of(name, as_rows(io[name]), 16)
    rows_of("final_norm", io["final_norm"].rearrange("(r c) -> r c", c=P), 8)
    rows_of("ckv_norm", io["dsa_ckv_norm"], 1)
    rows_of("norm_mix", as_rows(io["norm_mix_2"]), 16)
    rows_of("norm_ffn", as_rows(io["norm_ffn_2"]), 16)
    rows_of("b_pw1", as_rows(io["conv_b_pw1_2"]), 16)
    rows_of("w_dw", io["conv_w_dw_2"][0].rearrange("k (r c) -> (k r) c", c=P), CONV * DC)
    for name, src in (("b_dw", "conv_b_dw_2"), ("ln_g", "conv_ln_g_2"), ("ln_b", "conv_ln_b_2"),
                      ("b_pw2", "conv_b_pw2_2")):
        rows_of(name, as_rows(io[src]), 8)
    rows_of("norm_kv", io["norm_kv_2"].rearrange("(r c) -> r c", c=P), 8)
    rows_of("norm_final", io["norm_final_2"].rearrange("(r c) -> r c", c=P), 8)
    for name, src in (("pos_k", "nsa_cmp_pos_k"), ("pos_v", "nsa_cmp_pos_v")):
        rows_of(name, io[src][0].rearrange("(l two) d -> l (two d)", two=2), 16)
    assert len(vec_rows) <= 4 * P
    vec_tok = qb_flat[:, 0:4 * P].rearrange("p (t c) -> p t c", c=P)

    def vec(name, c):
        k = vec_col[name] + c
        return vec_t[:, k:k + 1]

    slots = []

    def cols(w, n0, n1):
        slots.append((w[:, n0:n1].rearrange("(c p) n -> p c n", p=P), DC, n1 - n0))

    def stage_slots(name, ranges):
        first = len(slots)
        for w, n0, n1 in ranges:
            cols(w, n0, n1)
        return first

    def ffn_slots(w_in, w_down):
        first = len(slots)
        for s in range(FF_STEPS + 1):
            if s < FF_STEPS:
                cols(w_in, 256 * s, 256 * s + 256)
                cols(w_in, DFF + 256 * s, DFF + 256 * s + 256)
            if s >= 1:
                slots.append((w_down[256 * (s - 1):256 * s, :].rearrange("(c p) n -> p c n", p=P), 2, D))
        return first, w_in, w_down

    kv0, kv1 = io["mem_w_kv"][0], io["mem_w_kv"][1]
    dsa, nsa = io["dsa_w_in"][0], io["nsa_w_in"][0]
    G_MEM = [stage_slots("mem0", [(kv0, 0, 256), (kv0, 256, 512)]),
             stage_slots("mem1", [(kv1, 0, 256), (kv1, 256, 512)])]
    G_DSA = stage_slots("dsa", [(dsa, 1424, 1496), (dsa, 912, 1168), (dsa, 1168, 1424), (dsa, 0, 256),
                                (dsa, 256, 512), (dsa, 512, 768), (dsa, 768, 912), (dsa, 1496, 1752)])
    G_WO0 = stage_slots("wo0", [(io["w_o"][0], 256 * i, 256 * i + 256) for i in range(4)])
    FF = [ffn_slots(io["ffn_w_in"][0], io["ffn_w_down"][0])]
    G_NSA = stage_slots("nsa", [(nsa, 256 * i, 256 * i + 256) for i in range(6)]
                        + [(nsa, 1536, 1572), (nsa, 1572, 1828)])
    G_WO1 = stage_slots("wo1", [(io["w_o"][1], 256 * i, 256 * i + 256) for i in range(4)])
    FF.append(ffn_slots(io["ffn_w_in"][1], io["ffn_w_down"][1]))
    pw1, pw2 = io["conv_w_pw1_2"][0], io["conv_w_pw2_2"][0]
    G_PW1 = stage_slots("pw1", [r for i in range(4) for r in
                                ((pw1, 256 * i, 256 * i + 256), (pw1, D + 256 * i, D + 256 * i + 256))])
    G_PW2 = stage_slots("pw2", [(pw2, 256 * i, 256 * i + 256) for i in range(4)])
    FF.append(ffn_slots(io["ffn_w_up_2"][0], io["ffn_w_down_2"][0]))
    G_KV = stage_slots("kv", [(io["w_kv_2"], 0, 256), (io["w_kv_2"], 256, 512)])
    G_Q = stage_slots("q", [(io["w_q_2"][0], 256 * i, 256 * i + 256) for i in range(4)])
    G_WO2 = stage_slots("wo2", [(io["w_o_2"][0], 256 * i, 256 * i + 256) for i in range(4)])
    FF.append(ffn_slots(io["ffn_w_up_2"][1], io["ffn_w_down_2"][1]))
    NSLOT = len(slots)

    proj_index, n = [], 0
    for g, (_, chunks, _) in enumerate(slots):
        proj_index.append(n if chunks == DC else None)
        n += chunks == DC

    proj_index, n = [], 0
    for _, chunks, _ in slots:
        proj_index.append(n)
        n += chunks == DC

    PROD = ["mem0", "mem1", "attn0", "o0", "ffn0", "attn1", "o1", "ffn1", "mix0", "conv", "ffn2",
            "kv", "mix1", "o2", "ffn3"]
    prod = {name: i for i, name in enumerate(PROD)}
    ff_last = [f[0] + 3 * FF_STEPS - 3 for f in FF]
    last_use = [G_MEM[0] + 1, G_MEM[1] + 1, G_DSA + 7, G_WO0 + 3, ff_last[0], G_NSA + 7, G_WO1 + 3,
                ff_last[1], G_PW1 + 7, G_PW2 + 3, ff_last[2], G_KV + 1, G_Q + 3, G_WO2 + 3, ff_last[3]]

    SUMS = ["mem", "attn0", "ckv", "ffn0", "attn1", "ffn1", "final1", "mix0", "ln", "ffn2", "kv",
            "ffn3", "final2"]
    sum_no = {name: i for i, name in enumerate(SUMS)}
    ADDED = [name for name in SUMS if name not in ("ckv", "ln")]
    added_no = {name: i for i, name in enumerate(ADDED)}

    UPDATE = ["load", "ff0", "ff1", "renorm", "ff2", "ff3"]
    BY_SLOT = {"wo0": G_WO0, "wo1": G_WO1, "pw2": G_PW2, "wo2": G_WO2}

    CAUSAL = [(0, P), (P, 3 * P)]
    FULL = [(0, 2 * P), (2 * P, 4 * P)]
    CAUSAL_BLOCKS = [(0, 0), (1, 0), (1, 1)]
    FULL_BLOCKS = [(0, 0), (0, 1), (1, 0), (1, 1)]
    RUNS, n = {}, 0
    for name, heads in (("dsa", N_TOK), ("mem0", N_MEM_H), ("slc", N_TOK), ("win", N_TOK),
                        ("mem1", N_MEM_H), ("band", N_BAND)):
        full = name.startswith("mem")
        RUNS[name] = (n, heads, FULL if full else CAUSAL, FULL_BLOCKS if full else CAUSAL_BLOCKS)
        n += heads
    TURNED = {"o0": 0, "o1": 1, "o2": 2}

    POOL_CHUNKS, PE_CHUNKS = (0, 2, 4), (5, 7)
    DVE_CHUNKS = tuple(c for c in range(DC) if c not in POOL_CHUNKS + PE_CHUNKS)
    PAIRS = (CONV + 1) // 2
    NPAIR, NDIAG = 3, 16
    pair_of = lambda j: qb_flat[:, 512 * (j % NPAIR):512 * (j % NPAIR) + 512]
    diag_of = lambda j: qa_flat[:, P * (j % NDIAG):P * (j % NDIAG) + P]

    ROT = ["k_idx", "q_idx0", "q_idx1", "q0", "q1", "q2", "k_rope",
           "nq0", "nq1", "nq2", "ks", "kw"]
    rot_no = {name: i for i, name in enumerate(ROT)}
    rot_src = {
        "k_idx": stage[2][0:HD, 0:S], "q_idx0": stage[0], "q_idx1": stage[1],
        "q0": stage[0], "q1": stage[1], "q2": stage[0], "k_rope": qa_flat[0:ROPE, S:2 * S],
        "nq0": qa_flat[:, 0:512], "nq1": qa_flat[:, 512:1024], "nq2": qa_flat[:, 1024:1536],
        "ks": stage[1][:, 0:S], "kw": stage[2][:, 0:S],
    }

    def rot_shape(name):
        src = rot_src[name]
        return src.shape[0], src.shape[1]

    def rot_bank(name):
        return bank[2 + rot_no[name] % 2]

    def landed(eng, g, j=0):
        eng.wait_ge(sem(f"raw_landed{g % NR}"), 16 * (g // NR + 1) + 32 * j)

    def slot_cols(g):
        return slots[g][1] * slots[g][2]

    def proj_bank(g):
        return bank[4 + proj_index[g] % 4]

    def used(eng, g, j=0):
        eng.wait_ge(sem("slot_used"), g + 1 + 6 * j)

    def evicted(eng, g, j=0):
        eng.wait_ge(sem("proj_evicted"), proj_index[g] + 1 + 4 * j)

    def x_updated(eng, u, c2):
        if u in BY_SLOT:
            evicted(eng, BY_SLOT[u] + c2)
        else:
            eng.wait_ge(sem("x_ready"), 4 * UPDATE.index(u) + c2 + 1)

    def set_free(eng, p):
        if p >= 2:
            used(eng, last_use[p - 2])

    def halves(ap):
        return ap.rearrange("p (c t) -> p c t", t=S)

    def over_two(ap):
        return bass.AP(ap.tensor, ap.offset, [ap.ap[0], [0, 2], ap.ap[1]])

    block = ctx.enter_context(nc.Block())

    @block.sync
    def _(sp):
        def load(g, j=0, src=None):
            ap, chunks, w = slots[g]
            if g >= NR:
                sp.wait_ge(sem("w_lo_done"), g - NR + 1 + 6 * j)
            sp.dma_start(raw[g % NR][:, 0:chunks * w].rearrange("p (c n) -> p c n", c=chunks),
                         ap if src is None else src).then_inc(sem(f"raw_landed{g % NR}"), 16)

        def ffn(first, w_in, w_down):
            for g in range(first, first + 5):
                load(g)
            with sp.Fori(0, (FF_STEPS - 3) // 2) as j:
                for u in (0, 1):
                    g = first + 5 + 3 * u
                    n0 = 256 * (2 + u)
                    gate = w_in[:, bass.ds(512 * j + n0, 256)].rearrange("(c p) n -> p c n", p=P)
                    up = w_in[:, bass.ds(512 * j + n0 + DFF, 256)].rearrange("(c p) n -> p c n", p=P)
                    down = w_down[bass.ds(512 * j + n0 - 256, 256), :].rearrange("(c p) n -> p c n", p=P)
                    load(g, j, gate)
                    load(g + 1, j, up)
                    load(g + 2, j, down)
            for g in range(first + 3 * FF_STEPS - 4, first + 3 * FF_STEPS):
                load(g)

        for b in range(TB):
            sp.dma_start(mem_tok[:, b, :], io["mem"][0, P * b:P * b + P, :]).then_inc(sem("mem_landed"), 16)
        g = 0
        firsts = {f[0]: f for f in FF}
        while g < NSLOT:
            if g in firsts:
                ffn(*firsts[g])
                g += 3 * FF_STEPS
            else:
                load(g)
                g += 1
        for b in range(TB):
            sp.wait_ge(sem("result_ready"), 2 * (b + 1))
            sp.dma_start(out[0, b * P:(b + 1) * P, :], tok[:, b, :]).then_inc(sem("out_written"), 16)
        sp.wait_ge(sem("out_written"), 16 * TB)
        sp.wait_ge(sem("t5_stored"), 16)

    pieces, r = [], 0
    while r < len(vec_rows):
        name, ap, r0 = vec_rows[r]
        m = 1
        while r + m < len(vec_rows) and vec_rows[r + m][0] == name and (r + m) % P:
            m += 1
        pieces.append((r, m, ap[r0:r0 + m, :]))
        r += m
    VEC_ALL, SMALL_ALL = 16 * len(pieces), 16 * 8

    @block.gpsimd
    def _(pool):
        def add_squares(name):
            k = added_no[name]
            for i in range(1, 4):
                pool.wait_ge(sem("squared"), 4 * k + i + 1)
                if i > 1:
                    pool.wait_ge(sem("partly_added"), 3 * k + i - 1)
                pool.tensor_tensor(qa_flat[:, 0:512], qa_flat[:, 0:512], qa_flat[:, 512 * i:512 * i + 512],
                                   ALU.add).then_inc(sem("partly_added"), 1)
            pool.wait_ge(sem("partly_added"), 3 * k + 3)
            pool.tensor_tensor(qa_flat[:, 0:S], qa_flat[:, 0:S], qa_flat[:, S:2 * S],
                               ALU.add).then_inc(sem("added"), 1)

        def clear_keys(tiles, k):
            if k:
                pool.wait_ge(sem("keys_cleared"), 2 * k)
            pool.memset(tiles[0:HD, 1::2, :], 0.0).then_inc(sem("keys_cleared"), 1)
            pool.wait_ge(sem("keys_cleared"), 2 * k + 1)
            pool.memset(tiles[HD:P, 0::2, :], 0.0).then_inc(sem("keys_cleared"), 1)

        pool.memset(vec_tok, 0.0).then_inc(sem("cleared"), 1)
        pool.memset(w_uk, 0.0).then_inc(sem("cleared"), 1)
        pool.memset(ones, 1.0).then_inc(sem("cleared"), 1)
        pool.memset(eps_col, EPS).then_inc(sem("cleared"), 1)
        pool.dma_start(const[:, P:C_MAIN], io["const"][:, P:C_MAIN]).then_inc(sem("const_landed"), 16)
        pool.wait_ge(sem("cleared"), 2)
        for half in (0, HD):
            pool.dma_start(w_uk[:, half + ROPE:half + HD], io["dsa_w_uk"][0]).then_inc(sem("small_landed"), 16)
        pool.dma_start(w_uv, io["dsa_w_uv"][0]).then_inc(sem("small_landed"), 16)
        for k, name in enumerate(("nsa_cmp_k_w2", "nsa_cmp_k_w2", "nsa_cmp_v_w2")):
            pool.dma_start(cmp_w2[:, k * HD:(k + 1) * HD], io[name][0]).then_inc(sem("small_landed"), 16)
        pool.dma_start(rel_bias[0:BUCKETS, :], io["rel_bias_2"]).then_inc(sem("small_landed"), 16)
        pool.dma_start(sinks, bass.AP(io["sinks_2"].tensor, 0, [[0, P], [1, N_BAND]])).then_inc(sem("small_landed"), 16)
        pool.memset(cmp_k, 0.0).then_inc(sem("cmp_k_cleared"), 1)
        pool.wait_ge(sem("cmp_k_cleared"), 1)
        for k, tiles in enumerate((keys, k_mem[1])):
            clear_keys(tiles, k)
        pool.wait_ge(sem("keys_cleared"), 4)
        add_squares("mem")
        pool.wait_ge(sem("h_ready"), 4 * (prod["mem1"] + 1))
        for m, name in enumerate(("nsa_cmp_k_w1", "nsa_cmp_v_w1")):
            pool.dma_start(cmp_w1[:, m], io[name][0].rearrange("(l p) h -> p l h", p=P)).then_inc(sem("cmp_w1_landed"), 16)
        for name in ("attn0", "ffn0", "attn1"):
            add_squares(name)
        pool.wait_ge(sem("h_ready"), 4 * (prod["o1"] + 1))
        pool.dma_start(t5_const, io["const"][:, C_MAIN:C_MAIN + C_T5]).then_inc(sem("t5_landed"), 16)
        pool.memset(glu_pad[:, :, 0:PAD], 0.0).then_inc(sem("pad_cleared"), 1)
        for name in ("ffn1", "final1", "mix0"):
            add_squares(name)
        pool.wait_ge(sem("t5_row_ready"), 1)
        row = tok_flat[0:N_BAND, C_T5:C_T5 + 383]
        pool.dma_start(t5_row.rearrange("q h m -> h q m"),
                       bass.AP(row.tensor, row.offset, [row.ap[0], [0, P], row.ap[1]])).then_inc(sem("t5_stored"), 16)
        acc = probs_t[0]
        for c in POOL_CHUNKS:
            for j in range(PAIRS):
                n = PAIRS * POOL_CHUNKS.index(c) + j
                w = S * min(2, CONV - 2 * j)
                pool.wait_ge(sem("pair_ready"), n + 1)
                if n:
                    pool.wait_ge(sem("pair_added"), n)
                if j == 0:
                    if c != POOL_CHUNKS[0]:
                        pool.wait_ge(sem("pool_chunk_done"), POOL_CHUNKS.index(c))
                    pool.tensor_copy(acc, pair_of(n)).then_inc(sem("pair_added"), 1)
                else:
                    pool.tensor_tensor(acc[:, 0:w], acc[:, 0:w], pair_of(n)[:, 0:w], ALU.add).then_inc(sem("pair_added"), 1)
            pool.wait_ge(sem("pair_added"), PAIRS * (POOL_CHUNKS.index(c) + 1))
            pool.tensor_tensor(conv_y[:, c, :], acc[:, 0:S], acc[:, S:2 * S], ALU.add).then_inc(sem("pool_chunk_done"), 1)
        pool.wait_ge(sem("t5_stored"), 16)
        pool.wait_ge(sem("h_ready"), 4 * (prod["conv"] + 1))
        for h0 in range(0, N_BAND, 4):
            pool.dma_start(t5_bias[:, h0:h0 + 4, :], bass.AP(t5_row.tensor, h0 * 383 + P - 1,
                                                            [[N_BAND * 383 - 1, P], [383, 4], [1, S]])
                           ).then_inc(sem("t5_bias_landed"), 16)
        for name in ("ffn2", "kv", "ffn3", "final2"):
            add_squares(name)

    @block.scalar
    def _(act):
        def convert(g, j=0):
            if g >= NSLOT:
                return
            landed(act, g, j)
            if g >= NS:
                used(act, g - NS, j)
            n = slot_cols(g)
            nc.scalar.activation(w_hi[g % NS][:, 0:n], raw[g % NR][:, 0:n], ACT.Copy).then_inc(sem("w_hi_done"), 1)

        def unit(g):
            convert(g + 2)

        def split_hi(p, src, gain, ready):
            set_free(act, p)
            for c in range(DC):
                if c % 2 == 0:
                    ready(c // 2)
                ins = nc.scalar.activation(h_hi[p % 2][:, c, :], src[:, c, :], ACT.Copy, scale=gain(c))
                if c % 2:
                    ins.then_inc(sem("h_hi_done"), 1)

        def squares(name, src, ready):
            k = sum_no[name]
            if k >= 1:
                act.wait_ge(sem("sum_ready"), k)
            for c2 in range(4):
                ready(c2)
                nc.scalar.activation(halves(qa_flat)[:, 2 * c2:2 * c2 + 2, :], src[:, 2 * c2:2 * c2 + 2, :],
                                     ACT.Square).then_inc(sem("squared"), 1)

        def root(name, scale=1.0 / D):
            k = sum_no[name]
            act.wait_ge(sem("sum_ready"), k + 1)
            if k >= 1:
                act.wait_ge(sem("rstd_ready"), k)
            nc.scalar.activation(rms, bank[0][:, 0:S], ACT.Sqrt, scale=scale,
                                 bias=eps_col[:, 0:1]).then_inc(sem("root_done"), 1)

        def norm(name, u, gain):
            split_hi(prod[name], x, gain, lambda c2: x_updated(act, u, c2))
            squares(name, x, lambda c2: x_updated(act, u, c2))
            root(name)

        def softmax(*runs):
            def exponentials(n, run, extent):
                in_psum = extent is FULL
                act.wait_ge(sem("max_ready"), n + 1)
                if n >= 2:
                    act.wait_ge(sem("probs_turned"), n - 1)
                for b in range(TB):
                    lo, hi = extent[b]
                    src = bank[n % 2] if in_psum else scores[n % 2]
                    col = slice(2 * n + b, 2 * n + b + 1)
                    ins = nc.scalar.activation(probs[n % 2][:, lo:hi], src[:, lo:hi], ACT.Exp,
                                               bias=shift[:, col], scale=SCALE if in_psum else -1.0,
                                               accum_out=row_sum[:, col])
                ins.then_inc(sem("exp_done"), 1)
                if run == "band":
                    h = n - RUNS[run][0]
                    nc.scalar.activation(sink_exp[:, 2 * h:2 * h + 2], shift[:, 2 * n:2 * n + 2], ACT.Exp,
                                         bias=sinks[:, h:h + 1]).then_inc(sem("sink_done"), 1)

            def copy_t(n, extent):
                width = extent[1][1]
                act.wait_ge(sem("probs_turned"), n + 1)
                if n >= 2:
                    act.wait_ge(sem("pv_done"), n - 1)
                nc.scalar.activation(probs_t[n % 2][:, 0:width], bank[2 + n % 2][:, 0:width],
                                     ACT.Copy).then_inc(sem("probs_t_ready"), 1)

            heads = [(RUNS[run][0] + i, run, RUNS[run][2]) for run in runs for i in range(RUNS[run][1])]
            for i, (n, run, extent) in enumerate(heads):
                exponentials(n, run, extent)
                if i:
                    copy_t(n - 1, heads[i - 1][2])
            copy_t(heads[-1][0], heads[-1][2])

        def turned_o(name):
            p, k = prod[name], TURNED[name]
            set_free(act, p)
            for c2 in range(4):
                act.wait_ge(sem("o_turned"), 4 * k + c2 + 1)
                nc.scalar.activation(h_hi[p % 2][:, 2 * c2:2 * c2 + 2, :], halves(bank[c2]),
                                     ACT.Copy).then_inc(sem("h_hi_done"), 1)

        def ffn(f):
            first = FF[f][0]

            def gate(s, g, j=0):
                evicted(act, g, j)
                nc.scalar.activation(scores[1], scores[0], ACT.Silu).then_inc(sem("silu_done"), 1)

            def hidden(s, g, j=0):
                evicted(act, g, j)
                nc.scalar.activation(ff_hi[s % 2], probs[0], ACT.Copy).then_inc(sem("ff_hi_done"), 1)

            def step(s, j=0):
                g = first + 3 * s - 1
                convert(g + 2, j)
                gate(s, g, j)
                convert(g + 3, j)
                convert(g + 4, j)
                hidden(s, g + 1, j)

            convert(first + 2)
            gate(0, first)
            convert(first + 3)
            hidden(0, first + 1)
            step(1)
            with act.Fori(0, (FF_STEPS - 3) // 2) as j:
                step(2, j)
                step(3, j)
            step(FF_STEPS - 1)
            convert(first + 3 * FF_STEPS - 1 + 2)

        act.dma_start(ident, io["const"][:, 0:P]).then_inc(sem("ident_landed"), 16)
        act.wait_ge(sem("cleared"), 1)
        for r, m, src in pieces:
            act.dma_start(vec_tok[r % P:r % P + m, r // P, :], src).then_inc(sem("vec_landed"), 16)
        act.dma_start(tok, io["x"][0].rearrange("(b p) n -> p b n", p=P)).then_inc(sem("x_landed"), 16)
        convert(0)
        convert(1)
        squares("mem", mem_t, lambda c2: act.wait_ge(sem("mem_turned"), c2 + 1))
        act.wait_ge(sem("vec_ready"), 1)
        act.wait_ge(sem("cleared"), 4)
        for layer in range(2):
            split_hi(prod[f"mem{layer}"], mem_t, lambda c: vec("mem_norm", DC * layer + c), lambda c2: None)
        root("mem")
        for g in range(4):
            unit(g)
        norm("attn0", "load", lambda c: vec("attn_norm", c))

        for g in range(G_DSA, G_DSA + 3):
            unit(g)
        for h in range(N_IDX):
            act.wait_ge(sem("idx_scored"), h + 1)
            if h >= 2:
                act.wait_ge(sem("idx_weighed"), h - 1)
            nc.scalar.activation(scores[h % 2][:, 0:3 * P], bank[h % 2][:, 0:3 * P],
                                 ACT.Relu).then_inc(sem("idx_relu"), 1)
        for g in range(G_DSA + 3, G_DSA + 7):
            unit(g)
        evicted(act, G_DSA + 6)
        nc.scalar.activation(qa_flat[:, 2 * S:3 * S], qa_flat[:, 0:S], ACT.Square).then_inc(sem("ckv_squared"), 1)
        root("ckv", 1.0 / P)
        unit(G_DSA + 7)
        softmax("dsa", "mem0")
        turned_o("o0")
        for g in range(G_WO0, G_WO0 + 4):
            unit(g)
        norm("ffn0", "wo0", lambda c: vec("ffn_norm", c))
        ffn(0)
        norm("attn1", "ff0", lambda c: vec("attn_norm", DC + c))

        for g in range(G_NSA, G_NSA + 4):
            unit(g)
        evicted(act, G_NSA + 3)
        for m in range(2):
            ft = probs_t[m][:, 0:32 * NCMP].rearrange("p (l g c) -> p l g c", l=16, g=2)
            for par in range(2):
                for grp in range(2):
                    src = stage[0][grp * HD:(grp + 1) * HD, m * S:(m + 1) * S]
                    view = bass.AP(src.tensor, src.offset + par, [src.ap[0], [2, 16], [CMP_STRIDE, NCMP]])
                    nc.scalar.activation(ft[par * HD:(par + 1) * HD, :, grp, :], view,
                                         ACT.Copy).then_inc(sem("ft_copied"), 1)
        unit(G_NSA + 4)
        unit(G_NSA + 5)
        for m in range(2):
            act.wait_ge(sem("cmp_hidden"), m + 1)
            nc.scalar.activation(scores[0][:, 32 * m:32 * m + 2 * NCMP], bank[m][:, 0:2 * NCMP],
                                 ACT.Gelu_apprx_tanh).then_inc(sem("gelu_done"), 1)
        unit(G_NSA + 6)
        evicted(act, G_NSA + 6)
        nc.scalar.activation(probs[1][0:36, 0:S], probs[1][0:36, S:2 * S], ACT.Sigmoid).then_inc(sem("gates_open"), 1)
        unit(G_NSA + 7)
        act.wait_ge(sem("cmp_shifted"), 1)
        nc.scalar.activation(probs[0][:, 0:24 * NCMP], scores[1][:, 0:24 * NCMP], ACT.Exp).then_inc(sem("cmp_exp"), 1)
        softmax("slc", "win", "mem1")
        turned_o("o1")
        for g in range(G_WO1, G_WO1 + 4):
            unit(g)
        norm("ffn1", "wo1", lambda c: vec("ffn_norm", DC + c))
        ffn(1)
        squares("final1", x, lambda c2: x_updated(act, "ff1", c2))
        root("final1")

        norm("mix0", "renorm", lambda c: vec("norm_mix", c))

        def sigmoids(i):
            evicted(act, G_PW1 + 2 * i + 1)
            for t in range(2):
                nc.scalar.activation(scores[1][:, S * t:S * t + S], scores[0][:, S * t:S * t + S], ACT.Sigmoid,
                                     bias=vec("b_pw1", DC + 2 * i + t)).then_inc(sem("glu_sigmoid"), 1)

        def products(c, j0, j1):
            act.wait_ge(sem("glu_ready"), c + 1)
            for j in range(j0, j1):
                n = PAIRS * POOL_CHUNKS.index(c) + j
                if n >= NPAIR:
                    act.wait_ge(sem("pair_added"), n - NPAIR + 1)
                for k in range(2 * j, min(2 * j + 2, CONV)):
                    ins = nc.scalar.activation(pair_of(n)[:, S * (k % 2):S * (k % 2) + S], glu_pad[:, c, k:k + S],
                                               ACT.Copy, scale=vec("w_dw", DC * k + c))
                ins.then_inc(sem("pair_ready"), 1)

        def diagonals(c, k0, k1):
            for k in range(k0, k1):
                n = CONV * PE_CHUNKS.index(c) + k
                if n >= NDIAG:
                    act.wait_ge(sem("diag_used"), n - NDIAG + 1)
                nc.scalar.activation(diag_of(n), ident, ACT.Copy,
                                     scale=vec("w_dw", DC * k + c)).then_inc(sem("diag_ready"), 1)

        unit(G_PW1)
        unit(G_PW1 + 1)
        sigmoids(0)
        unit(G_PW1 + 2)
        products(0, 0, 6)
        unit(G_PW1 + 3)
        products(0, 6, 8)
        sigmoids(1)
        products(0, 8, 11)
        unit(G_PW1 + 4)
        products(0, 11, PAIRS)
        unit(G_PW1 + 5)
        sigmoids(2)
        products(2, 0, 3)
        diagonals(5, 0, NDIAG)
        unit(G_PW1 + 6)
        products(2, 3, 4)
        unit(G_PW1 + 7)
        products(2, 4, 6)
        sigmoids(3)
        for j in range(6, PAIRS):
            products(2, j, j + 1)
            diagonals(5, min(NDIAG + 2 * (j - 6), CONV), min(NDIAG + 2 * (j - 6) + 2, CONV))
        for j in range(PAIRS):
            products(4, j, j + 1)
            diagonals(7, 2 * j, min(2 * j + 2, CONV))
        for c2 in range(4):
            act.wait_ge(sem("centred"), c2 + 1)
            nc.scalar.activation(halves(qa_flat)[:, 2 * c2:2 * c2 + 2, :], conv_y[:, 2 * c2:2 * c2 + 2, :],
                                 ACT.Square).then_inc(sem("ln_squared"), 1)
        root("ln")
        p = prod["conv"]
        set_free(act, p)
        for c2 in range(5):
            for c in range(2 * c2, min(2 * c2 + 2, DC)):
                act.wait_ge(sem("ln_scaled"), c2 + 1)
                nc.scalar.activation(conv_y[:, c, :], conv_y[:, c, :], ACT.Silu, scale=vec("ln_g", c),
                                     bias=vec("ln_b", c)).then_inc(sem("conv_silu"), 1)
            if c2 >= 1:
                act.wait_ge(sem("conv_silu"), 2 * c2)
                nc.scalar.activation(h_hi[p % 2][:, 2 * c2 - 2:2 * c2, :], conv_y[:, 2 * c2 - 2:2 * c2, :],
                                     ACT.Copy).then_inc(sem("h_hi_done"), 1)
        for g in range(G_PW2, G_PW2 + 4):
            unit(g)
        norm("ffn2", "pw2", lambda c: vec("norm_ffn", c))
        ffn(2)

        norm("kv", "ff2", lambda c: vec("norm_kv", c))
        split_hi(prod["mix1"], x, lambda c: vec("norm_mix", DC + c), lambda c2: None)
        for g in range(G_KV, G_KV + 2 + 4):
            unit(g)
        softmax("band")
        turned_o("o2")
        for g in range(G_WO2, G_WO2 + 4):
            unit(g)
        norm("ffn3", "wo2", lambda c: vec("norm_ffn", DC + c))
        ffn(3)
        squares("final2", x, lambda c2: x_updated(act, "ff3", c2))
        root("final2")

    @block.vector
    def _(dve):
        chain = [0]

        def link(ins):
            chain[0] += 1
            ins.then_inc(sem("dve_link"), 1)
            dve.wait_ge(sem("dve_link"), chain[0])

        def convert(g, j=0):
            if g >= NSLOT:
                return
            dve.wait_ge(sem("w_hi_done"), g + 1 + 6 * j)
            n = slot_cols(g)
            nc.vector.tensor_tensor(w_lo[g % NS][:, 0:n], raw[g % NR][:, 0:n], w_hi[g % NS][:, 0:n].bitcast(F32),
                                    ALU.subtract).then_inc(sem("w_lo_done"), 1)

        def take(g, dst, scale=rstd, j=0, rows=P, n=2):
            used(dve, g, j)
            src = proj_bank(g)[0:rows, 0:n * S]
            if n == 2:
                ins = nc.vector.tensor_tensor(halves(dst), halves(src), over_two(scale[0:rows]), ALU.mult)
            else:
                ins = nc.vector.tensor_tensor(dst, src, scale[0:rows], ALU.mult)
            ins.then_inc(sem("proj_evicted"), 1)

        def take_keys(g, upper, lower, scale=rstd):
            used(dve, g)
            nc.vector.tensor_tensor(upper[0:HD], halves(proj_bank(g))[0:HD], over_two(scale[0:HD]), ALU.mult)
            mark("proj_evicted", nc.vector.tensor_tensor(lower[HD:P], halves(proj_bank(g))[HD:P], over_two(scale[HD:P]),
                                                         ALU.mult))

        def split_lo(p, src, gain):
            for c in range(DC):
                if c % 2 == 0:
                    dve.wait_ge(sem("h_hi_done"), 4 * p + c // 2 + 1)
                ins = nc.vector.scalar_tensor_tensor(h_lo[p % 2][:, c, :], src[:, c, :], gain(c),
                                                     h_hi[p % 2][:, c, :].bitcast(F32), ALU.mult, ALU.subtract)
                if c % 2:
                    ins.then_inc(sem("h_ready"), 1)

        def split_lo_pairs(p, src):
            for c2 in range(4):
                dve.wait_ge(sem("h_hi_done"), 4 * p + c2 + 1)
                nc.vector.tensor_tensor(h_lo[p % 2][:, 2 * c2:2 * c2 + 2, :], src(c2),
                                        h_hi[p % 2][:, 2 * c2:2 * c2 + 2, :].bitcast(F32),
                                        ALU.subtract).then_inc(sem("h_ready"), 1)

        def inverse(name, dst=rstd):
            dve.wait_ge(sem("root_done"), sum_no[name] + 1)
            ins = nc.vector.reciprocal(dst, rms)
            ins.then_inc(sem("rstd_ready"), 1)
            dve.wait_ge(sem("rstd_ready"), sum_no[name] + 1)

        def norm(name, gain):
            split_lo(prod[name], x, gain)
            inverse(name)

        def rotate(name, dst, lower=None):
            rows, n = rot_shape(name)
            src, two = rot_src[name], n == 2 * S
            cos, sin = const_of("cos", rows), const_of("sin", rows)
            if two:
                cos, sin, src = over_two(cos), over_two(sin), halves(src)
            shape = halves if two else (lambda ap: ap)
            dve.wait_ge(sem("rotated"), rot_no[name] + 1)
            link(nc.vector.tensor_tensor(shape(rope_t[0:rows, 0:n]), shape(rot_bank(name)[0:rows, 0:n]), sin, ALU.mult))
            link(nc.vector.tensor_tensor(shape(dst) if lower is None else src, src, cos, ALU.mult))
            if lower is None:
                link(nc.vector.tensor_tensor(shape(dst), shape(dst), shape(rope_t[0:rows, 0:n]), ALU.add))
            else:
                nc.vector.tensor_tensor(lower[HD:P], src[HD:P], rope_t[HD:P, 0:n], ALU.add)
                link(nc.vector.tensor_tensor(dst[0:HD], src[0:HD], rope_t[0:HD, 0:n], ALU.add))

        def mark(name, ins):
            ins.then_inc(sem(name), 1)

        def attend(*parts):
            def masked(n, run, mask, init):
                first, _, extent, _ = RUNS[run]
                dve.wait_ge(sem("qk_done"), n + 1)
                pair = shift[:, 2 * n:2 * n + 2]
                if extent is FULL:
                    link(nc.vector.tensor_reduce(pair, halves(bank[n % 2]), AX.X, ALU.max))
                    mark("max_ready", nc.vector.tensor_scalar(pair, pair, -SCALE, None, ALU.mult))
                    return
                if n >= 2:
                    dve.wait_ge(sem("exp_done"), n - 1)
                for b in range(TB):
                    lo, hi = extent[b]
                    ins = nc.vector.tensor_tensor_reduce(
                        scores[n % 2][:, lo:hi], bank[n % 2][:, lo:hi], mask(n - first, b), -SCALE,
                        -NEG if init is None else init(n - first), ALU.add, ALU.min, shift[:, 2 * n + b:2 * n + b + 1])
                mark("max_ready", ins)

            def outputs(grp, run, gate, col0):
                dve.wait_ge(sem("pv_done"), 4 * grp + 4)
                fac = factor[:, 8 * grp:8 * grp + 8]
                den = row_sum[:, 8 * grp:8 * grp + 8]
                h0 = 4 * grp - RUNS[run][0]
                if run == "band":
                    dve.wait_ge(sem("sink_done"), h0 + 4)
                    link(nc.vector.tensor_tensor(fac, den, sink_exp[:, 2 * h0:2 * h0 + 8], ALU.add))
                    den = fac
                link(nc.vector.reciprocal(fac, den))
                if gate is not None:
                    of = gates.rearrange("p (b h k) -> p h b k", b=TB, k=3)[:, h0:h0 + 4, :, gate]
                    link(nc.vector.tensor_tensor(fac.rearrange("p (h b) -> p h b", b=TB),
                                                 fac.rearrange("p (h b) -> p h b", b=TB), of, ALU.mult))
                f = bass.AP(fac.tensor, fac.offset, [fac.ap[0], [1, TB], [TB, 4], [0, HD]])
                o = bank[4 + grp % 2].rearrange("p (b h d) -> p b h d", b=TB, h=4)
                dst = tok[:, :, col0 + HD * h0:col0 + HD * h0 + 4 * HD]
                if gate is None:
                    mark("o_evicted", nc.vector.tensor_tensor(dst.rearrange("p b (h d) -> p b h d", d=HD), o, f, ALU.mult))
                else:
                    part = qa_flat[:, 0:512]
                    link(nc.vector.tensor_tensor(part.rearrange("p (b h d) -> p b h d", b=TB, h=4), o, f, ALU.mult))
                    mark("o_evicted", nc.vector.tensor_tensor(dst, dst, halves(part), ALU.add))
                    dve.wait_ge(sem("o_evicted"), grp + 1)

            todo = [(RUNS[part[0]][0] + i, part) for part in parts for i in range(RUNS[part[0]][1])]
            for i in range(len(todo) + 2):
                if i < len(todo):
                    n, (run, mask, gate, col0, init) = todo[i]
                    masked(n, run, mask, init)
                if i >= 2 and todo[i - 2][0] % 4 == 3:
                    n, (run, mask, gate, col0, init) = todo[i - 2]
                    outputs(n // 4, run, gate, col0)

        def turned_o(name):
            split_lo_pairs(prod[name], lambda c2: halves(bank[c2]))

        def add_slots(g0, bias=None):
            for i in range(4):
                g = g0 + i
                convert(g + 2)
                used(dve, g)
                xs = x[:, 2 * i:2 * i + 2, :]
                if bias is None:
                    mark("proj_evicted", nc.vector.tensor_tensor(xs, halves(proj_bank(g)), xs, ALU.add))
                else:
                    for t in range(2):
                        c = 2 * i + t
                        ins = nc.vector.scalar_tensor_tensor(x[:, c, :], proj_bank(g)[:, S * t:S * t + S], vec(bias, c),
                                                             x[:, c, :], ALU.add, ALU.add)
                    mark("proj_evicted", ins)

        def ffn(f):
            first = FF[f][0]
            n0 = FF_STEPS * f

            def gates_of(g, j=0):
                take(g, scores[0], j=j)

            def hidden(s, g, j=0):
                dve.wait_ge(sem("silu_done"), n0 + s + 1 + 2 * j)
                mark("silu_scaled", nc.vector.tensor_tensor(halves(probs_t[0]), halves(scores[1]), over_two(rstd), ALU.mult))
                used(dve, g, j)
                dve.wait_ge(sem("silu_scaled"), n0 + s + 1 + 2 * j)
                mark("proj_evicted", nc.vector.tensor_tensor(probs[0], proj_bank(g), probs_t[0], ALU.mult))
                dve.wait_ge(sem("ff_hi_done"), n0 + s + 1 + 2 * j)
                mark("ff_ready", nc.vector.tensor_tensor(ff_lo[s % 2], probs[0], ff_hi[s % 2].bitcast(F32), ALU.subtract))

            def step(s, j=0):
                g = first + 3 * s - 1
                convert(g + 2, j)
                gates_of(g, j)
                convert(g + 3, j)
                convert(g + 4, j)
                hidden(s, g + 1, j)

            convert(first + 2)
            gates_of(first)
            convert(first + 3)
            hidden(0, first + 1)
            step(1)
            with dve.Fori(0, (FF_STEPS - 3) // 2) as j:
                step(2, j)
                step(3, j)
            step(FF_STEPS - 1)
            g = first + 3 * FF_STEPS - 1
            convert(g + 2)
            for c2 in range(4):
                dve.wait_ge(sem("down_done"), 4 * f + c2 + 1)
                xs = x[:, 2 * c2:2 * c2 + 2, :]
                mark("x_ready", nc.vector.tensor_tensor(xs, halves(bank[c2]), xs, ALU.add))

        def rescale_x(name, gain, signal):
            inverse(name)
            for c in range(DC):
                ins = nc.vector.scalar_tensor_tensor(x[:, c, :], x[:, c, :], gain(c), rstd, ALU.mult, ALU.mult)
                if c % 2:
                    mark(signal, ins)

        for c2 in range(4):
            dve.wait_ge(sem("mem_t_done"), c2 + 1)
            mark("mem_turned", nc.vector.tensor_copy(mem_t[:, 2 * c2:2 * c2 + 2, :], halves(bank[4 + c2])))
        dve.wait_ge(sem("vec_turned"), 1)
        mark("vec_ready", nc.vector.tensor_copy(vec_t, bank[1]))
        convert(0)
        convert(1)
        dve.wait_ge(sem("mem_turned"), 4)
        dve.wait_ge(sem("vec_ready"), 1)
        for layer in range(2):
            split_lo(prod[f"mem{layer}"], mem_t, lambda c: vec("mem_norm", DC * layer + c))
        inverse("mem", rstd_mem)
        for c2 in range(4):
            dve.wait_ge(sem("x_t_done"), c2 + 1)
            mark("x_ready", nc.vector.tensor_copy(x[:, 2 * c2:2 * c2 + 2, :], halves(bank[c2])))
        for layer in range(2):
            g = G_MEM[layer]
            convert(g + 2)
            take_keys(g, k_mem[layer][:, 0::2], k_mem[layer][:, 1::2], rstd_mem)
            convert(g + 3)
            take(g + 1, probs[layer], rstd_mem)
            dve.wait_ge(sem("v_turned"), layer + 1)
            mark("v_mem_ready", nc.vector.tensor_copy(v_mem[:, layer].rearrange("p b n -> p (b n)"), bank[1 + layer]))
        dve.wait_ge(sem("x_ready"), 4)
        norm("attn0", lambda c: vec("attn_norm", c))

        g = G_DSA
        convert(g + 2)
        take(g, stage[2][0:72, 0:S], rows=72, n=1)
        convert(g + 3)
        take(g + 1, stage[0])
        rotate("k_idx", keys[0:HD, 2, :])
        nc.vector.tensor_copy(keys[HD:P, 3, :], keys[0:HD, 2, :])
        dve.wait_ge(sem("w_idx_turned"), 1)
        link(nc.vector.tensor_scalar(w_idx, bank[1][:, 0:TB * N_IDX], N_IDX ** -0.5 * HD ** -0.5, None, ALU.mult))
        convert(g + 4)
        take(g + 2, stage[1])
        rotate("q_idx0", qa_flat[:, 1024:1536])
        dve.wait_ge(sem("rotated"), rot_no["q_idx1"] + 1)
        rotate("q_idx1", qa_flat[:, 1536:2048])
        mark("idx_inputs", nc.vector.tensor_copy(top8[:, 0:1], w_idx[:, 0:1]))
        for h in range(N_IDX):
            dve.wait_ge(sem("idx_relu"), h + 1)
            if h:
                dve.wait_ge(sem("idx_weighed"), h)
            for b, (lo, hi) in enumerate(CAUSAL):
                w = w_idx[:, b * N_IDX + h:b * N_IDX + h + 1]
                r, s_h = ranking[:, lo:hi], scores[h % 2][:, lo:hi]
                if h == 0:
                    ins = nc.vector.tensor_scalar(r, s_h, w, 0.0, ALU.mult, ALU.add)
                else:
                    ins = nc.vector.scalar_tensor_tensor(r, s_h, w, r, ALU.mult, ALU.add)
            mark("idx_weighed", ins)
        dve.wait_ge(sem("idx_weighed"), N_IDX)
        link(nc.vector.scalar_tensor_tensor(ranking, const_of("causal"), LATER, ranking, ALU.mult, ALU.add))

        def take_top(rounds):
            for _ in range(rounds):
                for b, (lo, hi) in enumerate(CAUSAL):
                    chain[0] += 1
                    nc.vector.max(top8[:, 8 * b:8 * b + 8], ranking[:, lo:hi]).then_inc(sem("dve_link"), 1)
                for b, (lo, hi) in enumerate(CAUSAL):
                    dve.wait_ge(sem("dve_link"), chain[0] - (1 - b) if b == 0 else chain[0] - 1)
                    chain[0] += 1
                    nc.vector.match_replace(ranking[:, lo:hi], top8[:, 8 * b:8 * b + 8], ranking[:, lo:hi],
                                            TAKEN).then_inc(sem("dve_link"), 1)
                dve.wait_ge(sem("dve_link"), chain[0])

        for i in range(3):
            g = G_DSA + 3 + i
            convert(g + 2)
            take(g, stage[i % 2])
            take_top(2)
            if i:
                rotate(f"q{i - 1}", qb_flat[:, 512 * (i - 1):512 * i])
        g = G_DSA + 6
        convert(g + 2)
        used(dve, g)
        link(nc.vector.tensor_tensor(qa_flat[0:ROPE, S:2 * S], proj_bank(g)[0:ROPE, S:2 * S], rstd[0:ROPE], ALU.mult))
        mark("proj_evicted", nc.vector.tensor_tensor(qa_flat[:, 0:S], proj_bank(g)[:, 0:S], rstd, ALU.mult))
        rotate("q2", qb_flat[:, 1024:1536])
        take_top(TOPK // 8 - 6)
        link(nc.vector.tensor_scalar(dsa_mask, ranking, TAKEN, NEG, ALU.not_equal, ALU.mult))
        link(nc.vector.tensor_tensor(dsa_mask, dsa_mask, const_of("causal"), ALU.add))
        inverse("ckv", rstd_mem)
        mark("ckv_normed", nc.vector.scalar_tensor_tensor(qa_flat[:, 3 * S:4 * S], qa_flat[:, 0:S], vec("ckv_norm", 0),
                                                          rstd_mem, ALU.mult, ALU.mult))
        g = G_DSA + 7
        convert(g + 2)
        take(g, q_mem.rearrange("p c t -> p (c t)"))
        dve.wait_ge(sem("k_nope_done"), 1)
        mark("k_nope_copied", nc.vector.tensor_copy(keys[0:HD, 0, :], bank[1][0:HD, 0:S]))
        mark("k_nope_copied", nc.vector.tensor_copy(keys[HD:P, 1, :], bank[1][HD:P, 0:S]))
        dve.wait_ge(sem("k_nope_copied"), 2)
        rotate("k_rope", keys[0:ROPE, 0, :])
        nc.vector.tensor_copy(keys[HD:HD + ROPE, 1, :], keys[0:ROPE, 0, :])
        dve.wait_ge(sem("dsa_v_done"), 1)
        mark("dsa_kv_ready", nc.vector.tensor_copy(va[:, 0:2 * HD], bank[1][:, 0:2 * HD]))
        attend(("dsa", lambda h, b: dsa_mask[:, CAUSAL[b][0]:CAUSAL[b][1]], None, 0, None),
               ("mem0", None, None, N_TOK * HD, None))
        turned_o("o0")
        add_slots(G_WO0)
        dve.wait_ge(sem("proj_evicted"), proj_index[G_WO0 + 3] + 1)
        norm("ffn0", lambda c: vec("ffn_norm", c))
        ffn(0)
        dve.wait_ge(sem("x_ready"), 4 * 2)
        norm("attn1", lambda c: vec("attn_norm", DC + c))

        for i in range(3):
            g = G_NSA + i
            convert(g + 2)
            take(g, qa_flat[:, 512 * i:512 * i + 512])
            if i:
                rotate(f"nq{i - 1}", qb_flat[:, 512 * (i - 1):512 * i])
        g = G_NSA + 3
        convert(g + 2)
        take(g, stage[0])
        rotate("nq2", qb_flat[:, 1024:1536])
        for m, name in enumerate(("pos_k", "pos_v")):
            dve.wait_ge(sem("ft_copied"), 4 * m + 4)
            ft = probs_t[m][:, 0:32 * NCMP].rearrange("p (l n) -> p l n", l=16)
            pos = vec_t[:, vec_col[name]:vec_col[name] + 16]
            mark("ft_ready", nc.vector.tensor_tensor(ft, ft, bass.AP(pos.tensor, pos.offset, [pos.ap[0], [1, 16], [0, 2 * NCMP]]),
                                                     ALU.add))
        g = G_NSA + 4
        convert(g + 2)
        take(g, stage[1])
        g = G_NSA + 5
        convert(g + 2)
        take(g, stage[2])
        dve.wait_ge(sem("gelu_done"), 2)
        hv = scores[0][:, 32:32 + 2 * NCMP]
        mark("hv_spread", nc.vector.tensor_copy(
            scores[1][:, 0:2 * HPG * NCMP].rearrange("p (g h c) -> p g h c", g=2, h=HPG),
            bass.AP(hv.tensor, hv.offset, [hv.ap[0], [NCMP, 2], [0, HPG], [1, NCMP]])))
        dve.wait_ge(sem("cmp_out"), 1)
        dve.wait_ge(sem("cmp_k_cleared"), 1)
        nc.vector.tensor_copy(cmp_k[0:HD, 0, :], bank[0][0:HD, 0:2 * NCMP])
        link(nc.vector.tensor_copy(cmp_k[HD:P, 1, :], bank[0][HD:P, 0:2 * NCMP]))
        rows = HPG * NCMP
        own = const_of("own_head", rows)
        for grp in range(2):
            v = bank[1][0:rows, HD * grp:HD * grp + HD]
            ins = nc.vector.tensor_tensor(
                cmp_v[0:rows, grp, :].rearrange("p (h d) -> p h d", h=HPG),
                bass.AP(v.tensor, v.offset, [v.ap[0], [0, HPG], [1, HD]]),
                bass.AP(own.tensor, own.offset, [own.ap[0], [1, HPG], [0, HD]]), ALU.mult)
        mark("cmp_kv_ready", ins)

        def both_ways(name, c):
            rotate(name, keys[:, c, :], lower=keys[:, c + 3, :])
            nc.vector.tensor_copy(keys[0:HD, c + 2, :], keys[HD:P, c + 3, :])
            link(nc.vector.tensor_copy(keys[HD:P, c + 1, :], keys[0:HD, c, :]))

        both_ways("ks", 0)
        g = G_NSA + 6
        convert(g + 2)
        take(g, probs[1][0:36, S:2 * S], rows=36, n=1)
        both_ways("kw", 4)
        dve.wait_ge(sem("v_turned"), 3)
        link(nc.vector.tensor_copy(va, bank[1]))
        g = G_NSA + 7
        convert(g + 2)
        take(g, q_mem.rearrange("p c t -> p (c t)"))
        dve.wait_ge(sem("gates_turned"), 1)
        mark("nsa_ready", nc.vector.tensor_copy(gates, bank[2][:, 0:TB * 36]))
        dve.wait_ge(sem("nsa_ready"), 1)
        nb = TB * N_TOK
        dve.wait_ge(sem("cmp_scored"), 1)
        sc3 = scores[1][:, 0:nb * NCMP].rearrange("p (n c) -> p n c", c=NCMP)
        cm = const_of("cmp_mask")
        for b in range(TB):
            ins = nc.vector.tensor_tensor(
                sc3[:, b * N_TOK:(b + 1) * N_TOK, :],
                bank[b][:, 0:N_TOK * NCMP].rearrange("p (n c) -> p n c", c=NCMP),
                bass.AP(cm.tensor, cm.offset + b * NCMP, [cm.ap[0], [0, N_TOK], [1, NCMP]]), ALU.add)
        link(ins)
        mx = factor[:, 128:128 + nb]
        den = factor[:, 160:160 + nb]
        fac = factor[:, 192:192 + nb]
        link(nc.vector.tensor_reduce(mx, sc3, AX.X, ALU.max))
        link(nc.vector.tensor_scalar(mx, mx, NEG / 10, None, ALU.max))

        def per_row(ap, n):
            return bass.AP(ap.tensor, ap.offset, [ap.ap[0], [1, nb], [0, n]])

        link(nc.vector.tensor_tensor(sc3, sc3, per_row(mx, NCMP), ALU.subtract))
        mark("cmp_shifted", nc.vector.tensor_scalar(scores[1][:, 0:nb * NCMP], scores[1][:, 0:nb * NCMP], SCALE, None, ALU.mult))
        dve.wait_ge(sem("cmp_exp"), 1)
        link(nc.vector.tensor_reduce(den, probs[0][:, 0:nb * NCMP].rearrange("p (n c) -> p n c", c=NCMP), AX.X, ALU.add))
        link(nc.vector.tensor_scalar(den, den, 1e-30, None, ALU.max))
        link(nc.vector.reciprocal(fac, den))
        link(nc.vector.tensor_tensor(fac, fac, gates.rearrange("p (n k) -> p n k", k=3)[:, :, 0], ALU.mult))
        dve.wait_ge(sem("cmp_turned"), 1)
        mark("cmp_t_ready", nc.vector.tensor_copy(probs_t[0][0:rows, :], bank[2][0:rows, :]))
        for b in range(TB):
            for grp in range(2):
                dve.wait_ge(sem("cmp_pv"), 2 * b + grp + 1)
                f = fac[:, b * N_TOK + grp * HPG:b * N_TOK + (grp + 1) * HPG]
                w = HPG * HD
                link(nc.vector.tensor_tensor(
                    tok[:, b, grp * w:(grp + 1) * w].rearrange("p (h d) -> p h d", d=HD),
                    bank[4 + 2 * b + grp][:, 0:w].rearrange("p (h d) -> p h d", d=HD),
                    bass.AP(f.tensor, f.offset, [f.ap[0], [1, HPG], [0, HD]]), ALU.mult))
        mark("cmp_evicted", nc.vector.tensor_copy(top8[:, 1:2], fac[:, 0:1]))
        causal = lambda h, b: const_of("causal")[:, CAUSAL[b][0]:CAUSAL[b][1]]
        attend(("slc", causal, 1, 0, None), ("win", causal, 2, 0, None), ("mem1", None, None, N_TOK * HD, None))
        turned_o("o1")
        add_slots(G_WO1)
        dve.wait_ge(sem("proj_evicted"), proj_index[G_WO1 + 3] + 1)
        norm("ffn1", lambda c: vec("ffn_norm", DC + c))
        ffn(1)
        dve.wait_ge(sem("x_ready"), 4 * 3)
        rescale_x("final1", lambda c: vec("final_norm", c), "x_ready")

        dve.wait_ge(sem("x_ready"), 4 * 4)
        norm("mix0", lambda c: vec("norm_mix", c))
        dve.wait_ge(sem("t5_rows_done"), 1)
        link(nc.vector.tensor_tensor(tok_flat[0:N_BAND, C_T5:C_T5 + 383], bank[2][0:N_BAND, 0:383],
                                     tok_flat[0:N_BAND, 383:766], ALU.add))
        mark("t5_row_ready", nc.vector.tensor_scalar(tok_flat[0:N_BAND, C_T5:C_T5 + 383], tok_flat[0:N_BAND, C_T5:C_T5 + 383],
                                                     1.0 / SCALE, None, ALU.mult))
        dve.wait_ge(sem("pad_cleared"), 1)

        def pw1_slot(g, dst):
            convert(g + 2)
            if g > G_PW1 + 1:
                dve.wait_ge(sem("glu_ready"), (g - G_PW1) // 2 * 2)
            take(g, dst)

        def glu(i):
            for t in range(2):
                dve.wait_ge(sem("glu_sigmoid"), 2 * i + t + 1)
                if t == 0:
                    evicted(dve, G_PW1 + 2 * i)
                c = 2 * i + t
                mark("glu_ready", nc.vector.scalar_tensor_tensor(
                    glu_pad[:, c, PAD:APAD], probs[0][:, S * t:S * t + S], vec("b_pw1", c),
                    scores[1][:, S * t:S * t + S], ALU.add, ALU.mult))

        def taps(c, k0, k1):
            if k0 == 0:
                dve.wait_ge(sem("glu_ready"), c + 1)
            for k in range(k0, k1):
                src, w = glu_pad[:, c, k:k + S], vec("w_dw", DC * k + c)
                if k == 0:
                    ins = nc.vector.tensor_scalar(conv_y[:, c, :], src, w, vec("b_dw", c), ALU.mult, ALU.add)
                else:
                    dve.wait_ge(sem(f"tap_done{c}"), k)
                    ins = nc.vector.scalar_tensor_tensor(conv_y[:, c, :], src, w, conv_y[:, c, :], ALU.mult, ALU.add)
                mark(f"tap_done{c}", ins)

        pw1_slot(G_PW1, probs[0])
        pw1_slot(G_PW1 + 1, scores[0])
        glu(0)
        pw1_slot(G_PW1 + 2, probs[0])
        taps(1, 0, 6)
        pw1_slot(G_PW1 + 3, scores[0])
        taps(1, 6, 8)
        glu(1)
        pw1_slot(G_PW1 + 4, probs[0])
        taps(1, 8, 14)
        pw1_slot(G_PW1 + 5, scores[0])
        taps(1, 14, 16)
        glu(2)
        pw1_slot(G_PW1 + 6, probs[0])
        taps(1, 16, 22)
        pw1_slot(G_PW1 + 7, scores[0])
        taps(1, 22, 24)
        glu(3)
        taps(1, 24, CONV)
        for k in range(CONV):
            for c in DVE_CHUNKS[1:]:
                taps(c, k, k + 1)
        for i, c in enumerate(POOL_CHUNKS):
            dve.wait_ge(sem("pool_chunk_done"), i + 1)
            mark("others_biased", nc.vector.tensor_scalar(conv_y[:, c, :], conv_y[:, c, :], vec("b_dw", c), None, ALU.add))
        for i, c in enumerate(PE_CHUNKS):
            dve.wait_ge(sem("diag_used"), CONV * (i + 1))
            mark("others_biased", nc.vector.tensor_scalar(conv_y[:, c, :], bank[2 + i][:, 0:S], vec("b_dw", c), None, ALU.add))
        dve.wait_ge(sem("ln_summed"), 1)
        mean = probs_t[0][:, 0:S]
        mark("mean_taken", nc.vector.tensor_scalar(mean, bank[0][:, 0:S], 1.0 / D, None, ALU.mult))
        dve.wait_ge(sem("mean_taken"), 1)
        for c2 in range(4):
            ys = conv_y[:, 2 * c2:2 * c2 + 2, :]
            mark("centred", nc.vector.tensor_tensor(ys, ys, over_two(mean), ALU.subtract))
        inverse("ln")
        for c2 in range(4):
            ys = conv_y[:, 2 * c2:2 * c2 + 2, :]
            mark("ln_scaled", nc.vector.tensor_tensor(ys, ys, over_two(rstd), ALU.mult))
        split_lo_pairs(prod["conv"], lambda c2: conv_y[:, 2 * c2:2 * c2 + 2, :])
        add_slots(G_PW2, "b_pw2")
        dve.wait_ge(sem("proj_evicted"), proj_index[G_PW2 + 3] + 1)
        norm("ffn2", lambda c: vec("norm_ffn", c))
        ffn(2)

        dve.wait_ge(sem("x_ready"), 4 * 5)
        norm("kv", lambda c: vec("norm_kv", c))
        split_lo(prod["mix1"], x, lambda c: vec("norm_mix", DC + c))
        g = G_KV
        convert(g + 2)
        take_keys(g, keys[:, 0::4], keys[:, 3::4])
        evicted(dve, g)
        nc.vector.tensor_copy(keys[0:HD, 2::4, :], keys[HD:P, 3::4, :])
        link(nc.vector.tensor_copy(keys[HD:P, 1::4, :], keys[0:HD, 0::4, :]))
        convert(g + 3)
        take(g + 1, probs[0])
        for i in range(4):
            g = G_Q + i
            convert(g + 2)
            take(g, qa_flat[:, 512 * i:512 * i + 512])
            if i == 0:
                dve.wait_ge(sem("v_turned"), 4)
                mark("band_v_ready", nc.vector.tensor_copy(va, bank[1]))
        dve.wait_ge(sem("small_landed"), SMALL_ALL)
        link(nc.vector.tensor_scalar(neg_sinks, sinks, -1.0, None, ALU.mult))
        dve.wait_ge(sem("t5_bias_landed"), 64)
        attend(("band", lambda h, b: t5_bias[:, h, P:S] if b == 0 else t5_bias[:, h, :], None, 0,
                lambda h: neg_sinks[:, h:h + 1]))
        turned_o("o2")
        add_slots(G_WO2)
        dve.wait_ge(sem("proj_evicted"), proj_index[G_WO2 + 3] + 1)
        norm("ffn3", lambda c: vec("norm_ffn", DC + c))
        ffn(3)
        dve.wait_ge(sem("x_ready"), 4 * 6)
        rescale_x("final2", lambda c: vec("norm_final", c), "y_ready")
        for i in range(4):
            dve.wait_ge(sem("y_turned"), i + 1)
            mark("result_ready", nc.vector.tensor_copy(tok[:, i // 2, 512 * (i % 2):512 * (i % 2) + 512], bank[4 + i]))

    @block.tensor
    def _(pe):
        mm = nc.tensor.matmul
        turn = nc.tensor.transpose

        def mark(name, ins):
            ins.then_inc(sem(name), 1)

        def three(out_ap, hi, lo, act_hi, act_lo, start, stop, skip=False):
            mm(out_ap, hi, act_hi, start=start, stop=False, skip_group_check=skip)
            mm(out_ap, hi, act_lo, start=False, stop=False, skip_group_check=skip)
            return mm(out_ap, lo, act_hi, start=False, stop=stop, skip_group_check=skip)

        def project(g, p, fresh=False, j=0):
            w = slots[g][2]
            hi = w_hi[g % NS][:, 0:DC * w].rearrange("p (c n) -> p c n", c=DC)
            lo = w_lo[g % NS][:, 0:DC * w].rearrange("p (c n) -> p c n", c=DC)
            pe.wait_ge(sem("w_lo_done"), g + 1 + 6 * j)
            if proj_index[g] >= 4:
                pe.wait_ge(sem("proj_evicted"), proj_index[g] - 3 + 4 * j)
            for t, n0 in enumerate(range(0, w, P)):
                m = min(P, w - n0)
                for c in range(DC):
                    if fresh and t == 0 and c % 2 == 0:
                        pe.wait_ge(sem("h_ready"), 4 * p + c // 2 + 1)
                    ins = three(proj_bank(g)[0:m, S * t:S * t + S], hi[:, c, n0:n0 + m], lo[:, c, n0:n0 + m],
                                h_hi[p % 2][:, c, :], h_lo[p % 2][:, c, :], c == 0, c == DC - 1)
            mark("slot_used", ins)

        def total(name, src=None):
            if src is None:
                pe.wait_ge(sem("added"), added_no[name] + 1)
                src = qa_flat[:, 0:S]
            mark("sum_ready", mm(bank[0][:, 0:S], ones, src, start=True, stop=True))

        def rotate(name):
            rows, n = rot_shape(name)
            mark("rotated", mm(rot_bank(name)[0:rows, 0:n], const_of("rot", rows)[:, 0:rows], rot_src[name],
                               start=True, stop=True))

        def turn_v(src, dst):
            for t in range(2):
                for b in range(TB):
                    ins = turn(dst[:, S * b + P * t:S * b + P * t + P], src[:, S * t + P * b:S * t + P * b + P], ident)
            mark("v_turned", ins)

        def attend(*parts):
            def qk(n, run, q, k, v, ready):
                first, _, extent, _ = RUNS[run]
                if n == first:
                    ready()
                for b in range(TB):
                    lo, hi = extent[b]
                    ins = mm(bank[n % 2][:, lo:hi], q(n - first)[:, P * b:P * b + P], k(n - first)[:, 0:hi - lo],
                             start=True, stop=True)
                mark("qk_done", ins)

            def turn_probs(n, run, *_):
                pe.wait_ge(sem("exp_done"), n + 1)
                if n >= 2:
                    pe.wait_ge(sem("probs_t_ready"), n - 1)
                for i in range(len(RUNS[run][3])):
                    ins = turn(bank[2 + n % 2][:, P * i:P * i + P], probs[n % 2][:, P * i:P * i + P], ident)
                mark("probs_turned", ins)

            def pv(n, run, q, k, v, ready):
                first, _, _, blocks = RUNS[run]
                pe.wait_ge(sem("probs_t_ready"), n + 1)
                if n % 4 == 0 and n >= 8:
                    pe.wait_ge(sem("o_evicted"), n // 4 - 1)
                for b in range(TB):
                    mine = [i for i, (qb_, _) in enumerate(blocks) if qb_ == b]
                    for i in mine:
                        ins = mm(bank[4 + n // 4 % 2][:, S * b + HD * (n % 4):S * b + HD * (n % 4) + HD],
                                 probs_t[n % 2][:, P * i:P * i + P], v(n - first, blocks[i][1]),
                                 start=i == mine[0], stop=i == mine[-1])
                mark("pv_done", ins)

            heads = [(RUNS[part[0]][0] + i,) + part for part in parts for i in range(RUNS[part[0]][1])]
            qk(*heads[0])
            qk(*heads[1])
            for i in range(len(heads)):
                turn_probs(*heads[i])
                if i + 2 < len(heads):
                    qk(*heads[i + 2])
                if i >= 1:
                    pv(*heads[i - 1])
            pv(*heads[-1])

        def turn_o(name):
            pe.wait_ge(sem("o_evicted"), {"o0": 4, "o1": 11, "o2": 15}[name])
            for c2 in range(4):
                for c in (2 * c2, 2 * c2 + 1):
                    for b in range(TB):
                        at = S * (c % 2) + P * b
                        ins = turn(bank[c2][:, at:at + P], tok[:, b, P * c:P * c + P], ident)
                mark("o_turned", ins)

        def turn_tokens(src, banks, name):
            for c2 in range(4):
                for c in (2 * c2, 2 * c2 + 1):
                    for b in range(TB):
                        at = S * (c % 2) + P * b
                        ins = turn(banks[c2][:, at:at + P], src[:, b, P * c:P * c + P], ident)
                mark(name, ins)

        def ffn(f, p):
            first = FF[f][0]
            n0 = FF_STEPS * f

            def down(s, g, j=0, start=False, stop=False):
                pe.wait_ge(sem("w_lo_done"), g + 1 + 6 * j)
                pe.wait_ge(sem("ff_ready"), n0 + s + 1 + 2 * j)
                hi = w_hi[g % NS].rearrange("p (c n) -> p c n", c=2)
                lo = w_lo[g % NS].rearrange("p (c n) -> p c n", c=2)
                for m in range(DC):
                    for c in range(2):
                        ins = three(bank[m // 2][:, S * (m % 2):S * (m % 2) + S], hi[:, c, P * m:P * m + P],
                                    lo[:, c, P * m:P * m + P], ff_hi[s % 2][:, S * c:S * c + S],
                                    ff_lo[s % 2][:, S * c:S * c + S], start and c == 0 and m % 2 == 0,
                                    stop and c == 1 and m % 2 == 1, skip=True)
                    if stop and m % 2 == 1:
                        mark("down_done", ins)
                if not stop:
                    mark("slot_used", ins)

            def step(s, j=0):
                g = first + 3 * s - 1
                project(g, p, j=j)
                project(g + 1, p, j=j)
                down(s - 1, g + 2, j, start=(s == 1))

            project(first, p, fresh=True)
            total(PROD[p])
            project(first + 1, p)
            pe.wait_ge(sem("root_done"), sum_no[PROD[p]] + 1)
            step(1)
            with pe.Fori(0, (FF_STEPS - 3) // 2) as j:
                step(2, j)
                step(3, j)
            step(FF_STEPS - 1)
            down(FF_STEPS - 1, first + 3 * FF_STEPS - 1, stop=True)
            pe.wait_ge(sem("down_done"), 4 * f + 4)
            pe.nop().then_inc(sem("slot_used"), 1)

        pe.wait_ge(sem("ident_landed"), 16)
        pe.wait_ge(sem("mem_landed"), 16 * TB)
        turn_tokens(mem_tok, bank[4:8], "mem_t_done")
        pe.wait_ge(sem("vec_landed"), VEC_ALL)
        for t in range(4):
            ins = turn(bank[1][:, P * t:P * t + P], vec_tok[:, t, :], ident)
        mark("vec_turned", ins)
        pe.wait_ge(sem("cleared"), 4)
        total("mem")
        pe.wait_ge(sem("root_done"), 1)
        pe.wait_ge(sem("vec_ready"), 1)
        pe.wait_ge(sem("x_landed"), 16)
        turn_tokens(tok, bank[0:4], "x_t_done")
        for layer in range(2):
            g = G_MEM[layer]
            p = prod[f"mem{layer}"]
            project(g, p, fresh=True)
            project(g + 1, p)
            pe.wait_ge(sem("x_ready"), 4)
            evicted(pe, g + 1)
            turn_v(probs[layer], bank[1 + layer])
        p = prod["attn0"]
        g = G_DSA
        project(g, p, fresh=True)
        total("attn0")
        project(g + 1, p)
        pe.wait_ge(sem("v_mem_ready"), 2)
        evicted(pe, g)
        pe.wait_ge(sem("const_landed"), 16)
        rotate("k_idx")
        for b in range(TB):
            ins = turn(bank[1][:, N_IDX * b:N_IDX * b + N_IDX], stage[2][HD:HD + N_IDX, P * b:P * b + P],
                       ident[HD:HD + N_IDX, HD:HD + N_IDX])
        mark("w_idx_turned", ins)
        project(g + 2, p)
        evicted(pe, g + 1)
        rotate("q_idx0")
        evicted(pe, g + 2)
        rotate("q_idx1")
        project(g + 3, p)
        pe.wait_ge(sem("idx_inputs"), 1)
        pe.wait_ge(sem("keys_cleared"), 4)
        for h in range(N_IDX):
            if h >= 2:
                pe.wait_ge(sem("idx_relu"), h - 1)
            for b, (lo, hi) in enumerate(CAUSAL):
                ins = mm(bank[h % 2][:, lo:hi], qa[:, 4 + h // 2, P * b:P * b + P], keys[:, 2 + h % 2, 0:hi - lo],
                         start=True, stop=True)
            mark("idx_scored", ins)
        for i in range(3):
            project(g + 4 + i, p)
            evicted(pe, g + 3 + i)
            rotate(f"q{i}")
        pe.wait_ge(sem("ckv_squared"), 1)
        pe.wait_ge(sem("idx_relu"), N_IDX)
        total("ckv", qa_flat[:, 2 * S:3 * S])
        project(g + 7, p)
        pe.wait_ge(sem("ckv_normed"), 1)
        pe.wait_ge(sem("small_landed"), SMALL_ALL)
        ckv = qa_flat[:, 3 * S:4 * S]
        mark("k_nope_done", mm(bank[1][:, 0:S], w_uk, ckv, start=True, stop=True))
        rotate("k_rope")
        pe.wait_ge(sem("k_nope_copied"), 2)
        for b in range(TB):
            ins = mm(bank[1][:, HD * b:HD * b + HD], ckv[:, P * b:P * b + P], w_uv, start=True, stop=True)
        mark("dsa_v_done", ins)

        def dsa_ready():
            pe.wait_ge(sem("dsa_kv_ready"), 1)

        attend(("dsa", lambda h: qb[:, h // 2, :], lambda h: keys[:, h % 2, :],
                lambda h, kb: va[:, HD * kb:HD * kb + HD], dsa_ready),
               ("mem0", lambda h: q_mem[:, h // 2, :], lambda h: k_mem[0][:, h, :],
                lambda h, kb: v_mem[:, 0, kb, HD * h:HD * h + HD], lambda: None))
        turn_o("o0")
        for i in range(4):
            project(G_WO0 + i, prod["o0"], fresh=(i == 0))
        ffn(0, prod["ffn0"])
        p = prod["attn1"]
        g = G_NSA
        project(g, p, fresh=True)
        total("attn1")
        for i in range(3):
            project(g + 1 + i, p)
            evicted(pe, g + i)
            rotate(f"nq{i}")
        project(g + 4, p)
        pe.wait_ge(sem("cmp_w1_landed"), 32)
        for m in range(2):
            pe.wait_ge(sem("ft_ready"), m + 1)
            for l in range(16):
                ins = mm(bank[m][:, 0:2 * NCMP], cmp_w1[:, m, l, :], probs_t[m][:, 2 * NCMP * l:2 * NCMP * (l + 1)],
                         start=(l == 0), stop=(l == 15))
            mark("cmp_hidden", ins)
        project(g + 5, p)
        pe.wait_ge(sem("hv_spread"), 1)
        mm(bank[0][:, 0:2 * NCMP], cmp_w2[:, 0:2 * HD], scores[0][:, 0:2 * NCMP], start=True, stop=True)
        rows = HPG * NCMP
        for grp in range(2):
            ins = mm(bank[1][0:rows, HD * grp:HD * grp + HD], scores[1][:, rows * grp:rows * (grp + 1)],
                     cmp_w2[:, 2 * HD:3 * HD], start=True, stop=True)
        mark("cmp_out", ins)
        rotate("ks")
        project(g + 6, p)
        evicted(pe, g + 5)
        rotate("kw")
        pe.wait_ge(sem("cmp_kv_ready"), 1)
        for k in range(2):
            for b in range(TB):
                ins = turn(bank[1][:, S * k + P * b:S * k + P * b + P], stage[1 + k][:, S + P * b:S + P * b + P], ident)
        mark("v_turned", ins)
        project(g + 7, p)
        pe.wait_ge(sem("gates_open"), 1)
        evicted(pe, g + 7)
        for b in range(TB):
            ins = turn(bank[2][:, 36 * b:36 * b + 36], probs[1][0:36, P * b:P * b + P], ident[0:36, 0:36])
        mark("gates_turned", ins)
        for b in range(TB):
            for h in range(N_TOK):
                ins = mm(bank[b][:, h * NCMP:(h + 1) * NCMP], qa[:, h // 2, P * b:P * b + P],
                         cmp_k[:, h % 2, NCMP * (h // HPG):NCMP * (h // HPG + 1)], start=True, stop=True)
        mark("cmp_scored", ins)
        pe.wait_ge(sem("cmp_exp"), 1)
        pe.wait_ge(sem("nsa_ready"), 1)
        for b in range(TB):
            for grp in range(2):
                i = 2 * b + grp
                ins = turn(bank[2][0:rows, P * i:P * i + P], probs[0][:, rows * i:rows * (i + 1)], ident)
        mark("cmp_turned", ins)
        pe.wait_ge(sem("cmp_t_ready"), 1)
        for i in range(4):
            mark("cmp_pv", mm(bank[4 + i][:, 0:HPG * HD], probs_t[0][0:rows, P * i:P * i + P], cmp_v[0:rows, i % 2, :],
                              start=True, stop=True))

        def nsa_k(first_tile):
            return lambda h: keys[:, first_tile + 2 * (h // HPG) + h % 2, :]

        def nsa_v(k):
            return lambda h, kb: va[:, S * k + P * kb + HD * (h // HPG):S * k + P * kb + HD * (h // HPG) + HD]

        attend(("slc", lambda h: qb[:, h // 2, :], nsa_k(0), nsa_v(0), lambda: pe.wait_ge(sem("cmp_evicted"), 1)),
               ("win", lambda h: qb[:, h // 2, :], nsa_k(4), nsa_v(1), lambda: None),
               ("mem1", lambda h: q_mem[:, h // 2, :], lambda h: k_mem[1][:, h, :],
                lambda h, kb: v_mem[:, 1, kb, HD * h:HD * h + HD], lambda: None))
        turn_o("o1")
        for i in range(4):
            project(G_WO1 + i, prod["o1"], fresh=(i == 0))
        ffn(1, prod["ffn1"])
        total("final1")
        p = prod["mix0"]
        pe.wait_ge(sem("t5_landed"), 16)
        pe.wait_ge(sem("x_ready"), 4 * 3)
        mark("t5_rows_done", mm(bank[2][0:N_BAND, 0:383], rel_bias[0:BUCKETS, :], tok_flat[0:BUCKETS, 0:383],
                                start=True, stop=True))
        project(G_PW1, p, fresh=True)
        total("mix0")
        for g in range(G_PW1 + 1, G_PW1 + 8):
            project(g, p)
        pe.wait_ge(sem("root_done"), sum_no["mix0"] + 1)
        pe.wait_ge(sem("t5_row_ready"), 1)
        for i, c in enumerate(PE_CHUNKS):
            pe.wait_ge(sem("glu_ready"), c + 1)
            for k in range(CONV):
                pe.wait_ge(sem("diag_ready"), CONV * i + k + 1)
                mark("diag_used", mm(bank[2 + i][:, 0:S], diag_of(CONV * i + k), glu_pad[:, c, k:k + S],
                                     start=(k == 0), stop=(k == CONV - 1)))
        for i, c in enumerate(DVE_CHUNKS):
            pe.wait_ge(sem(f"tap_done{c}"), CONV)
            mm(bank[0][:, 0:S], ones, conv_y[:, c, :], start=(i == 0), stop=False)
        for i, c in enumerate(POOL_CHUNKS + PE_CHUNKS):
            pe.wait_ge(sem("others_biased"), i + 1)
            ins = mm(bank[0][:, 0:S], ones, conv_y[:, c, :], start=False,
                     stop=(c == PE_CHUNKS[-1]))
        mark("ln_summed", ins)
        pe.wait_ge(sem("mean_taken"), 1)
        for c in range(DC):
            pe.wait_ge(sem("ln_squared"), c // 2 + 1)
            ins = mm(bank[0][:, 0:S], ones, qa[:, c, :], start=(c == 0), stop=(c == DC - 1))
        mark("sum_ready", ins)
        for i in range(4):
            project(G_PW2 + i, prod["conv"], fresh=(i == 0))
        ffn(2, prod["ffn2"])
        project(G_KV, prod["kv"], fresh=True)
        total("kv")
        project(G_KV + 1, prod["kv"])
        project(G_Q, prod["mix1"], fresh=True)
        evicted(pe, G_KV + 1)
        turn_v(probs[0], bank[1])
        for g in range(G_Q + 1, G_Q + 4):
            project(g, prod["mix1"])

        def band_ready():
            pe.wait_ge(sem("band_v_ready"), 1)
            evicted(pe, G_Q + 3)

        attend(("band", lambda h: qa[:, h // 2, :], lambda h: keys[:, 2 * (h // 4) + h % 2, :],
                lambda h, kb: va[:, S * kb + HD * (h // 4):S * kb + HD * (h // 4) + HD], band_ready))
        turn_o("o2")
        for i in range(4):
            project(G_WO2 + i, prod["o2"], fresh=(i == 0))
        ffn(3, prod["ffn3"])
        total("final2")
        for i in range(4):
            b = i // 2
            for k in range(4):
                c = 4 * (i % 2) + k
                if b == 0 and c % 2 == 0:
                    pe.wait_ge(sem("y_ready"), c // 2 + 1)
                ins = turn(bank[4 + i][:, P * k:P * k + P], x[:, c, P * b:P * b + P], ident)
            mark("y_turned", ins)


_INS = ["x", "mem", "attn_norm", "mem_norm", "ffn_norm", "final_norm", "dsa_w_in", "dsa_ckv_norm", "dsa_w_uk",
        "dsa_w_uv", "nsa_w_in", "nsa_cmp_pos_k", "nsa_cmp_pos_v", "nsa_cmp_k_w1", "nsa_cmp_k_w2",
        "nsa_cmp_v_w1", "nsa_cmp_v_w2", "mem_w_kv", "w_o", "ffn_w_in", "ffn_w_down", "norm_mix_2",
        "norm_ffn_2", "conv_w_pw1_2", "conv_b_pw1_2", "conv_w_dw_2", "conv_b_dw_2", "conv_ln_g_2",
        "conv_ln_b_2", "conv_w_pw2_2", "conv_b_pw2_2", "norm_kv_2", "w_kv_2", "w_q_2", "w_o_2", "sinks_2",
        "rel_bias_2", "ffn_w_up_2", "ffn_w_down_2", "norm_final_2"]


def kernel(**inputs):
    import concourse.bacc as bacc
    from concourse.bass_utils import run_bass_kernel_spmd

    nc = bacc.Bacc("TRN2", target_bir_lowering=False, num_devices=1)
    arrays = {name: np.ascontiguousarray(inputs[name]) for name in _INS}
    arrays["const"] = constants()
    io = {name: nc.dram_tensor(f"in_{name}", a.shape, mybir.dt.from_np(a.dtype), kind="ExternalInput").ap()
          for name, a in arrays.items()}
    out = nc.dram_tensor("result", (1, S, D), F32, kind="ExternalOutput").ap()
    build(nc, io, out)
    r = run_bass_kernel_spmd(nc, [{f"in_{name}": a for name, a in arrays.items()}], core_ids=[0])
    return r.results[0]["result"]
```

```python
from contextlib import ExitStack

import numpy as np

import concourse.bass as bass
from concourse import mybir

F32 = mybir.dt.float32
F32R = mybir.dt.float32r
ALU = mybir.AluOpType
ACT = mybir.ActivationFunctionType
AX = mybir.AxisListType

P = 128
S = 256
D = 1024
DC = D // P
TB = S // P
DFF = 2816
HD = 64
N_TOK, N_MEM_H, N_BAND = 12, 4, 16
N_IDX = 8
TOPK = min(256, S // 4)
ROPE = 16
EPS = 1e-6
SCALE = HD ** -0.5
NEG = -1e30
LATER = 3.0e8
TAKEN = -3.3e38
CMP_LEN, CMP_STRIDE = 32, 16
NCMP = (S - CMP_LEN) // CMP_STRIDE + 1
HPG = 6
BUCKETS = 32
CONV = 31
SLOT = 2048
NR = 3
NS = 3
FF_STEPS = DFF // 256


def rope_constants():
    inv = 500000.0 ** (-np.arange(0, ROPE, 2, dtype=np.float64) / ROPE)
    ang = np.arange(S, dtype=np.float64)[:, None] * inv[None, :]
    cos, sin = np.cos(ang).astype(np.float32).T, np.sin(ang).astype(np.float32).T
    c, s = np.ones((P, S), np.float32), np.zeros((P, S), np.float32)
    rot = np.zeros((P, P), np.float32)
    half = ROPE // 2
    for h in range(0, P, HD):
        c[h:h + half], c[h + half:h + ROPE] = cos, cos
        s[h:h + half], s[h + half:h + ROPE] = sin, sin
        for d in range(half):
            rot[h + half + d, h + d] = -1.0
            rot[h + d, h + half + d] = 1.0
    return c, s, rot


def t5_bucket(dist):
    max_exact = BUCKETS // 2
    d = np.maximum(dist, 0)
    ratio = (np.log(np.maximum(d, 1).astype(np.float32) / np.float32(max_exact)).astype(np.float32)
             / np.float32(np.log(128 / max_exact)))
    large = max_exact + (ratio * np.float32(BUCKETS - max_exact)).astype(np.int32)
    return np.where(d < max_exact, d, np.minimum(large, BUCKETS - 1))


CONST_COLS = {}


def constants():
    c, s, rot = rope_constants()
    q, k = np.arange(P)[:, None], np.arange(S)[None, :]
    causal = np.concatenate([np.where(k[:, :P] <= q, 0, NEG), np.where(k <= q + P, 0, NEG)], 1)
    end = np.arange(NCMP) * CMP_STRIDE + CMP_LEN - 1
    cmp_mask = np.concatenate([np.where(end[None] <= q + P * b, 0, NEG) for b in range(TB)], 1)
    row = np.arange(P)[:, None]
    own_head = row // NCMP == np.arange(HPG)[None]
    dist = 255 - np.arange(383)
    inside = (dist >= 0) & (dist < P)
    onehot = np.zeros((P, 383))
    onehot[:BUCKETS] = (t5_bucket(dist)[None] == np.arange(BUCKETS)[:, None]) & inside[None]
    outside = np.broadcast_to(np.where(inside, 0, NEG)[None], (P, 383))
    parts = [("ident", np.eye(P)), ("rot", rot), ("cos", c), ("sin", s), ("causal", causal),
             ("cmp_mask", cmp_mask), ("own_head", own_head),
             ("onehot", onehot), ("outside", outside)]
    at = 0
    for name, a in parts:
        CONST_COLS[name] = (at, at + a.shape[1])
        at += a.shape[1]
    return np.ascontiguousarray(np.concatenate([a for _, a in parts], 1).astype(np.float32))


constants()
C_MAIN = CONST_COLS["onehot"][0]
C_T5 = CONST_COLS["outside"][1] - C_MAIN


def build(nc, io, out):
    ctx = ExitStack()
    with ctx:
        _build(nc, ctx, io, out)


def _build(nc, ctx, io, out):
    def sb(name, cols, dt=F32):
        return ctx.enter_context(nc.sbuf_tensor(name, [P, cols], dt))[:, :]

    sems = {}

    def sem(name):
        if name not in sems:
            sems[name] = ctx.enter_context(nc.semaphore(name))
        return sems[name]

    raw = [sb(f"raw{i}", SLOT) for i in range(NR)]
    w_hi = [sb(f"w_hi{i}", SLOT, F32R) for i in range(NS)]
    w_lo = [sb(f"w_lo{i}", SLOT, F32R) for i in range(NS)]
    h_hi = [sb(f"h_hi{i}", DC * S, F32R).rearrange("p (c t) -> p c t", t=S) for i in range(2)]
    h_lo = [sb(f"h_lo{i}", DC * S, F32R).rearrange("p (c t) -> p c t", t=S) for i in range(2)]
    ff_hi = [sb(f"ff_hi{i}", 2 * S, F32R) for i in range(2)]
    ff_lo = [sb(f"ff_lo{i}", 2 * S, F32R) for i in range(2)]
    x_flat = sb("x", DC * S)
    x = x_flat.rearrange("p (c t) -> p c t", t=S)
    rstd = sb("rstd", S)
    rstd_mem = sb("rstd_mem", S)
    tok_flat = sb("tok", TB * D)
    tok = tok_flat.rearrange("p (b n) -> p b n", n=D)
    PAD = CONV - 1
    APAD = S + PAD
    big = sb("big", max(DC * APAD + DC * S, 32 * P, N_BAND * S))
    mem_tok = big[:, 0:TB * D].rearrange("p (b n) -> p b n", n=D)
    mem_t = big[:, TB * D:2 * TB * D].rearrange("p (c t) -> p c t", t=S)
    cmp_w1 = big[:, 0:32 * P].rearrange("p (m l h) -> p m l h", m=2, l=16)
    glu_pad = big[:, 0:DC * APAD].rearrange("p (c t) -> p c t", t=APAD)
    conv_y = big[:, DC * APAD:DC * APAD + DC * S].rearrange("p (c t) -> p c t", t=S)
    t5_bias = big[:, 0:N_BAND * S].rearrange("p (h k) -> p h k", k=S)
    qa_flat = sb("qa", 8 * S)
    qa = qa_flat.rearrange("p (c t) -> p c t", t=S)
    qb_flat = sb("qb", 6 * S)
    qb = qb_flat.rearrange("p (c t) -> p c t", t=S)
    va = sb("va", 2 * S)
    q_mem = sb("q_mem", 2 * S).rearrange("p (c t) -> p c t", t=S)
    keys = sb("keys", 8 * S).rearrange("p (c t) -> p c t", t=S)
    k_mem = [keys[:, 4:8], sb("k_mem1", 4 * S).rearrange("p (h t) -> p h t", h=N_MEM_H)]
    v_mem = sb("v_mem", 4 * S).rearrange("p (l b n) -> p l b n", l=2, b=2)
    scores = [sb(f"scores{i}", 2 * S) for i in range(2)]
    probs = [sb(f"probs{i}", 2 * S) for i in range(2)]
    probs_t = [sb(f"probs_t{i}", 2 * S) for i in range(2)]
    rms = probs_t[1][:, 0:S]
    dsa_flat = sb("dsa_flat", 6 * P)
    dsa_mask, ranking = dsa_flat[:, 0:3 * P], dsa_flat[:, 3 * P:6 * P]
    cmp_v = dsa_flat.rearrange("p (g n) -> p g n", g=2)
    cmp_k = sb("cmp_k", 4 * NCMP).rearrange("p (g n) -> p g n", g=2)
    sink_exp = sb("sink_exp", 2 * N_BAND)
    top8 = sb("top8", 16)
    shift = sb("shift", 128)
    row_sum = sb("row_sum", 128)
    factor = sb("factor", 256)
    gates = sb("gates", TB * 36)
    w_idx = sb("w_idx", TB * N_IDX)
    vec_t = sb("vec_t", 4 * P)
    const = sb("const", C_MAIN)
    ones = sb("ones", P)
    w_uk = sb("w_uk", P)
    w_uv = sb("w_uv", HD)
    cmp_w2 = sb("cmp_w2", 3 * HD)
    rel_bias = sb("rel_bias", N_BAND)
    sinks = sb("sinks", N_BAND)
    neg_sinks = sb("neg_sinks", N_BAND)
    eps_col = sb("eps_col", 1)
    bank = [ctx.enter_context(nc.psum_tensor(f"bank{i}", [P, 512], F32))[:, :] for i in range(8)]
    t5_row = nc.dram_tensor("t5_row", [P, N_BAND, 383], F32, kind="Internal").ap()

    def const_of(name, rows=P):
        a, b = CONST_COLS[name]
        return const[0:rows, a:b]

    ident = const_of("ident")
    rope_t = tok_flat[:, 0:512]
    stage = [tok_flat[:, 512 * k + 512:512 * k + 1024] for k in range(3)]
    turned = probs_t + [stage[2]]
    soft = {"o0": probs + [qa_flat[:, 6 * S:8 * S]], "o1": probs + [qa_flat[:, 6 * S:8 * S]],
            "o2": probs + [qb_flat[:, 4 * S:6 * S]]}
    cmp_t = stage[0]
    t5_const = tok_flat[:, 0:C_T5]

    vec_rows, vec_col = [], {}

    def rows_of(name, ap, n):
        vec_col[name] = len(vec_rows)
        vec_rows.extend((name, ap, r) for r in range(n))

    def as_rows(ap):
        return ap.rearrange("a (r c) -> (a r) c", c=P)

    for name in ("attn_norm", "mem_norm", "ffn_norm"):
        rows_of(name, as_rows(io[name]), 16)
    rows_of("final_norm", io["final_norm"].rearrange("(r c) -> r c", c=P), 8)
    rows_of("ckv_norm", io["dsa_ckv_norm"], 1)
    rows_of("norm_mix", as_rows(io["norm_mix_2"]), 16)
    rows_of("norm_ffn", as_rows(io["norm_ffn_2"]), 16)
    rows_of("b_pw1", as_rows(io["conv_b_pw1_2"]), 16)
    rows_of("w_dw", io["conv_w_dw_2"][0].rearrange("k (r c) -> (k r) c", c=P), CONV * DC)
    for name, src in (("b_dw", "conv_b_dw_2"), ("ln_g", "conv_ln_g_2"), ("ln_b", "conv_ln_b_2"),
                      ("b_pw2", "conv_b_pw2_2")):
        rows_of(name, as_rows(io[src]), 8)
    rows_of("norm_kv", io["norm_kv_2"].rearrange("(r c) -> r c", c=P), 8)
    rows_of("norm_final", io["norm_final_2"].rearrange("(r c) -> r c", c=P), 8)
    for name, src in (("pos_k", "nsa_cmp_pos_k"), ("pos_v", "nsa_cmp_pos_v")):
        rows_of(name, io[src][0].rearrange("(l two) d -> l (two d)", two=2), 16)
    assert len(vec_rows) <= 4 * P
    vec_tok = qb_flat[:, 0:4 * P].rearrange("p (t c) -> p t c", c=P)

    def vec(name, c):
        k = vec_col[name] + c
        return vec_t[:, k:k + 1]

    slots = []

    def cols(w, n0, n1):
        slots.append((w[:, n0:n1].rearrange("(c p) n -> p c n", p=P), DC, n1 - n0))

    def stage_slots(ranges):
        first = len(slots)
        for w, n0, n1 in ranges:
            cols(w, n0, n1)
        return first

    def ffn_slots(w_in, w_down):
        first = len(slots)
        for s in range(FF_STEPS + 1):
            if s < FF_STEPS:
                cols(w_in, 256 * s, 256 * s + 256)
                cols(w_in, DFF + 256 * s, DFF + 256 * s + 256)
            if s >= 1:
                slots.append((w_down[256 * (s - 1):256 * s, :].rearrange("(c p) n -> p c n", p=P), 2, D))
        return first, w_in, w_down

    kv0, kv1 = io["mem_w_kv"][0], io["mem_w_kv"][1]
    dsa, nsa = io["dsa_w_in"][0], io["nsa_w_in"][0]
    G_MEM = [stage_slots([(kv0, 0, 256), (kv0, 256, 512)]),
             stage_slots([(kv1, 0, 256), (kv1, 256, 512)])]
    G_DSA = stage_slots([(dsa, 1424, 1496), (dsa, 912, 1168), (dsa, 1168, 1424), (dsa, 768, 912),
                                (dsa, 0, 256), (dsa, 256, 512), (dsa, 512, 768), (dsa, 1496, 1752)])
    G_WO0 = stage_slots([(io["w_o"][0], 256 * i, 256 * i + 256) for i in range(4)])
    FF = [ffn_slots(io["ffn_w_in"][0], io["ffn_w_down"][0])]
    G_NSA = stage_slots([(nsa, 256 * i, 256 * i + 256) for i in range(4)]
                        + [(nsa, 1536, 1572), (nsa, 1024, 1280), (nsa, 1280, 1536), (nsa, 1572, 1828)])
    G_WO1 = stage_slots([(io["w_o"][1], 256 * i, 256 * i + 256) for i in range(4)])
    FF.append(ffn_slots(io["ffn_w_in"][1], io["ffn_w_down"][1]))
    pw1, pw2 = io["conv_w_pw1_2"][0], io["conv_w_pw2_2"][0]
    G_PW1 = stage_slots([r for i in range(4) for r in
                                ((pw1, 256 * i, 256 * i + 256), (pw1, D + 256 * i, D + 256 * i + 256))])
    G_PW2 = stage_slots([(pw2, 256 * i, 256 * i + 256) for i in range(4)])
    FF.append(ffn_slots(io["ffn_w_up_2"][0], io["ffn_w_down_2"][0]))
    G_KV = stage_slots([(io["w_kv_2"], 0, 256), (io["w_kv_2"], 256, 512)])
    G_Q = stage_slots([(io["w_q_2"][0], 256 * i, 256 * i + 256) for i in range(4)])
    G_WO2 = stage_slots([(io["w_o_2"][0], 256 * i, 256 * i + 256) for i in range(4)])
    FF.append(ffn_slots(io["ffn_w_up_2"][1], io["ffn_w_down_2"][1]))
    NSLOT = len(slots)

    proj_index, n = [], 0
    for _, chunks, _ in slots:
        proj_index.append(n)
        n += chunks == DC

    assert proj_index[G_DSA + 5] % 4 == 1

    PROD = ["mem0", "mem1", "attn0", "o0", "ffn0", "attn1", "o1", "ffn1", "mix0", "conv", "ffn2",
            "kv", "mix1", "o2", "ffn3"]
    prod = {name: i for i, name in enumerate(PROD)}
    ff_last = [f[0] + 3 * FF_STEPS - 3 for f in FF]
    last_use = [G_MEM[0] + 1, G_MEM[1] + 1, G_DSA + 7, G_WO0 + 3, ff_last[0], G_NSA + 7, G_WO1 + 3,
                ff_last[1], G_PW1 + 7, G_PW2 + 3, ff_last[2], G_KV + 1, G_Q + 3, G_WO2 + 3, ff_last[3]]

    SUMS = ["mem", "attn0", "ckv", "ffn0", "attn1", "ffn1", "final1", "mix0", "ln", "ffn2", "kv",
            "ffn3", "final2"]
    sum_no = {name: i for i, name in enumerate(SUMS)}
    ADDED = [name for name in SUMS if name not in ("ckv", "ln", "final1", "final2")]
    squares_no = {name: i for i, name in enumerate(name for name in SUMS if name != "ckv")}
    added_no = {name: i for i, name in enumerate(ADDED)}

    UPDATE = ["load", "ff0", "ff1", "renorm", "ff2", "ff3"]
    BY_SLOT = {"wo0": G_WO0, "wo1": G_WO1, "pw2": G_PW2, "wo2": G_WO2}

    CAUSAL = [(0, P), (P, 3 * P)]
    FULL = [(0, 2 * P), (2 * P, 4 * P)]
    EXTENT = {"dsa": CAUSAL, "slc": CAUSAL, "win": CAUSAL, "band": CAUSAL, "mem0": FULL, "mem1": FULL}
    TURN_TO = {3: (0, 1, 2), 4: (0, 2, 1, 3)}
    token_pairs = [(run, 2 * c + i) for c in range(N_TOK // 2) for run in ("slc", "win") for i in (0, 1)]
    HEADS, n = {}, 0
    for name, order in (("o0", [("dsa", h) for h in range(N_TOK)] + [("mem0", h) for h in range(N_MEM_H)]),
                        ("o1", token_pairs + [("mem1", h) for h in range(N_MEM_H)]),
                        ("o2", [("band", h) for h in range(N_BAND)])):
        HEADS[name] = [(n + i, run, h) for i, (run, h) in enumerate(order)]
        n += len(order)
    G_OUT = {"o0": G_WO0, "o1": G_WO1, "o2": G_WO2}

    GATE = {"slc": 1, "win": 2}

    def scaling(n, run, h, b):
        own = factor[:, 2 * n + b:2 * n + b + 1]
        if run not in GATE:
            return own, None, ALU.mult
        at = 36 * b + 3 * h + GATE[run]
        return own, gates[:, at:at + 1], ALU.mult, ALU.mult

    def chunk_of(run, h):
        return h // 2 + (N_TOK // 2 if run.startswith("mem") else 0)

    def last_head(name, c2):
        return max(i for i, (_, run, h) in enumerate(HEADS[name]) if chunk_of(run, h) // 2 == c2)

    def out_bank(name, c2):
        return proj_bank(G_OUT[name] + c2)

    def out_done(eng, name, c2):
        eng.wait_ge(sem("pv_done"), HEADS[name][last_head(name, c2)][0] // 2 + 1)

    POOL_SLOTS = [g + i for g in (G_WO0, G_WO1, G_WO2) for i in range(2)]

    POOL_CHUNKS, PE_CHUNKS = (0, 2, 4), (5, 6, 7)
    DVE_CHUNKS = tuple(c for c in range(DC) if c not in POOL_CHUNKS + PE_CHUNKS)
    PAIRS = (CONV + 1) // 2
    NPAIR, NDIAG = 3, 16
    pair_of = lambda j: qb_flat[:, 512 * (j % NPAIR):512 * (j % NPAIR) + 512]
    diag_of = lambda j: qa_flat[:, P * (j % NDIAG):P * (j % NDIAG) + P]

    ROT = ["k_idx", "q_idx0", "q_idx1", "q0", "k_rope", "q1", "q2",
           "nq0", "nq1", "nq2", "ks", "kw"]
    rot_no = {name: i for i, name in enumerate(ROT)}
    rot_src = {
        "k_idx": stage[2][0:HD, 0:S], "q_idx0": stage[0], "q_idx1": stage[1],
        "q0": stage[0], "q1": stage[1], "q2": stage[0], "k_rope": qa_flat[0:ROPE, S:2 * S],
        "nq0": qa_flat[:, 0:512], "nq1": qa_flat[:, 512:1024], "nq2": qa_flat[:, 1024:1536],
        "ks": stage[1][:, 0:S], "kw": stage[2][:, 0:S],
    }

    def rot_shape(name):
        src = rot_src[name]
        return src.shape[0], src.shape[1]

    def rot_bank(name):
        return bank[{"q1": 5, "q2": 6}[name]] if name in ("q1", "q2") else bank[2 + rot_no[name] % 2]

    def landed(eng, g, j=0):
        eng.wait_ge(sem(f"raw_landed{g % NR}"), 16 * (g // NR + 1) + 32 * j)

    def slot_cols(g):
        return slots[g][1] * slots[g][2]

    def proj_bank(g):
        return bank[4 + proj_index[g] % 4]

    def used(eng, g, j=0):
        eng.wait_ge(sem("slot_used"), g + 1 + 6 * j)

    def evicted(eng, g, j=0):
        eng.wait_ge(sem("proj_evicted"), proj_index[g] + 1 + 4 * j)

    def x_updated(eng, u, c2):
        if u in BY_SLOT:
            evicted(eng, BY_SLOT[u] + c2)
        else:
            eng.wait_ge(sem("x_ready"), 4 * UPDATE.index(u) + c2 + 1)

    def set_free(eng, p):
        if p >= 2:
            used(eng, last_use[p - 2])

    def halves(ap):
        return ap.rearrange("p (c t) -> p c t", t=S)

    def over_two(ap):
        return bass.AP(ap.tensor, ap.offset, [ap.ap[0], [0, 2], ap.ap[1]])

    block = ctx.enter_context(nc.Block())

    pieces, r = [], 0
    while r < len(vec_rows):
        name, ap, r0 = vec_rows[r]
        m = 1
        while r + m < len(vec_rows) and vec_rows[r + m][0] == name and (r + m) % P:
            m += 1
        pieces.append((r, m, ap[r0:r0 + m, :]))
        r += m
    VEC_ALL, SMALL_ALL = 16 * len(pieces), 16 * 8

    @block.sync
    def _(sp):
        def load(g, j=0, src=None):
            ap, chunks, w = slots[g]
            if g >= NR:
                sp.wait_ge(sem("w_lo_done"), g - NR + 1 + 6 * j)
            sp.dma_start(raw[g % NR][:, 0:chunks * w].rearrange("p (c n) -> p c n", c=chunks),
                         ap if src is None else src).then_inc(sem(f"raw_landed{g % NR}"), 16)

        def ffn(first, w_in, w_down):
            for g in range(first, first + 5):
                load(g)
            with sp.Fori(0, (FF_STEPS - 3) // 2) as j:
                for u in (0, 1):
                    g = first + 5 + 3 * u
                    n0 = 256 * (2 + u)
                    gate = w_in[:, bass.ds(512 * j + n0, 256)].rearrange("(c p) n -> p c n", p=P)
                    up = w_in[:, bass.ds(512 * j + n0 + DFF, 256)].rearrange("(c p) n -> p c n", p=P)
                    down = w_down[bass.ds(512 * j + n0 - 256, 256), :].rearrange("(c p) n -> p c n", p=P)
                    load(g, j, gate)
                    load(g + 1, j, up)
                    load(g + 2, j, down)
            for g in range(first + 3 * FF_STEPS - 4, first + 3 * FF_STEPS):
                load(g)

        for b in range(TB):
            sp.dma_start(mem_tok[:, b, :], io["mem"][0, P * b:P * b + P, :]).then_inc(sem("mem_landed"), 16)
        sp.wait_ge(sem("cleared"), 1)
        for r, m, src in pieces[1::2]:
            sp.dma_start(vec_tok[r % P:r % P + m, r // P, :], src).then_inc(sem("vec_landed"), 16)
        load(0)
        load(1)
        sp.dma_start(tok, io["x"][0].rearrange("(b p) n -> p b n", p=P)).then_inc(sem("x_landed"), 16)
        g = 2
        firsts = {f[0]: f for f in FF}
        while g < NSLOT:
            if g in firsts:
                ffn(*firsts[g])
                g += 3 * FF_STEPS
            else:
                load(g)
                g += 1
        for i in range(4):
            b, half = i % 2, slice(512 * (i // 2), 512 * (i // 2) + 512)
            sp.wait_ge(sem("result_ready"), i + 1)
            sp.dma_start(out[0, b * P:(b + 1) * P, half], tok[:, b, half]).then_inc(sem("out_written"), 16)
        sp.wait_ge(sem("out_written"), 16 * 4)
        sp.wait_ge(sem("t5_stored"), 16)

    @block.gpsimd
    def _(pool):
        def add_squares(name):
            k = added_no[name]
            for i in range(1, 4):
                pool.wait_ge(sem("squared"), 4 * squares_no[name] + i + 1)
                if i > 1:
                    pool.wait_ge(sem("partly_added"), 3 * k + i - 1)
                pool.tensor_tensor(qa_flat[:, 0:512], qa_flat[:, 0:512], qa_flat[:, 512 * i:512 * i + 512],
                                   ALU.add).then_inc(sem("partly_added"), 1)
            pool.wait_ge(sem("partly_added"), 3 * k + 3)
            pool.tensor_tensor(qa_flat[:, 0:S], qa_flat[:, 0:S], qa_flat[:, S:2 * S],
                               ALU.add).then_inc(sem("added"), 1)

        def clear_keys(tiles, k):
            if k:
                pool.wait_ge(sem("keys_cleared"), 2 * k)
            pool.memset(tiles[0:HD, 1::2, :], 0.0).then_inc(sem("keys_cleared"), 1)
            pool.wait_ge(sem("keys_cleared"), 2 * k + 1)
            pool.memset(tiles[HD:P, 0::2, :], 0.0).then_inc(sem("keys_cleared"), 1)

        def convert(g):
            pool.wait_ge(sem("w_lo_done"), g)
            pool.wait_ge(sem("w_hi_done"), g + 1)
            n = slot_cols(g)
            pool.tensor_tensor(w_lo[g % NS][:, 0:n], raw[g % NR][:, 0:n], w_hi[g % NS][:, 0:n].bitcast(F32),
                               ALU.subtract).then_inc(sem("w_lo_done"), 1)

        def scale_first(name):
            for n, run, h in HEADS[name]:
                lo, hi = EXTENT[run][0]
                block = soft[name][n % 3][:, lo:hi]
                pool.wait_ge(sem("factor_ready"), n + 1)
                pool.tensor_scalar(block, block, *scaling(n, run, h, 0)).then_inc(sem("first_scaled"), 1)

        pool.memset(vec_tok, 0.0).then_inc(sem("cleared"), 1)
        pool.memset(w_uk, 0.0).then_inc(sem("cleared"), 1)
        pool.memset(ones, 1.0).then_inc(sem("cleared"), 1)
        pool.memset(eps_col, EPS).then_inc(sem("cleared"), 1)
        pool.dma_start(const[:, P:C_MAIN], io["const"][:, P:C_MAIN]).then_inc(sem("const_landed"), 16)
        pool.wait_ge(sem("cleared"), 2)
        for half in (0, HD):
            pool.dma_start(w_uk[:, half + ROPE:half + HD], io["dsa_w_uk"][0]).then_inc(sem("small_landed"), 16)
        pool.dma_start(w_uv, io["dsa_w_uv"][0]).then_inc(sem("small_landed"), 16)
        for k, name in enumerate(("nsa_cmp_k_w2", "nsa_cmp_k_w2", "nsa_cmp_v_w2")):
            pool.dma_start(cmp_w2[:, k * HD:(k + 1) * HD], io[name][0]).then_inc(sem("small_landed"), 16)
        pool.dma_start(rel_bias[0:BUCKETS, :], io["rel_bias_2"]).then_inc(sem("small_landed"), 16)
        pool.dma_start(sinks, bass.AP(io["sinks_2"].tensor, 0, [[0, P], [1, N_BAND]])).then_inc(sem("small_landed"), 16)
        pool.memset(cmp_k, 0.0).then_inc(sem("cmp_k_cleared"), 1)
        pool.wait_ge(sem("cmp_k_cleared"), 1)
        for k, tiles in enumerate((keys, k_mem[1])):
            clear_keys(tiles, k)
        pool.wait_ge(sem("keys_cleared"), 4)
        add_squares("mem")
        pool.wait_ge(sem("h_ready"), 4 * (prod["mem1"] + 1))
        for m, name in enumerate(("nsa_cmp_k_w1", "nsa_cmp_v_w1")):
            pool.dma_start(cmp_w1[:, m], io[name][0].rearrange("(l p) h -> p l h", p=P)).then_inc(sem("cmp_w1_landed"), 16)
        add_squares("attn0")
        convert(G_WO0)
        convert(G_WO0 + 1)
        scale_first("o0")
        for name in ("ffn0", "attn1"):
            add_squares(name)
        convert(G_WO1)
        convert(G_WO1 + 1)
        scale_first("o1")
        pool.wait_ge(sem("h_ready"), 4 * (prod["o1"] + 1))
        pool.dma_start(t5_const, io["const"][:, C_MAIN:C_MAIN + C_T5]).then_inc(sem("t5_landed"), 16)
        pool.memset(glu_pad[:, :, 0:PAD], 0.0).then_inc(sem("pad_cleared"), 1)
        for name in ("ffn1", "mix0"):
            add_squares(name)
        pool.wait_ge(sem("t5_row_ready"), 1)
        row = tok_flat[0:N_BAND, C_T5:C_T5 + 383]
        pool.dma_start(t5_row.rearrange("q h m -> h q m"),
                       bass.AP(row.tensor, row.offset, [row.ap[0], [0, P], row.ap[1]])).then_inc(sem("t5_stored"), 16)
        acc = probs_t[0]
        for c in POOL_CHUNKS:
            for j in range(PAIRS):
                n = PAIRS * POOL_CHUNKS.index(c) + j
                w = S * min(2, CONV - 2 * j)
                pool.wait_ge(sem("pair_ready"), n + 1)
                if n:
                    pool.wait_ge(sem("pair_added"), n)
                if j == 0:
                    if c != POOL_CHUNKS[0]:
                        pool.wait_ge(sem("pool_chunk_done"), POOL_CHUNKS.index(c))
                    pool.tensor_copy(acc, pair_of(n)).then_inc(sem("pair_added"), 1)
                else:
                    pool.tensor_tensor(acc[:, 0:w], acc[:, 0:w], pair_of(n)[:, 0:w], ALU.add).then_inc(sem("pair_added"), 1)
            pool.wait_ge(sem("pair_added"), PAIRS * (POOL_CHUNKS.index(c) + 1))
            pool.tensor_tensor(conv_y[:, c, :], acc[:, 0:S], acc[:, S:2 * S], ALU.add).then_inc(sem("pool_chunk_done"), 1)
        pool.wait_ge(sem("t5_stored"), 16)
        pool.wait_ge(sem("h_ready"), 4 * (prod["conv"] + 1))
        for h0 in range(0, N_BAND, 4):
            pool.dma_start(t5_bias[:, h0:h0 + 4, :], bass.AP(t5_row.tensor, h0 * 383 + P - 1,
                                                            [[N_BAND * 383 - 1, P], [383, 4], [1, S]])
                           ).then_inc(sem("t5_bias_landed"), 16)
        for name in ("ffn2", "kv"):
            add_squares(name)
        convert(G_WO2)
        convert(G_WO2 + 1)
        scale_first("o2")
        add_squares("ffn3")

    @block.scalar
    def _(act):
        def convert(g, j=0):
            if g >= NSLOT:
                return
            landed(act, g, j)
            if g >= NS:
                used(act, g - NS, j)
            n = slot_cols(g)
            nc.scalar.activation(w_hi[g % NS][:, 0:n], raw[g % NR][:, 0:n], ACT.Copy).then_inc(sem("w_hi_done"), 1)

        def unit(g):
            convert(g + 2)

        def split_hi(p, src, gain, ready, pairs=range(4)):
            set_free(act, p)
            for c in (2 * c2 + i for c2 in pairs for i in range(2)):
                if c % 2 == 0:
                    ready(c // 2)
                ins = nc.scalar.activation(h_hi[p % 2][:, c, :], src[:, c, :], ACT.Copy, scale=gain(c))
                if c % 2:
                    ins.then_inc(sem("h_hi_done"), 1)

        def squares(name, src, ready, pairs=range(4)):
            k = sum_no[name]
            if k >= 1 and 0 in pairs:
                act.wait_ge(sem("sum_ready"), k)
            for c2 in pairs:
                ready(c2)
                nc.scalar.activation(halves(qa_flat)[:, 2 * c2:2 * c2 + 2, :], src[:, 2 * c2:2 * c2 + 2, :],
                                     ACT.Square).then_inc(sem("squared"), 1)

        def root(name, scale=1.0 / D):
            k = sum_no[name]
            act.wait_ge(sem("sum_ready"), k + 1)
            if k >= 1:
                act.wait_ge(sem("rstd_ready"), k)
            nc.scalar.activation(rms, bank[0][:, 0:S], ACT.Sqrt, scale=scale,
                                 bias=eps_col[:, 0:1]).then_inc(sem("root_done"), 1)

        def split_pair(name, u, gain, c2):
            split_hi(prod[name], x, gain, lambda c2: x_updated(act, u, c2), (c2,))
            squares(name, x, lambda c2: None, (c2,))

        def norm(name, u, gain):
            for c2 in range(4):
                split_pair(name, u, gain, c2)
            root(name)

        def added_slots(g0, u, name, gain):
            for i in range(4):
                unit(g0 + i)
                if i >= 1:
                    split_pair(name, u, gain, i - 1)
            split_pair(name, u, gain, 3)
            root(name)

        def softmax(name):
            heads, p = HEADS[name], prod[name]

            def exponentials(n, run, h):
                extent = EXTENT[run]
                in_psum = extent is FULL
                act.wait_ge(sem("max_ready"), n + 1)
                if n >= 3:
                    act.wait_ge(sem("probs_turned"), n - 2)
                for b in range(TB):
                    lo, hi = extent[b]
                    src = bank[n % 2] if in_psum else scores[n % 2]
                    col = slice(2 * n + b, 2 * n + b + 1)
                    ins = nc.scalar.activation(soft[name][n % 3][:, lo:hi], src[:, lo:hi], ACT.Exp,
                                               bias=shift[:, col], scale=SCALE if in_psum else -1.0,
                                               accum_out=row_sum[:, col])
                ins.then_inc(sem("exp_done"), 1)
                if run == "band":
                    nc.scalar.activation(sink_exp[:, 2 * h:2 * h + 2], shift[:, 2 * n:2 * n + 2], ACT.Exp,
                                         bias=sinks[:, h:h + 1]).then_inc(sem("sink_done"), 1)

            def copy_t(n, run, h):
                width = EXTENT[run][1][1]
                act.wait_ge(sem("probs_turned"), n + 1)
                if n >= 3:
                    act.wait_ge(sem("pv_done"), (n - 3) // 2 + 1)
                nc.scalar.activation(turned[n % 3][:, 0:width], bank[2 + n % 2][:, 0:width],
                                     ACT.Copy).then_inc(sem("probs_t_ready"), 1)

            def output_hi(c2):
                if c2 == 0:
                    set_free(act, p)
                out_done(act, name, c2)
                nc.scalar.activation(h_hi[p % 2][:, 2 * c2:2 * c2 + 2, :], halves(out_bank(name, c2)),
                                     ACT.Copy).then_inc(sem("h_hi_done"), 1)

            for i in range(len(heads) + 4):
                if i < len(heads):
                    exponentials(*heads[i])
                if 0 <= i - 2 < len(heads):
                    copy_t(*heads[i - 2])
                for c2 in range(4):
                    if i == last_head(name, c2) + 4:
                        output_hi(c2)

        def ffn(f):
            first = FF[f][0]

            def gate(s, g, j=0):
                evicted(act, g, j)
                nc.scalar.activation(scores[1], scores[0], ACT.Silu).then_inc(sem("silu_done"), 1)

            def hidden(s, g, j=0):
                evicted(act, g, j)
                nc.scalar.activation(ff_hi[s % 2], probs[0], ACT.Copy).then_inc(sem("ff_hi_done"), 1)

            def step(s, j=0):
                g = first + 3 * s - 1
                convert(g + 2, j)
                gate(s, g, j)
                convert(g + 3, j)
                hidden(s, g + 1, j)
                convert(g + 4, j)

            convert(first + 2)
            gate(0, first)
            convert(first + 3)
            hidden(0, first + 1)
            step(1)
            with act.Fori(0, (FF_STEPS - 3) // 2) as j:
                step(2, j)
                step(3, j)
            step(FF_STEPS - 1)
            convert(first + 3 * FF_STEPS - 1 + 2)

        act.dma_start(ident, io["const"][:, 0:P]).then_inc(sem("ident_landed"), 16)
        act.wait_ge(sem("cleared"), 1)
        for r, m, src in pieces[0::2]:
            act.dma_start(vec_tok[r % P:r % P + m, r // P, :], src).then_inc(sem("vec_landed"), 16)
        squares("mem", mem_t, lambda c2: act.wait_ge(sem("mem_turned"), c2 + 1))
        act.wait_ge(sem("vec_ready"), 1)
        act.wait_ge(sem("cleared"), 4)
        convert(0)
        split_hi(prod["mem0"], mem_t, lambda c: vec("mem_norm", c), lambda c2: None)
        convert(1)
        root("mem")
        split_hi(prod["mem1"], mem_t, lambda c: vec("mem_norm", DC + c), lambda c2: None)
        for g in range(3):
            unit(g)
        for c2 in range(4):
            split_pair("attn0", "load", lambda c: vec("attn_norm", c), c2)
        unit(3)
        root("attn0")

        for g in range(G_DSA, G_DSA + 3):
            unit(g)
        unit(G_DSA + 3)
        evicted(act, G_DSA + 3)
        nc.scalar.activation(qa_flat[:, 2 * S:3 * S], qa_flat[:, 0:S], ACT.Square).then_inc(sem("ckv_squared"), 1)
        for h in range(N_IDX):
            act.wait_ge(sem("idx_scored"), h + 1)
            if h >= 2:
                act.wait_ge(sem("idx_weighed"), h - 1)
            nc.scalar.activation(scores[h % 2][:, 0:3 * P], bank[h % 2][:, 0:3 * P],
                                 ACT.Relu).then_inc(sem("idx_relu"), 1)
        unit(G_DSA + 4)
        root("ckv", 1.0 / P)
        for g in range(G_DSA + 5, G_DSA + 8):
            unit(g)
        softmax("o0")
        added_slots(G_WO0, "wo0", "ffn0", lambda c: vec("ffn_norm", c))
        ffn(0)
        norm("attn1", "ff0", lambda c: vec("attn_norm", DC + c))

        for g in range(G_NSA, G_NSA + 4):
            unit(g)
        evicted(act, G_NSA + 3)
        for m in range(2):
            ft = probs_t[m][:, 0:32 * NCMP].rearrange("p (l g c) -> p l g c", l=16, g=2)
            for par in range(2):
                for grp in range(2):
                    src = stage[0][grp * HD:(grp + 1) * HD, m * S:(m + 1) * S]
                    view = bass.AP(src.tensor, src.offset + par, [src.ap[0], [2, 16], [CMP_STRIDE, NCMP]])
                    nc.scalar.activation(ft[par * HD:(par + 1) * HD, :, grp, :], view,
                                         ACT.Copy).then_inc(sem("ft_copied"), 1)
        unit(G_NSA + 4)
        evicted(act, G_NSA + 4)
        nc.scalar.activation(probs[1][0:36, 0:S], probs[1][0:36, S:2 * S], ACT.Sigmoid).then_inc(sem("gates_open"), 1)
        unit(G_NSA + 5)
        for m in range(2):
            act.wait_ge(sem("cmp_hidden"), m + 1)
            nc.scalar.activation(scores[0][:, 32 * m:32 * m + 2 * NCMP], bank[m][:, 0:2 * NCMP],
                                 ACT.Gelu_apprx_tanh).then_inc(sem("gelu_done"), 1)
        unit(G_NSA + 6)
        unit(G_NSA + 7)
        act.wait_ge(sem("cmp_shifted"), 1)
        nc.scalar.activation(probs[0][:, 0:24 * NCMP], scores[1][:, 0:24 * NCMP], ACT.Exp).then_inc(sem("cmp_exp"), 1)
        softmax("o1")
        added_slots(G_WO1, "wo1", "ffn1", lambda c: vec("ffn_norm", DC + c))
        ffn(1)
        squares("final1", x, lambda c2: x_updated(act, "ff1", c2))
        root("final1")

        norm("mix0", "renorm", lambda c: vec("norm_mix", c))

        def sigmoids(i):
            evicted(act, G_PW1 + 2 * i + 1)
            for t in range(2):
                nc.scalar.activation(scores[1][:, S * t:S * t + S], scores[0][:, S * t:S * t + S], ACT.Sigmoid,
                                     bias=vec("b_pw1", DC + 2 * i + t)).then_inc(sem("glu_sigmoid"), 1)

        def products(c, j0, j1):
            act.wait_ge(sem("glu_ready"), c + 1)
            for j in range(j0, j1):
                n = PAIRS * POOL_CHUNKS.index(c) + j
                if n >= NPAIR:
                    act.wait_ge(sem("pair_added"), n - NPAIR + 1)
                for k in range(2 * j, min(2 * j + 2, CONV)):
                    ins = nc.scalar.activation(pair_of(n)[:, S * (k % 2):S * (k % 2) + S], glu_pad[:, c, k:k + S],
                                               ACT.Copy, scale=vec("w_dw", DC * k + c))
                ins.then_inc(sem("pair_ready"), 1)

        unit(G_PW1)
        unit(G_PW1 + 1)
        unit(G_PW1 + 2)
        sigmoids(0)
        products(0, 0, 6)
        unit(G_PW1 + 3)
        products(0, 6, 8)
        unit(G_PW1 + 4)
        sigmoids(1)
        products(0, 8, 11)
        unit(G_PW1 + 5)
        products(0, 11, 14)
        unit(G_PW1 + 6)
        sigmoids(2)
        products(0, 14, PAIRS)
        products(2, 0, 2)
        unit(G_PW1 + 7)
        products(2, 2, 6)
        sigmoids(3)
        products(2, 6, PAIRS)
        products(4, 0, PAIRS)
        squares("ln", conv_y, lambda c2: act.wait_ge(sem("centred"), c2 + 1))
        root("ln")
        p = prod["conv"]
        for c2 in range(4):
            act.wait_ge(sem("ln_scaled"), c2 + 1)
            for c in (2 * c2, 2 * c2 + 1):
                nc.scalar.activation(conv_y[:, c, :], conv_y[:, c, :], ACT.Silu, scale=vec("ln_g", c),
                                     bias=vec("ln_b", c)).then_inc(sem("conv_silu"), 1)
            act.wait_ge(sem("conv_silu"), 2 * c2 + 2)
            if c2 == 0:
                set_free(act, p)
            nc.scalar.activation(h_hi[p % 2][:, 2 * c2:2 * c2 + 2, :], conv_y[:, 2 * c2:2 * c2 + 2, :],
                                 ACT.Copy).then_inc(sem("h_hi_done"), 1)
        added_slots(G_PW2, "pw2", "ffn2", lambda c: vec("norm_ffn", c))
        ffn(2)

        for c2 in range(4):
            split_pair("kv", "ff2", lambda c: vec("norm_kv", c), c2)
        split_hi(prod["mix1"], x, lambda c: vec("norm_mix", DC + c), lambda c2: None)
        root("kv")
        for g in range(G_KV, G_KV + 2 + 4):
            unit(g)
        softmax("o2")
        added_slots(G_WO2, "wo2", "ffn3", lambda c: vec("norm_ffn", DC + c))
        ffn(3)
        squares("final2", x, lambda c2: x_updated(act, "ff3", c2))
        root("final2")

    @block.vector
    def _(dve):
        chain = [0]

        def link(ins):
            chain[0] += 1
            ins.then_inc(sem("dve_link"), 1)
            dve.wait_ge(sem("dve_link"), chain[0])

        def convert(g, j=0):
            if g >= NSLOT or g in POOL_SLOTS:
                return
            dve.wait_ge(sem("w_hi_done"), g + 1 + 6 * j)
            if g - 1 in POOL_SLOTS:
                dve.wait_ge(sem("w_lo_done"), g)
            n = slot_cols(g)
            nc.vector.tensor_tensor(w_lo[g % NS][:, 0:n], raw[g % NR][:, 0:n], w_hi[g % NS][:, 0:n].bitcast(F32),
                                    ALU.subtract).then_inc(sem("w_lo_done"), 1)

        def take(g, dst, scale=rstd, j=0, rows=P, n=2):
            used(dve, g, j)
            src = proj_bank(g)[0:rows, 0:n * S]
            if n == 2:
                ins = nc.vector.tensor_tensor(halves(dst), halves(src), over_two(scale[0:rows]), ALU.mult)
            else:
                ins = nc.vector.tensor_tensor(dst, src, scale[0:rows], ALU.mult)
            ins.then_inc(sem("proj_evicted"), 1)

        def take_keys(g, upper, lower, scale=rstd):
            used(dve, g)
            nc.vector.tensor_tensor(upper[0:HD], halves(proj_bank(g))[0:HD], over_two(scale[0:HD]), ALU.mult)
            mark("proj_evicted", nc.vector.tensor_tensor(lower[HD:P], halves(proj_bank(g))[HD:P], over_two(scale[HD:P]),
                                                         ALU.mult))

        def split_lo(p, src, gain, pairs=range(4)):
            for c in (2 * c2 + i for c2 in pairs for i in range(2)):
                if c % 2 == 0:
                    dve.wait_ge(sem("h_hi_done"), 4 * p + c // 2 + 1)
                ins = nc.vector.scalar_tensor_tensor(h_lo[p % 2][:, c, :], src[:, c, :], gain(c),
                                                     h_hi[p % 2][:, c, :].bitcast(F32), ALU.mult, ALU.subtract)
                if c % 2:
                    ins.then_inc(sem("h_ready"), 1)

        def split_lo_pairs(p, src):
            for c2 in range(4):
                dve.wait_ge(sem("h_hi_done"), 4 * p + c2 + 1)
                nc.vector.tensor_tensor(h_lo[p % 2][:, 2 * c2:2 * c2 + 2, :], src(c2),
                                        h_hi[p % 2][:, 2 * c2:2 * c2 + 2, :].bitcast(F32),
                                        ALU.subtract).then_inc(sem("h_ready"), 1)

        def inverse(name, dst=rstd):
            dve.wait_ge(sem("root_done"), sum_no[name] + 1)
            ins = nc.vector.reciprocal(dst, rms)
            ins.then_inc(sem("rstd_ready"), 1)
            dve.wait_ge(sem("rstd_ready"), sum_no[name] + 1)

        def split_pair(name, u, gain, c2):
            x_updated(dve, u, c2)
            split_lo(prod[name], x, gain, (c2,))

        def rotate(name, dst, lower=None, signal=None):
            rows, n = rot_shape(name)
            src, two = rot_src[name], n == 2 * S
            cos, sin = const_of("cos", rows), const_of("sin", rows)
            if two:
                cos, sin, src = over_two(cos), over_two(sin), halves(src)
            shape = halves if two else (lambda ap: ap)
            dve.wait_ge(sem("rotated"), rot_no[name] + 1)
            link(nc.vector.tensor_tensor(shape(rope_t[0:rows, 0:n]), shape(rot_bank(name)[0:rows, 0:n]), sin, ALU.mult))
            link(nc.vector.tensor_tensor(shape(dst) if lower is None else src, src, cos, ALU.mult))
            if lower is None:
                ins = nc.vector.tensor_tensor(shape(dst), shape(dst), shape(rope_t[0:rows, 0:n]), ALU.add)
                if signal is None:
                    link(ins)
                else:
                    mark(signal, ins)
                    dve.wait_ge(sem(signal), 1)
            else:
                nc.vector.tensor_tensor(lower[HD:P], src[HD:P], rope_t[HD:P, 0:n], ALU.add)
                link(nc.vector.tensor_tensor(dst[0:HD], src[0:HD], rope_t[0:HD, 0:n], ALU.add))

        def mark(name, ins):
            ins.then_inc(sem(name), 1)

        def attend(name, mask, init=None, between={}):
            heads, p = HEADS[name], prod[name]

            def masked(n, run, h):
                dve.wait_ge(sem("qk_done"), n + 1)
                pair = shift[:, 2 * n:2 * n + 2]
                if EXTENT[run] is FULL:
                    link(nc.vector.tensor_reduce(pair, halves(bank[n % 2]), AX.X, ALU.max))
                    mark("max_ready", nc.vector.tensor_scalar(pair, pair, -SCALE, None, ALU.mult))
                    return
                if n >= 2:
                    dve.wait_ge(sem("exp_done"), n - 1)
                for b in range(TB):
                    lo, hi = CAUSAL[b]
                    ins = nc.vector.tensor_tensor_reduce(
                        scores[n % 2][:, lo:hi], bank[n % 2][:, lo:hi], mask[run](h, b), -SCALE,
                        -NEG if init is None else init(h), ALU.add, ALU.min, shift[:, 2 * n + b:2 * n + b + 1])
                mark("max_ready", ins)

            def scaled(n, run, h):
                fac, den = factor[:, 2 * n:2 * n + 2], row_sum[:, 2 * n:2 * n + 2]
                dve.wait_ge(sem("exp_done"), n + 1)
                if run == "band":
                    dve.wait_ge(sem("sink_done"), h + 1)
                    link(nc.vector.tensor_tensor(fac, den, sink_exp[:, 2 * h:2 * h + 2], ALU.add))
                    den = fac
                mark("factor_ready", nc.vector.reciprocal(fac, den))
                dve.wait_ge(sem("factor_ready"), n + 1)
                lo, hi = EXTENT[run][1]
                block = soft[name][n % 3][:, lo:hi]
                mark("probs_scaled", nc.vector.tensor_scalar(block, block, *scaling(n, run, h, 1)))

            def output_lo(c2):
                dve.wait_ge(sem("h_hi_done"), 4 * p + c2 + 1)
                mark("h_ready", nc.vector.tensor_tensor(
                    h_lo[p % 2][:, 2 * c2:2 * c2 + 2, :], halves(out_bank(name, c2)),
                    h_hi[p % 2][:, 2 * c2:2 * c2 + 2, :].bitcast(F32), ALU.subtract))

            for i in range(len(heads) + 6):
                if 0 <= i - 2 < len(heads):
                    scaled(*heads[i - 2])
                if i < len(heads):
                    masked(*heads[i])
                if i in between:
                    between[i]()
                for c2 in range(4):
                    if i == last_head(name, c2) + 6:
                        output_lo(c2)

        def add_slots(g0, u, name, gain, bias=None):
            for i in range(4):
                g = g0 + i
                convert(g + 2)
                if i >= 1:
                    split_pair(name, u, gain, i - 1)
                used(dve, g)
                xs = x[:, 2 * i:2 * i + 2, :]
                if bias is None:
                    mark("proj_evicted", nc.vector.tensor_tensor(xs, halves(proj_bank(g)), xs, ALU.add))
                else:
                    for t in range(2):
                        c = 2 * i + t
                        ins = nc.vector.scalar_tensor_tensor(x[:, c, :], proj_bank(g)[:, S * t:S * t + S], vec(bias, c),
                                                             x[:, c, :], ALU.add, ALU.add)
                    mark("proj_evicted", ins)
            split_pair(name, u, gain, 3)
            inverse(name)

        def ffn(f, name=None, gain=None, then=lambda: None):
            first = FF[f][0]
            n0 = FF_STEPS * f

            def gates_of(g, j=0):
                take(g, scores[0], j=j)

            def hidden(s, g, j=0):
                dve.wait_ge(sem("silu_done"), n0 + s + 1 + 2 * j)
                mark("silu_scaled", nc.vector.tensor_tensor(halves(probs_t[0]), halves(scores[1]), over_two(rstd), ALU.mult))
                used(dve, g, j)
                dve.wait_ge(sem("silu_scaled"), n0 + s + 1 + 2 * j)
                mark("proj_evicted", nc.vector.tensor_tensor(probs[0], proj_bank(g), probs_t[0], ALU.mult))
                dve.wait_ge(sem("ff_hi_done"), n0 + s + 1 + 2 * j)
                mark("ff_ready", nc.vector.tensor_tensor(ff_lo[s % 2], probs[0], ff_hi[s % 2].bitcast(F32), ALU.subtract))

            def step(s, j=0):
                g = first + 3 * s - 1
                convert(g + 2, j)
                gates_of(g, j)
                convert(g + 3, j)
                hidden(s, g + 1, j)
                convert(g + 4, j)

            convert(first + 2)
            gates_of(first)
            convert(first + 3)
            hidden(0, first + 1)
            step(1)
            with dve.Fori(0, (FF_STEPS - 3) // 2) as j:
                step(2, j)
                step(3, j)
            step(FF_STEPS - 1)
            for c2 in range(4):
                dve.wait_ge(sem("down_done"), 4 * f + c2 + 1)
                xs = x[:, 2 * c2:2 * c2 + 2, :]
                mark("x_ready", nc.vector.tensor_tensor(xs, halves(bank[c2]), xs, ALU.add))
                if name is not None and c2 >= 1:
                    split_pair(name, f"ff{f}", gain, c2 - 1)
            if name is not None:
                split_pair(name, f"ff{f}", gain, 3)
            convert(first + 3 * FF_STEPS - 1 + 2)
            then()
            if name is not None:
                inverse(name)

        def rescale_x(name, gain, signal, then=None):
            inverse(name)
            for c in range(DC):
                ins = nc.vector.scalar_tensor_tensor(x[:, c, :], x[:, c, :], gain(c), rstd, ALU.mult, ALU.mult)
                if c % 2:
                    mark(signal, ins)
                if then is not None and c in (3, 5, 7):
                    then(c // 2 - 1)

        for c2 in range(4):
            dve.wait_ge(sem("mem_t_done"), c2 + 1)
            mark("mem_turned", nc.vector.tensor_copy(mem_t[:, 2 * c2:2 * c2 + 2, :], halves(bank[4 + c2])))
        dve.wait_ge(sem("vec_turned"), 1)
        mark("vec_ready", nc.vector.tensor_copy(vec_t, bank[1]))
        dve.wait_ge(sem("mem_turned"), 4)
        dve.wait_ge(sem("vec_ready"), 1)
        convert(0)
        split_lo(prod["mem0"], mem_t, lambda c: vec("mem_norm", c))
        convert(1)
        inverse("mem", rstd_mem)

        def mem_slots(layer, *between):
            g = G_MEM[layer]
            convert(g + 2)
            for step in between:
                step()
            take_keys(g, k_mem[layer][:, 0::2], k_mem[layer][:, 1::2], rstd_mem)
            convert(g + 3)
            take(g + 1, probs[layer], rstd_mem)

        def mem_values(layer):
            dve.wait_ge(sem("v_turned"), layer + 1)
            mark("v_mem_ready", nc.vector.tensor_copy(v_mem[:, layer].rearrange("p b n -> p (b n)"), bank[1 + layer]))

        mem_slots(0, lambda: split_lo(prod["mem1"], mem_t, lambda c: vec("mem_norm", DC + c)))
        for c2 in range(4):
            dve.wait_ge(sem("x_t_done"), c2 + 1)
            mark("x_ready", nc.vector.tensor_copy(x[:, 2 * c2:2 * c2 + 2, :], halves(bank[c2])))
        def split_x():
            for c2 in range(4):
                split_pair("attn0", "load", lambda c: vec("attn_norm", c), c2)

        mem_slots(1, split_x, lambda: mem_values(0))
        inverse("attn0")

        g = G_DSA
        convert(g + 2)
        take(g, stage[2][0:72, 0:S], rows=72, n=1)
        mem_values(1)
        convert(g + 3)
        take(g + 1, stage[0])
        rotate("k_idx", keys[0:HD, 2, :])
        nc.vector.tensor_copy(keys[HD:P, 3, :], keys[0:HD, 2, :])
        dve.wait_ge(sem("w_idx_turned"), 1)
        link(nc.vector.tensor_scalar(w_idx, bank[1][:, 0:TB * N_IDX], N_IDX ** -0.5 * HD ** -0.5, None, ALU.mult))
        convert(g + 4)
        take(g + 2, stage[1])
        rotate("q_idx0", qa_flat[:, 1024:1536])
        dve.wait_ge(sem("rotated"), rot_no["q_idx1"] + 1)
        rotate("q_idx1", qa_flat[:, 1536:2048], signal="idx_inputs")
        g = G_DSA + 3
        used(dve, g)
        link(nc.vector.tensor_tensor(qa_flat[0:ROPE, S:2 * S], proj_bank(g)[0:ROPE, S:2 * S], rstd[0:ROPE], ALU.mult))
        mark("proj_evicted", nc.vector.tensor_tensor(qa_flat[:, 0:S], proj_bank(g)[:, 0:S], rstd, ALU.mult))
        convert(g + 2)
        for h in range(N_IDX):
            dve.wait_ge(sem("idx_relu"), h + 1)
            if h:
                dve.wait_ge(sem("idx_weighed"), h)
            for b, (lo, hi) in enumerate(CAUSAL):
                w = w_idx[:, b * N_IDX + h:b * N_IDX + h + 1]
                r, s_h = ranking[:, lo:hi], scores[h % 2][:, lo:hi]
                if h == 0:
                    ins = nc.vector.tensor_scalar(r, s_h, w, 0.0, ALU.mult, ALU.add)
                else:
                    ins = nc.vector.scalar_tensor_tensor(r, s_h, w, r, ALU.mult, ALU.add)
            mark("idx_weighed", ins)
        dve.wait_ge(sem("idx_weighed"), N_IDX)
        link(nc.vector.scalar_tensor_tensor(ranking, const_of("causal"), LATER, ranking, ALU.mult, ALU.add))

        def take_top(rounds):
            for _ in range(rounds):
                for b, (lo, hi) in enumerate(CAUSAL):
                    chain[0] += 1
                    nc.vector.max(top8[:, 8 * b:8 * b + 8], ranking[:, lo:hi]).then_inc(sem("dve_link"), 1)
                for b, (lo, hi) in enumerate(CAUSAL):
                    dve.wait_ge(sem("dve_link"), chain[0] - (1 - b) if b == 0 else chain[0] - 1)
                    chain[0] += 1
                    nc.vector.match_replace(ranking[:, lo:hi], top8[:, 8 * b:8 * b + 8], ranking[:, lo:hi],
                                            TAKEN).then_inc(sem("dve_link"), 1)
                dve.wait_ge(sem("dve_link"), chain[0])

        g = G_DSA + 4
        convert(g + 2)
        take(g, stage[0])
        take_top(2)
        inverse("ckv", rstd_mem)
        mark("ckv_normed", nc.vector.scalar_tensor_tensor(qa_flat[:, 3 * S:4 * S], qa_flat[:, 0:S], vec("ckv_norm", 0),
                                                          rstd_mem, ALU.mult, ALU.mult))
        g = G_DSA + 5
        convert(g + 2)
        take(g, stage[1])
        rotate("q0", qb_flat[:, 0:512])
        take_top(2)
        dve.wait_ge(sem("k_nope_done"), 1)
        mark("k_nope_copied", nc.vector.tensor_copy(keys[0:HD, 0, :], bank[1][0:HD, 0:S]))
        mark("k_nope_copied", nc.vector.tensor_copy(keys[HD:P, 1, :], bank[1][HD:P, 0:S]))
        dve.wait_ge(sem("k_nope_copied"), 2)
        rotate("k_rope", keys[0:ROPE, 0, :])
        nc.vector.tensor_copy(keys[HD:HD + ROPE, 1, :], keys[0:ROPE, 0, :])
        g = G_DSA + 6
        take(g, stage[0])
        take_top(2)
        g = G_DSA + 7
        take_top(TOPK // 8 - 6)
        link(nc.vector.tensor_scalar(dsa_mask, ranking, TAKEN, NEG, ALU.not_equal, ALU.mult))
        link(nc.vector.tensor_tensor(dsa_mask, dsa_mask, const_of("causal"), ALU.add))
        take(g, q_mem.rearrange("p c t -> p (c t)"))
        dve.wait_ge(sem("dsa_v_done"), 1)
        mark("dsa_kv_ready", nc.vector.tensor_copy(va[:, 0:2 * HD], bank[1][:, 0:2 * HD]))
        attend("o0", {"dsa": lambda h, b: dsa_mask[:, CAUSAL[b][0]:CAUSAL[b][1]]},
               between={0: lambda: rotate("q1", qb_flat[:, 512:1024], signal="q1_rotated"),
                        2: lambda: rotate("q2", qb_flat[:, 1024:1536], signal="q2_rotated")})
        add_slots(G_WO0, "wo0", "ffn0", lambda c: vec("ffn_norm", c))
        ffn(0, "attn1", lambda c: vec("attn_norm", DC + c))

        for i in range(3):
            g = G_NSA + i
            convert(g + 2)
            take(g, qa_flat[:, 512 * i:512 * i + 512])
            if i:
                rotate(f"nq{i - 1}", qb_flat[:, 512 * (i - 1):512 * i])
        g = G_NSA + 3
        convert(g + 2)
        take(g, stage[0])
        rotate("nq2", qb_flat[:, 1024:1536])
        for m, name in enumerate(("pos_k", "pos_v")):
            dve.wait_ge(sem("ft_copied"), 4 * m + 4)
            ft = probs_t[m][:, 0:32 * NCMP].rearrange("p (l n) -> p l n", l=16)
            pos = vec_t[:, vec_col[name]:vec_col[name] + 16]
            mark("ft_ready", nc.vector.tensor_tensor(ft, ft, bass.AP(pos.tensor, pos.offset, [pos.ap[0], [1, 16], [0, 2 * NCMP]]),
                                                     ALU.add))
        g = G_NSA + 4
        convert(g + 2)
        take(g, probs[1][0:36, S:2 * S], rows=36, n=1)
        g = G_NSA + 5
        convert(g + 2)
        take(g, stage[1])
        dve.wait_ge(sem("gates_turned"), 1)
        mark("gates_ready", nc.vector.tensor_copy(gates, bank[2][:, 0:TB * 36]))
        dve.wait_ge(sem("gelu_done"), 2)
        hv = scores[0][:, 32:32 + 2 * NCMP]
        mark("hv_spread", nc.vector.tensor_copy(
            scores[1][:, 0:2 * HPG * NCMP].rearrange("p (g h c) -> p g h c", g=2, h=HPG),
            bass.AP(hv.tensor, hv.offset, [hv.ap[0], [NCMP, 2], [0, HPG], [1, NCMP]])))
        dve.wait_ge(sem("cmp_out"), 1)
        dve.wait_ge(sem("cmp_k_cleared"), 1)
        by_group = bank[0][:, 0:2 * NCMP].rearrange("p (g c) -> p g c", g=2)
        nc.vector.tensor_copy(cmp_k[0:HD, :, 0:NCMP], by_group[0:HD])
        link(nc.vector.tensor_copy(cmp_k[HD:P, :, NCMP:2 * NCMP], by_group[HD:P]))
        rows = HPG * NCMP
        own = const_of("own_head", rows)
        for grp in range(2):
            v = bank[1][0:rows, HD * grp:HD * grp + HD]
            ins = nc.vector.tensor_tensor(
                cmp_v[0:rows, grp, :].rearrange("p (h d) -> p h d", h=HPG),
                bass.AP(v.tensor, v.offset, [v.ap[0], [0, HPG], [1, HD]]),
                bass.AP(own.tensor, own.offset, [own.ap[0], [1, HPG], [0, HD]]), ALU.mult)
        mark("cmp_kv_ready", ins)

        def both_ways(name, c):
            rotate(name, keys[:, c, :], lower=keys[:, c + 3, :])
            nc.vector.tensor_copy(keys[0:HD, c + 2, :], keys[HD:P, c + 3, :])
            link(nc.vector.tensor_copy(keys[HD:P, c + 1, :], keys[0:HD, c, :]))

        both_ways("ks", 0)
        g = G_NSA + 6
        convert(g + 2)
        take(g, stage[2])
        nb = TB * N_TOK
        dve.wait_ge(sem("cmp_scored"), 1)
        sc3 = scores[1][:, 0:nb * NCMP].rearrange("p (n c) -> p n c", c=NCMP)
        cm = const_of("cmp_mask")
        for b in range(TB):
            ins = nc.vector.tensor_tensor(
                sc3[:, b * N_TOK:(b + 1) * N_TOK, :],
                bank[b][:, 0:N_TOK * NCMP].rearrange("p (n c) -> p n c", c=NCMP),
                bass.AP(cm.tensor, cm.offset + b * NCMP, [cm.ap[0], [0, N_TOK], [1, NCMP]]), ALU.add)
        link(ins)
        mx = factor[:, 128:128 + nb]
        den = factor[:, 160:160 + nb]
        fac = factor[:, 192:192 + nb]
        link(nc.vector.tensor_reduce(mx, sc3, AX.X, ALU.max))
        link(nc.vector.tensor_scalar(mx, mx, NEG / 10, None, ALU.max))

        def per_row(ap, n):
            return bass.AP(ap.tensor, ap.offset, [ap.ap[0], [1, nb], [0, n]])

        link(nc.vector.tensor_tensor(sc3, sc3, per_row(mx, NCMP), ALU.subtract))
        mark("cmp_shifted", nc.vector.tensor_scalar(scores[1][:, 0:nb * NCMP], scores[1][:, 0:nb * NCMP], SCALE, None, ALU.mult))
        g = G_NSA + 7
        take(g, q_mem.rearrange("p c t -> p (c t)"))
        dve.wait_ge(sem("gates_ready"), 1)
        dve.wait_ge(sem("cmp_exp"), 1)
        link(nc.vector.tensor_reduce(den, probs[0][:, 0:nb * NCMP].rearrange("p (n c) -> p n c", c=NCMP), AX.X, ALU.add))
        link(nc.vector.tensor_scalar(den, den, 1e-30, None, ALU.max))
        link(nc.vector.reciprocal(fac, den))
        link(nc.vector.tensor_tensor(fac, fac, gates.rearrange("p (n k) -> p n k", k=3)[:, :, 0], ALU.mult))
        pc = probs[0][:, 0:nb * NCMP].rearrange("p (n c) -> p n c", c=NCMP)
        mark("cmp_scaled", nc.vector.tensor_tensor(pc, pc, per_row(fac, NCMP), ALU.mult))
        dve.wait_ge(sem("cmp_turned"), 1)
        mark("cmp_t_ready", nc.vector.tensor_copy(cmp_t[0:rows, :], bank[2][0:rows, :]))
        both_ways("kw", 4)
        dve.wait_ge(sem("v_turned"), 3)
        mark("nsa_ready", nc.vector.tensor_copy(va, bank[1]))
        causal = lambda h, b: const_of("causal")[:, CAUSAL[b][0]:CAUSAL[b][1]]
        attend("o1", {"slc": causal, "win": causal})
        add_slots(G_WO1, "wo1", "ffn1", lambda c: vec("ffn_norm", DC + c))
        ffn(1)
        dve.wait_ge(sem("x_ready"), 4 * 3)
        mix_gain = lambda c: vec("norm_mix", c)

        def first_pairs(c2):
            dve.wait_ge(sem("x_ready"), 4 * 3 + c2 + 1)
            split_lo(prod["mix0"], x, mix_gain, (c2,))

        rescale_x("final1", lambda c: vec("final_norm", c), "x_ready", first_pairs)

        dve.wait_ge(sem("x_ready"), 4 * 4)
        split_lo(prod["mix0"], x, mix_gain, (3,))
        inverse("mix0")
        dve.wait_ge(sem("t5_rows_done"), 1)
        link(nc.vector.tensor_tensor(tok_flat[0:N_BAND, C_T5:C_T5 + 383], bank[2][0:N_BAND, 0:383],
                                     tok_flat[0:N_BAND, 383:766], ALU.add))
        mark("t5_row_ready", nc.vector.tensor_scalar(tok_flat[0:N_BAND, C_T5:C_T5 + 383], tok_flat[0:N_BAND, C_T5:C_T5 + 383],
                                                     1.0 / SCALE, None, ALU.mult))
        dve.wait_ge(sem("pad_cleared"), 1)

        def pw1_slot(g, dst):
            if g > G_PW1 + 1:
                dve.wait_ge(sem("glu_ready"), (g - G_PW1) // 2 * 2)
            take(g, dst)

        def glu(i):
            for t in range(2):
                dve.wait_ge(sem("glu_sigmoid"), 2 * i + t + 1)
                if t == 0:
                    evicted(dve, G_PW1 + 2 * i)
                c = 2 * i + t
                mark("glu_ready", nc.vector.scalar_tensor_tensor(
                    glu_pad[:, c, PAD:APAD], probs[0][:, S * t:S * t + S], vec("b_pw1", c),
                    scores[1][:, S * t:S * t + S], ALU.add, ALU.mult))

        def taps(c, k0, k1):
            if k0 == 0:
                dve.wait_ge(sem("glu_ready"), c + 1)
            for k in range(k0, k1):
                src, w = glu_pad[:, c, k:k + S], vec("w_dw", DC * k + c)
                if k == 0:
                    ins = nc.vector.tensor_scalar(conv_y[:, c, :], src, w, vec("b_dw", c), ALU.mult, ALU.add)
                else:
                    dve.wait_ge(sem(f"tap_done{c}"), k)
                    ins = nc.vector.scalar_tensor_tensor(conv_y[:, c, :], src, w, conv_y[:, c, :], ALU.mult, ALU.add)
                mark(f"tap_done{c}", ins)

        def diagonals(c, k0, k1):
            for k in range(max(k0, 0), min(k1, CONV)):
                n = CONV * PE_CHUNKS.index(c) + k
                if n >= NDIAG:
                    dve.wait_ge(sem("diag_used"), n - NDIAG + 1)
                mark("diag_ready", nc.vector.tensor_scalar(diag_of(n), ident, vec("w_dw", DC * k + c), None, ALU.mult))

        convert(G_PW1 + 2)
        pw1_slot(G_PW1, probs[0])
        convert(G_PW1 + 3)
        pw1_slot(G_PW1 + 1, scores[0])
        convert(G_PW1 + 4)
        glu(0)
        taps(1, 0, 4)
        pw1_slot(G_PW1 + 2, probs[0])
        convert(G_PW1 + 5)
        taps(1, 4, 8)
        pw1_slot(G_PW1 + 3, scores[0])
        convert(G_PW1 + 6)
        glu(1)
        taps(1, 8, 10)
        pw1_slot(G_PW1 + 4, probs[0])
        convert(G_PW1 + 7)
        taps(1, 10, 14)
        pw1_slot(G_PW1 + 5, scores[0])
        convert(G_PW1 + 8)
        glu(2)
        diagonals(5, 0, 8)
        pw1_slot(G_PW1 + 6, probs[0])
        convert(G_PW1 + 9)
        diagonals(5, 8, NDIAG)
        taps(1, 14, 20)
        pw1_slot(G_PW1 + 7, scores[0])
        taps(1, 20, 24)
        glu(3)
        for k in range(24, CONV):
            taps(1, k, k + 1)
            diagonals(5, NDIAG + 3 * (k - 24), NDIAG + 3 * (k - 24) + 3)
        for k in range(CONV):
            diagonals(6, 2 * k, 2 * k + 2)
            diagonals(7, 2 * k + 1 - CONV, 2 * k + 3 - CONV)
            taps(3, k, k + 1)
        for i, c in enumerate(POOL_CHUNKS):
            dve.wait_ge(sem("pool_chunk_done"), i + 1)
            mark("others_biased", nc.vector.tensor_scalar(conv_y[:, c, :], conv_y[:, c, :], vec("b_dw", c), None, ALU.add))
        for i, c in enumerate(PE_CHUNKS):
            dve.wait_ge(sem("diag_used"), CONV * (i + 1))
            mark("others_biased", nc.vector.tensor_scalar(conv_y[:, c, :], bank[1 + i][:, 0:S], vec("b_dw", c), None, ALU.add))
        dve.wait_ge(sem("ln_summed"), 1)
        mean = probs_t[0][:, 0:S]
        mark("mean_taken", nc.vector.tensor_scalar(mean, bank[0][:, 0:S], 1.0 / D, None, ALU.mult))
        dve.wait_ge(sem("mean_taken"), 1)
        for c2 in range(4):
            ys = conv_y[:, 2 * c2:2 * c2 + 2, :]
            mark("centred", nc.vector.tensor_tensor(ys, ys, over_two(mean), ALU.subtract))
        inverse("ln")
        for c2 in range(4):
            ys = conv_y[:, 2 * c2:2 * c2 + 2, :]
            mark("ln_scaled", nc.vector.tensor_tensor(ys, ys, over_two(rstd), ALU.mult))
        split_lo_pairs(prod["conv"], lambda c2: conv_y[:, 2 * c2:2 * c2 + 2, :])
        add_slots(G_PW2, "pw2", "ffn2", lambda c: vec("norm_ffn", c), bias="b_pw2")
        ffn(2, "kv", lambda c: vec("norm_kv", c),
            lambda: split_lo(prod["mix1"], x, lambda c: vec("norm_mix", DC + c)))

        g = G_KV
        convert(g + 2)
        take_keys(g, keys[:, 0::4], keys[:, 3::4])
        evicted(dve, g)
        nc.vector.tensor_copy(keys[0:HD, 2::4, :], keys[HD:P, 3::4, :])
        link(nc.vector.tensor_copy(keys[HD:P, 1::4, :], keys[0:HD, 0::4, :]))
        convert(g + 3)
        take(g + 1, probs[0])
        for i in range(4):
            g = G_Q + i
            convert(g + 2)
            take(g, qa_flat[:, 512 * i:512 * i + 512])
            if i == 0:
                dve.wait_ge(sem("v_turned"), 4)
                mark("band_v_ready", nc.vector.tensor_copy(va, bank[1]))
        dve.wait_ge(sem("small_landed"), SMALL_ALL)
        link(nc.vector.tensor_scalar(neg_sinks, sinks, -1.0, None, ALU.mult))
        dve.wait_ge(sem("t5_bias_landed"), 64)
        attend("o2", {"band": lambda h, b: t5_bias[:, h, P:S] if b == 0 else t5_bias[:, h, :]},
               init=lambda h: neg_sinks[:, h:h + 1])
        add_slots(G_WO2, "wo2", "ffn3", lambda c: vec("norm_ffn", DC + c))
        ffn(3)
        dve.wait_ge(sem("x_ready"), 4 * 6)
        rescale_x("final2", lambda c: vec("norm_final", c), "y_ready")
        for i in range(4):
            dve.wait_ge(sem("y_turned"), i + 1)
            mark("result_ready", nc.vector.tensor_copy(tok[:, i % 2, 512 * (i // 2):512 * (i // 2) + 512], bank[4 + i]))

    @block.tensor
    def _(pe):
        mm = nc.tensor.matmul
        turn = nc.tensor.transpose

        def mark(name, ins):
            ins.then_inc(sem(name), 1)

        def three(out_ap, hi, lo, act_hi, act_lo, start, stop, skip=False):
            mm(out_ap, hi, act_hi, start=start, stop=False, skip_group_check=skip)
            mm(out_ap, hi, act_lo, start=False, stop=False, skip_group_check=skip)
            return mm(out_ap, lo, act_hi, start=False, stop=stop, skip_group_check=skip)

        def project(g, p, fresh=False, j=0):
            w = slots[g][2]
            hi = w_hi[g % NS][:, 0:DC * w].rearrange("p (c n) -> p c n", c=DC)
            lo = w_lo[g % NS][:, 0:DC * w].rearrange("p (c n) -> p c n", c=DC)
            pe.wait_ge(sem("w_lo_done"), g + 1 + 6 * j)
            if proj_index[g] >= 4:
                pe.wait_ge(sem("proj_evicted"), proj_index[g] - 3 + 4 * j)
            tiles = list(enumerate(range(0, w, P)))
            order = ([(t, n0, c) for c in range(DC) for t, n0 in tiles] if fresh
                     else [(t, n0, c) for t, n0 in tiles for c in range(DC)])
            for t, n0, c in order:
                m = min(P, w - n0)
                if fresh and t == 0 and c % 2 == 0:
                    pe.wait_ge(sem("h_ready"), 4 * p + c // 2 + 1)
                ins = three(proj_bank(g)[0:m, S * t:S * t + S], hi[:, c, n0:n0 + m], lo[:, c, n0:n0 + m],
                            h_hi[p % 2][:, c, :], h_lo[p % 2][:, c, :], c == 0 and (t == 0 or not fresh),
                            c == DC - 1 and ((t, n0) == tiles[-1] or not fresh), skip=fresh)
            mark("slot_used", ins)

        def project_ahead(g, p, c2):
            w = slots[g][2]
            hi = w_hi[g % NS][:, 0:DC * w].rearrange("p (c n) -> p c n", c=DC)
            lo = w_lo[g % NS][:, 0:DC * w].rearrange("p (c n) -> p c n", c=DC)
            pe.wait_ge(sem("h_ready"), 4 * p + c2 + 1)
            if c2 == 0:
                pe.wait_ge(sem("w_lo_done"), g + 1)
            for c in (2 * c2, 2 * c2 + 1):
                for t in range(2):
                    ins = three(proj_bank(g)[:, S * t:S * t + S], hi[:, c, P * t:P * t + P], lo[:, c, P * t:P * t + P],
                                h_hi[p % 2][:, c, :], h_lo[p % 2][:, c, :], c == 0 and t == 0,
                                c == DC - 1 and t == 1, skip=True)
            if c2 == 3:
                mark("slot_used", ins)

        def total(name, src=None):
            if src is None:
                pe.wait_ge(sem("added"), added_no[name] + 1)
                src = qa_flat[:, 0:S]
            mark("sum_ready", mm(bank[0][:, 0:S], ones, src, start=True, stop=True))

        def total_of_chunks(name):
            for c in range(DC):
                pe.wait_ge(sem("squared"), 4 * squares_no[name] + c // 2 + 1)
                ins = mm(bank[0][:, 0:S], ones, qa[:, c, :], start=(c == 0), stop=(c == DC - 1))
            mark("sum_ready", ins)

        def rotate(name):
            rows, n = rot_shape(name)
            mark("rotated", mm(rot_bank(name)[0:rows, 0:n], const_of("rot", rows)[:, 0:rows], rot_src[name],
                               start=True, stop=True))

        def turn_v(src, dst):
            for t in range(2):
                for b in range(TB):
                    ins = turn(dst[:, S * b + P * t:S * b + P * t + P], src[:, S * t + P * b:S * t + P * b + P], ident)
            mark("v_turned", ins)

        def attend(name, **parts):
            heads = HEADS[name]

            def qk(n, run, h):
                q, k, _, ready = parts[run]
                ready(h)
                if n >= 2:
                    pe.wait_ge(sem("exp_done" if run.startswith("mem") and h >= 2 else "max_ready"), n - 1)
                queries = q(h)
                for b in range(TB):
                    lo, hi = EXTENT[run][b]
                    ins = mm(bank[n % 2][:, lo:hi], queries[:, P * b:P * b + P], k(h)[:, 0:hi - lo],
                             start=True, stop=True)
                mark("qk_done", ins)

            def turn_probs(n, run, h):
                pe.wait_ge(sem("probs_scaled"), n + 1)
                pe.wait_ge(sem("first_scaled"), n + 1)
                if n >= 2:
                    pe.wait_ge(sem("probs_t_ready"), n - 1)
                blocks = EXTENT[run][1][1] // P
                for i in range(blocks):
                    to = TURN_TO[blocks][i]
                    ins = turn(bank[2 + n % 2][:, P * to:P * to + P], soft[name][n % 3][:, P * i:P * i + P], ident)
                mark("probs_turned", ins)

            def pv(pair):
                n, run, h = pair[1]
                c = chunk_of(run, h)
                dst = out_bank(name, c // 2)[:, S * (c % 2):S * (c % 2) + S]
                if run == "slc":
                    grp, at = c // 3, P * (c % 3)
                    pe.wait_ge(sem("cmp_t_ready"), 1)
                    mm(dst, cmp_v[0:HPG * NCMP, grp, at:at + P], cmp_t[0:HPG * NCMP, S * grp:S * grp + S],
                       start=True, stop=False, skip_group_check=True)
                pe.wait_ge(sem("probs_t_ready"), n + 1)
                for kb in range(2):
                    q0 = P if kb == 1 and EXTENT[run] is CAUSAL else 0
                    for n, run, h in pair:
                        ins = mm(dst[HD * (h % 2):HD * (h % 2) + HD, q0:S], parts[run][2](h, kb),
                                 turned[n % 3][:, S * kb:S * kb + S - q0],
                                 start=kb == 0 and run not in ("slc", "win"), stop=kb == 1 and run != "slc",
                                 skip_group_check=True)
                mark("pv_done", ins)

            for i in range(3):
                qk(*heads[i])
            g, p = G_OUT[name], prod[name]
            for i in range(len(heads)):
                turn_probs(*heads[i])
                if i + 3 < len(heads):
                    qk(*heads[i + 3])
                if i >= 2 and i % 2 == 0:
                    pv(heads[i - 2:i])
                if i == len(heads) - 2:
                    project_ahead(g, p, 0)
                    project_ahead(g, p, 1)
            project_ahead(g, p, 2)
            pe.wait_ge(sem("h_ready"), 4 * p + 2)
            project_ahead(g + 1, p, 0)
            pv(heads[-2:])
            for c2 in (1, 2):
                project_ahead(g + 1, p, c2)
            for i in range(2):
                project_ahead(g + i, p, 3)

        def turn_tokens(src, banks, name):
            for c2 in range(4):
                for c in (2 * c2, 2 * c2 + 1):
                    for b in range(TB):
                        at = S * (c % 2) + P * b
                        ins = turn(banks[c2][:, at:at + P], src[:, b, P * c:P * c + P], ident)
                mark(name, ins)

        def ffn(f, p):
            first = FF[f][0]
            n0 = FF_STEPS * f

            def down(s, g, j=0, start=False, stop=False):
                pe.wait_ge(sem("w_lo_done"), g + 1 + 6 * j)
                pe.wait_ge(sem("ff_ready"), n0 + s + 1 + 2 * j)
                hi = w_hi[g % NS].rearrange("p (c n) -> p c n", c=2)
                lo = w_lo[g % NS].rearrange("p (c n) -> p c n", c=2)
                for m in range(DC):
                    for c in range(2):
                        ins = three(bank[m // 2][:, S * (m % 2):S * (m % 2) + S], hi[:, c, P * m:P * m + P],
                                    lo[:, c, P * m:P * m + P], ff_hi[s % 2][:, S * c:S * c + S],
                                    ff_lo[s % 2][:, S * c:S * c + S], start and c == 0 and m % 2 == 0,
                                    stop and c == 1 and m % 2 == 1, skip=True)
                    if stop and m % 2 == 1:
                        mark("down_done", ins)
                if not stop:
                    mark("slot_used", ins)

            def step(s, j=0):
                g = first + 3 * s - 1
                project(g, p, j=j)
                project(g + 1, p, j=j)
                down(s - 1, g + 2, j, start=(s == 1))

            project(first, p, fresh=True)
            total(PROD[p])
            project(first + 1, p)
            pe.wait_ge(sem("root_done"), sum_no[PROD[p]] + 1)
            step(1)
            with pe.Fori(0, (FF_STEPS - 3) // 2) as j:
                step(2, j)
                step(3, j)
            step(FF_STEPS - 1)
            down(FF_STEPS - 1, first + 3 * FF_STEPS - 1, stop=True)
            pe.wait_ge(sem("down_done"), 4 * f + 4)
            pe.nop().then_inc(sem("slot_used"), 1)

        pe.wait_ge(sem("ident_landed"), 16)
        pe.wait_ge(sem("mem_landed"), 16 * TB)
        turn_tokens(mem_tok, bank[4:8], "mem_t_done")
        pe.wait_ge(sem("vec_landed"), VEC_ALL)
        for t in range(4):
            ins = turn(bank[1][:, P * t:P * t + P], vec_tok[:, t, :], ident)
        mark("vec_turned", ins)
        pe.wait_ge(sem("cleared"), 4)
        total("mem")
        project(0, prod["mem0"], fresh=True)
        project(1, prod["mem0"])
        pe.wait_ge(sem("root_done"), 1)
        pe.wait_ge(sem("vec_ready"), 1)
        pe.wait_ge(sem("x_landed"), 16)
        turn_tokens(tok, bank[0:4], "x_t_done")
        project(2, prod["mem1"], fresh=True)
        pe.wait_ge(sem("x_ready"), 4)
        evicted(pe, 1)
        turn_v(probs[0], bank[1])
        project(3, prod["mem1"])
        p = prod["attn0"]
        g = G_DSA
        project(g, p, fresh=True)
        evicted(pe, 3)
        turn_v(probs[1], bank[2])
        total("attn0")
        project(g + 1, p)
        pe.wait_ge(sem("v_mem_ready"), 2)
        evicted(pe, g)
        pe.wait_ge(sem("const_landed"), 16)
        rotate("k_idx")
        for b in range(TB):
            ins = turn(bank[1][:, N_IDX * b:N_IDX * b + N_IDX], stage[2][HD:HD + N_IDX, P * b:P * b + P],
                       ident[HD:HD + N_IDX, HD:HD + N_IDX])
        mark("w_idx_turned", ins)
        project(g + 2, p)
        evicted(pe, g + 1)
        rotate("q_idx0")
        evicted(pe, g + 2)
        rotate("q_idx1")
        project(g + 3, p)
        pe.wait_ge(sem("idx_inputs"), 1)
        pe.wait_ge(sem("keys_cleared"), 4)
        for h in range(N_IDX):
            if h >= 2:
                pe.wait_ge(sem("idx_relu"), h - 1)
            for b, (lo, hi) in enumerate(CAUSAL):
                ins = mm(bank[h % 2][:, lo:hi], qa[:, 4 + h // 2, P * b:P * b + P], keys[:, 2 + h % 2, 0:hi - lo],
                         start=True, stop=True)
            mark("idx_scored", ins)
        project(g + 4, p)
        pe.wait_ge(sem("ckv_squared"), 1)
        pe.wait_ge(sem("idx_relu"), N_IDX)
        total("ckv", qa_flat[:, 2 * S:3 * S])
        project(g + 5, p)
        evicted(pe, g + 4)
        rotate("q0")
        pe.wait_ge(sem("ckv_normed"), 1)
        pe.wait_ge(sem("small_landed"), SMALL_ALL)
        ckv = qa_flat[:, 3 * S:4 * S]
        mark("k_nope_done", mm(bank[1][:, 0:S], w_uk, ckv, start=True, stop=True))
        evicted(pe, g + 5)
        rotate("k_rope")
        project(g + 6, p)
        pe.wait_ge(sem("k_nope_copied"), 2)
        rotate("q1")
        for b in range(TB):
            ins = mm(bank[1][:, HD * b:HD * b + HD], ckv[:, P * b:P * b + P], w_uv, start=True, stop=True)
        mark("dsa_v_done", ins)
        project(g + 7, p)
        evicted(pe, g + 6)
        rotate("q2")

        def dsa_ready(h):
            if h == 1:
                pe.wait_ge(sem("dsa_kv_ready"), 1)

        def dsa_q(h):
            if h in (4, 8):
                pe.wait_ge(sem(f"q{h // 4}_rotated"), 1)
            return qb[:, h // 2, :]

        attend("o0",
               dsa=(dsa_q, lambda h: keys[:, h % 2, :], lambda h, kb: va[:, HD * kb:HD * kb + HD], dsa_ready),
               mem0=(lambda h: q_mem[:, h // 2, :], lambda h: k_mem[0][:, h, :],
                     lambda h, kb: v_mem[:, 0, kb, HD * h:HD * h + HD], lambda h: None))
        for i in (2, 3):
            project(G_WO0 + i, prod["o0"])
        ffn(0, prod["ffn0"])
        p = prod["attn1"]
        g = G_NSA
        project(g, p, fresh=True)
        total("attn1")
        for i in range(3):
            project(g + 1 + i, p)
            evicted(pe, g + i)
            rotate(f"nq{i}")
        project(g + 4, p)
        pe.wait_ge(sem("cmp_w1_landed"), 32)
        for m in range(2):
            pe.wait_ge(sem("ft_ready"), m + 1)
            for l in range(16):
                ins = mm(bank[m][:, 0:2 * NCMP], cmp_w1[:, m, l, :], probs_t[m][:, 2 * NCMP * l:2 * NCMP * (l + 1)],
                         start=(l == 0), stop=(l == 15))
            mark("cmp_hidden", ins)
        project(g + 5, p)
        pe.wait_ge(sem("gates_open"), 1)
        evicted(pe, g + 5)
        for b in range(TB):
            ins = turn(bank[2][:, 36 * b:36 * b + 36], probs[1][0:36, P * b:P * b + P], ident[0:36, 0:36])
        mark("gates_turned", ins)
        pe.wait_ge(sem("hv_spread"), 1)
        mm(bank[0][:, 0:2 * NCMP], cmp_w2[:, 0:2 * HD], scores[0][:, 0:2 * NCMP], start=True, stop=True)
        rows = HPG * NCMP
        for grp in range(2):
            ins = mm(bank[1][0:rows, HD * grp:HD * grp + HD], scores[1][:, rows * grp:rows * (grp + 1)],
                     cmp_w2[:, 2 * HD:3 * HD], start=True, stop=True)
        mark("cmp_out", ins)
        pe.wait_ge(sem("gates_ready"), 1)
        rotate("ks")
        project(g + 6, p)
        pe.wait_ge(sem("cmp_kv_ready"), 1)
        for b in range(TB):
            for c in range(N_TOK // 2):
                ins = mm(bank[b][:, 2 * c * NCMP:2 * (c + 1) * NCMP], qa[:, c, P * b:P * b + P],
                         cmp_k[:, 2 * c // HPG], start=True, stop=True)
        mark("cmp_scored", ins)
        project(g + 7, p)
        pe.wait_ge(sem("cmp_scaled"), 1)
        for b in range(TB):
            for grp in range(2):
                ins = turn(bank[2][0:rows, S * grp + P * b:S * grp + P * b + P],
                           probs[0][:, rows * (2 * b + grp):rows * (2 * b + grp + 1)], ident)
        mark("cmp_turned", ins)
        evicted(pe, g + 6)
        rotate("kw")
        for k in range(2):
            for b in range(TB):
                ins = turn(bank[1][:, S * k + P * b:S * k + P * b + P], stage[1 + k][:, S + P * b:S + P * b + P], ident)
        mark("v_turned", ins)
        evicted(pe, g + 7)

        def nsa_ready(h):
            if h == 1:
                pe.wait_ge(sem("nsa_ready"), 1)

        def nsa_k(first_tile):
            return lambda h: keys[:, first_tile + 2 * (h // HPG) + h % 2, :]

        def nsa_v(k):
            return lambda h, kb: va[:, S * k + P * kb + HD * (h // HPG):S * k + P * kb + HD * (h // HPG) + HD]

        attend("o1",
               slc=(lambda h: qb[:, h // 2, :], nsa_k(0), nsa_v(0), nsa_ready),
               win=(lambda h: qb[:, h // 2, :], nsa_k(4), nsa_v(1), lambda h: None),
               mem1=(lambda h: q_mem[:, h // 2, :], lambda h: k_mem[1][:, h, :],
                     lambda h, kb: v_mem[:, 1, kb, HD * h:HD * h + HD], lambda h: None))
        for i in (2, 3):
            project(G_WO1 + i, prod["o1"])
        ffn(1, prod["ffn1"])
        pe.wait_ge(sem("x_ready"), 4 * 2 + 1)
        total_of_chunks("final1")
        p = prod["mix0"]
        pe.wait_ge(sem("t5_landed"), 16)
        pe.wait_ge(sem("x_ready"), 4 * 3)
        mark("t5_rows_done", mm(bank[2][0:N_BAND, 0:383], rel_bias[0:BUCKETS, :], tok_flat[0:BUCKETS, 0:383],
                                start=True, stop=True))
        project(G_PW1, p, fresh=True)
        total("mix0")
        for g in range(G_PW1 + 1, G_PW1 + 8):
            project(g, p)
        pe.wait_ge(sem("root_done"), sum_no["mix0"] + 1)
        pe.wait_ge(sem("t5_row_ready"), 1)
        for i, c in enumerate(PE_CHUNKS):
            pe.wait_ge(sem("glu_ready"), c + 1)
            for k in range(CONV):
                pe.wait_ge(sem("diag_ready"), CONV * i + k + 1)
                mark("diag_used", mm(bank[1 + i][:, 0:S], diag_of(CONV * i + k), glu_pad[:, c, k:k + S],
                                     start=(k == 0), stop=(k == CONV - 1)))
        for i, c in enumerate(DVE_CHUNKS):
            pe.wait_ge(sem(f"tap_done{c}"), CONV)
            mm(bank[0][:, 0:S], ones, conv_y[:, c, :], start=(i == 0), stop=False)
        for i, c in enumerate(POOL_CHUNKS + PE_CHUNKS):
            pe.wait_ge(sem("others_biased"), i + 1)
            ins = mm(bank[0][:, 0:S], ones, conv_y[:, c, :], start=False,
                     stop=(c == PE_CHUNKS[-1]))
        mark("ln_summed", ins)
        pe.wait_ge(sem("mean_taken"), 1)
        total_of_chunks("ln")
        for i in range(4):
            project(G_PW2 + i, prod["conv"], fresh=(i == 0))
        ffn(2, prod["ffn2"])
        project(G_KV, prod["kv"], fresh=True)
        total("kv")
        project(G_KV + 1, prod["kv"])
        project(G_Q, prod["mix1"], fresh=True)
        evicted(pe, G_KV + 1)
        turn_v(probs[0], bank[1])
        for g in range(G_Q + 1, G_Q + 4):
            project(g, prod["mix1"])

        def band_ready(h):
            if h == 1:
                pe.wait_ge(sem("band_v_ready"), 1)
            if h == 2:
                evicted(pe, G_Q + 3)

        attend("o2", band=(lambda h: qa[:, h // 2, :], lambda h: keys[:, 2 * (h // 4) + h % 2, :],
                           lambda h, kb: va[:, S * kb + HD * (h // 4):S * kb + HD * (h // 4) + HD], band_ready))
        for i in (2, 3):
            project(G_WO2 + i, prod["o2"])
        ffn(3, prod["ffn3"])
        pe.wait_ge(sem("x_ready"), 4 * 5 + 1)
        total_of_chunks("final2")
        for i in range(4):
            b = i % 2
            for k in range(4):
                c = 4 * (i // 2) + k
                if b == 0 and c % 2 == 0:
                    pe.wait_ge(sem("y_ready"), c // 2 + 1)
                ins = turn(bank[4 + i][:, P * k:P * k + P], x[:, c, P * b:P * b + P], ident)
            mark("y_turned", ins)


_INS = ["x", "mem", "attn_norm", "mem_norm", "ffn_norm", "final_norm", "dsa_w_in", "dsa_ckv_norm", "dsa_w_uk",
        "dsa_w_uv", "nsa_w_in", "nsa_cmp_pos_k", "nsa_cmp_pos_v", "nsa_cmp_k_w1", "nsa_cmp_k_w2",
        "nsa_cmp_v_w1", "nsa_cmp_v_w2", "mem_w_kv", "w_o", "ffn_w_in", "ffn_w_down", "norm_mix_2",
        "norm_ffn_2", "conv_w_pw1_2", "conv_b_pw1_2", "conv_w_dw_2", "conv_b_dw_2", "conv_ln_g_2",
        "conv_ln_b_2", "conv_w_pw2_2", "conv_b_pw2_2", "norm_kv_2", "w_kv_2", "w_q_2", "w_o_2", "sinks_2",
        "rel_bias_2", "ffn_w_up_2", "ffn_w_down_2", "norm_final_2"]


def kernel(**inputs):
    import concourse.bacc as bacc
    from concourse.bass_utils import run_bass_kernel_spmd

    nc = bacc.Bacc("TRN2", target_bir_lowering=False, num_devices=1)
    arrays = {name: np.ascontiguousarray(inputs[name]) for name in _INS}
    arrays["const"] = constants()
    io = {name: nc.dram_tensor(f"in_{name}", a.shape, mybir.dt.from_np(a.dtype), kind="ExternalInput").ap()
          for name, a in arrays.items()}
    out = nc.dram_tensor("result", (1, S, D), F32, kind="ExternalOutput").ap()
    build(nc, io, out)
    r = run_bass_kernel_spmd(nc, [{f"in_{name}": a for name, a in arrays.items()}], core_ids=[0])
    return r.results[0]["result"]
```
